# Optimizing a Trainium2 kernel written in Bass

```python
import math
import jax
import jax.numpy as jnp
from jax import lax
import numpy as np

D_MODEL = 1024
BATCH = 1
SEQ = 512
DEPTH = 2

CTX_LEN = 256
GRID_W = 64
HEAD_DIM = 64
ROPE_BASE = 10000.0
EPS = 1e-6
NEG_INF = -1e30

GDN_HEADS = D_MODEL // 128
GDN_DIM = 64
GDN_CHUNK = 64
SHORT_CONV = 3
DIFF_HEADS = D_MODEL // 256
DIFF_DIM = 64
DIFF_VDIM = 2 * DIFF_DIM
Q_BLOCK = 128
SWA_HEADS = D_MODEL // 128
SWA_KV_HEADS = 2
SWA_GROUP = SWA_HEADS // SWA_KV_HEADS
SWA_WINDOW = 128
SWA_BLOCK = 128
HY_CH = D_MODEL // 2
HY_ORDER = 2
HY_BANDS = 16
HY_EMB = 1 + 2 * HY_BANDS
HY_HID = 64
HY_MIN_DECAY = math.log(1e-2) / 1.5
HY_MAX_DECAY = math.log(1e-2) / 0.3
D_FF = ((8 * D_MODEL // 3 + 127) // 128) * 128
FFN_CONV = 3
N_MOD = 6

AB_SPLITS = (3 * GDN_HEADS * GDN_DIM, GDN_HEADS * GDN_DIM, 2 * GDN_HEADS, 2 * GDN_HEADS,
             DIFF_HEADS * 2 * DIFF_DIM, DIFF_HEADS * 2 * DIFF_DIM, DIFF_HEADS * DIFF_VDIM)
AB_OUT = GDN_HEADS * GDN_DIM + DIFF_HEADS * DIFF_VDIM
CD_SPLITS = (SWA_HEADS * HEAD_DIM, SWA_KV_HEADS * HEAD_DIM, SWA_KV_HEADS * HEAD_DIM, 3 * HY_CH)
CD_OUT = SWA_HEADS * HEAD_DIM + HY_CH

kernel_name = 'hybrid_dit_deltanet_diffattn_swa_hyena'

def rmsnorm(x, g):
    xf = x.astype(jnp.float32)
    y = xf * lax.rsqrt(jnp.mean(xf * xf, axis=-1, keepdims=True) + EPS)
    return (y * g.astype(jnp.float32)).astype(x.dtype)

def l2norm(x):
    return x * lax.rsqrt(jnp.sum(x * x, axis=-1, keepdims=True) + EPS)

def modulate(h, shift, scale):
    return h * (1.0 + scale) + shift

def split_cols(t, sizes):
    return jnp.split(t, np.cumsum(sizes)[:-1].tolist(), axis=-1)

def dwconv(x, w):
    k = w.shape[0]
    r = k // 2
    n = x.shape[1]
    xp = jnp.pad(x, ((0, 0), (r, r), (0, 0)))
    return sum(xp[:, i:i + n] * w[i] for i in range(k))

def axial_rope_angles(n_tokens):
    rows = n_tokens // GRID_W
    row = jnp.repeat(jnp.arange(rows, dtype=jnp.float32), GRID_W)
    col = jnp.tile(jnp.arange(GRID_W, dtype=jnp.float32), rows)
    half = HEAD_DIM // 2
    inv = ROPE_BASE ** (-jnp.arange(0, half, 2, dtype=jnp.float32) / half)
    return row[:, None] * inv, col[:, None] * inv

def rope_rotate(x, ang):
    cos = jnp.cos(ang)[:, None, :].astype(x.dtype)
    sin = jnp.sin(ang)[:, None, :].astype(x.dtype)
    x1, x2 = jnp.split(x, 2, axis=-1)
    return jnp.concatenate([x1 * cos - x2 * sin, x2 * cos + x1 * sin], axis=-1)

def rope2d(x, ang_row, ang_col):
    xr, xc = jnp.split(x, 2, axis=-1)
    return jnp.concatenate([rope_rotate(xr, ang_row), rope_rotate(xc, ang_col)], axis=-1)

def gated_delta_chunked(q, k, v, g, beta, s0):
    b, h, n, dk = q.shape
    dv = v.shape[-1]
    c = GDN_CHUNK
    nc = n // c
    f32 = jnp.float32
    q = q.astype(f32).reshape(b, h, nc, c, dk)
    k = k.astype(f32).reshape(b, h, nc, c, dk)
    v = v.astype(f32).reshape(b, h, nc, c, dv)
    g = g.astype(f32).reshape(b, h, nc, c)
    beta = beta.astype(f32).reshape(b, h, nc, c)
    gc = jnp.cumsum(g, axis=-1)
    pos = jnp.arange(c)
    incl = pos[:, None] >= pos[None, :]
    strict = pos[:, None] > pos[None, :]
    diff = gc[..., :, None] - gc[..., None, :]
    decay = jnp.where(incl, jnp.exp(jnp.where(incl, diff, 0.0)), 0.0)
    kb = k * beta[..., None]
    a = jnp.where(strict, jnp.einsum('bhnid,bhnjd->bhnij', kb, k) * decay, 0.0)
    rhs = jnp.concatenate([v * beta[..., None], kb * jnp.exp(gc)[..., None]], axis=-1)
    sol = lax.linalg.triangular_solve(a, rhs, left_side=True, lower=True, unit_diagonal=True)
    u, w = sol[..., :dv], sol[..., dv:]
    qk = jnp.where(incl, jnp.einsum('bhnid,bhnjd->bhnij', q, k) * decay, 0.0)
    g_last = gc[..., -1]
    q_dec = q * jnp.exp(gc)[..., None]
    k_tail = k * jnp.exp(g_last[..., None] - gc)[..., None]

    def step(s, xs):
        w_n, u_n, qk_n, q_n, k_n, gl_n = xs
        v_new = u_n - jnp.einsum('bhcd,bhde->bhce', w_n, s)
        o_n = jnp.einsum('bhcd,bhde->bhce', q_n, s) + jnp.einsum('bhij,bhje->bhie', qk_n, v_new)
        s = s * jnp.exp(gl_n)[..., None, None] + jnp.einsum('bhcd,bhce->bhde', k_n, v_new)
        return s, o_n

    xs = tuple(jnp.moveaxis(t, 2, 0) for t in (w, u, qk, q_dec, k_tail, g_last))
    s_final, o = lax.scan(step, s0.astype(f32), xs)
    return jnp.moveaxis(o, 0, 2).reshape(b, h, n, dv), s_final

def gdn_prep(p_qkv, p_beta, p_alpha, conv_w, a_log, dt_bias):
    b, n, _ = p_qkv.shape
    qkv = jax.nn.silu(dwconv(p_qkv, conv_w)).astype(jnp.float32)
    q, k, v = (t.reshape(b, n, GDN_HEADS, GDN_DIM).transpose(0, 2, 1, 3) for t in jnp.split(qkv, 3, axis=-1))
    q = l2norm(q) * GDN_DIM ** -0.5
    k = l2norm(k)
    to_dir = lambda t: t.astype(jnp.float32).reshape(b, n, 2, GDN_HEADS).transpose(2, 0, 3, 1)
    beta = jax.nn.sigmoid(to_dir(p_beta))
    g = -jnp.exp(a_log.astype(jnp.float32))[:, None, :, None] * jax.nn.softplus(
        to_dir(p_alpha) + dt_bias.astype(jnp.float32)[:, None, :, None])
    return q, k, v, g, beta

def gdn_bidir(q, k, v, g, beta, s0):
    flip = lambda t: jnp.flip(t, axis=2)
    o_f, s_f = gated_delta_chunked(q, k, v, g[0], beta[0], s0[0])
    o_b, s_b = gated_delta_chunked(flip(q), flip(k), flip(v), flip(g[1]), flip(beta[1]), s0[1])
    return o_f + flip(o_b), jnp.stack([s_f, s_b])

def gdn_out(o, gate, norm_g):
    b, h, n, d = o.shape
    o = rmsnorm(o.transpose(0, 2, 1, 3).astype(gate.dtype), norm_g)
    return (o * jax.nn.silu(gate.reshape(b, n, h, d))).reshape(b, n, h * d)

def diff_lambda_value(lam_p, lam_init):
    lp = lam_p.astype(jnp.float32)
    return jnp.exp(jnp.sum(lp[0] * lp[1])) - jnp.exp(jnp.sum(lp[2] * lp[3])) + lam_init

def diff_attention(q, k, v, lam):
    s = jnp.einsum('bqhtd,bmhtd->bhtqm', q, k).astype(jnp.float32) * DIFF_DIM ** -0.5
    p = jax.nn.softmax(s, axis=-1)
    a = p[:, :, 0] - lam * p[:, :, 1]
    return jnp.einsum('bhqm,bmhe->bqhe', a.astype(v.dtype), v)

def diff_attention_blocks(q, k, v, lam):
    b, n = q.shape[:2]
    qb = jnp.moveaxis(q.reshape(b, n // Q_BLOCK, Q_BLOCK, *q.shape[2:]), 1, 0)
    o = lax.map(lambda t: diff_attention(t, k, v, lam), qb)
    return jnp.moveaxis(o, 0, 1).reshape(b, n, *o.shape[3:])

def diff_out(o, norm_g, lam_init):
    b, n, h, d = o.shape
    return (rmsnorm(o, norm_g) * (1.0 - lam_init)).reshape(b, n, h * d)

def rope_pairs(t, rope):
    b, n, h, two, d = t.shape
    return rope2d(t.reshape(b, n, h * two, d), *rope).reshape(b, n, h, two, d)

def sink_probs(s, sink):
    col = jnp.broadcast_to(sink.astype(jnp.float32).reshape(SWA_KV_HEADS, SWA_GROUP, 1, 1), s.shape[:-1] + (1,))
    return jax.nn.softmax(jnp.concatenate([col, s], axis=-1), axis=-1)[..., 1:]

def swa_context(q, k, v, sink):
    b, n = q.shape[:2]
    qg = q.reshape(b, n, SWA_KV_HEADS, SWA_GROUP, HEAD_DIM)
    s = jnp.einsum('bqkgd,bmkd->bkgqm', qg, k).astype(jnp.float32) * HEAD_DIM ** -0.5
    p = sink_probs(s, sink)
    return jnp.einsum('bkgqm,bmkd->bqkgd', p.astype(v.dtype), v).reshape(b, n, SWA_HEADS * HEAD_DIM)

def swa_latent(q, k, v, kc, vc, sink):
    b, n = q.shape[:2]
    nb = n // SWA_BLOCK
    qb = jnp.moveaxis(q.reshape(b, nb, SWA_BLOCK, SWA_KV_HEADS, SWA_GROUP, HEAD_DIM), 1, 0)
    pad = ((0, 0), (SWA_BLOCK, SWA_BLOCK), (0, 0), (0, 0))
    kp, vp = jnp.pad(k, pad), jnp.pad(v, pad)
    span = 3 * SWA_BLOCK
    qi = jnp.arange(SWA_BLOCK)[:, None]
    m = jnp.arange(span)[None, :]
    in_window = jnp.abs(qi + SWA_BLOCK - m) <= SWA_WINDOW
    ctx_ok = jnp.ones((SWA_BLOCK, kc.shape[1]), bool)

    def block(args):
        i, qblk = args
        start = i * SWA_BLOCK
        kw = jnp.concatenate([lax.dynamic_slice_in_dim(kp, start, span, axis=1), kc], axis=1)
        vw = jnp.concatenate([lax.dynamic_slice_in_dim(vp, start, span, axis=1), vc], axis=1)
        j = start - SWA_BLOCK + m
        valid = jnp.concatenate([in_window & (j >= 0) & (j < n), ctx_ok], axis=1)
        s = jnp.einsum('bqkgd,bmkd->bkgqm', qblk, kw).astype(jnp.float32) * HEAD_DIM ** -0.5
        p = sink_probs(jnp.where(valid, s, NEG_INF), sink)
        return jnp.einsum('bkgqm,bmkd->bqkgd', p.astype(vw.dtype), vw)

    o = lax.map(block, (jnp.arange(nb), qb))
    return jnp.moveaxis(o, 0, 1).reshape(b, n, SWA_HEADS * HEAD_DIM)

def hyena_filters(n, w1, b1, w2, b2, w3, freq):
    f32 = jnp.float32
    pos = jnp.arange(n, dtype=f32)
    t = pos / max(n - 1, 1)
    ang = (2.0 * math.pi * pos / n)[:, None] * jnp.linspace(1e-4, HY_BANDS - 1, HY_BANDS, dtype=f32)[None, :]
    feats = jnp.concatenate([t[:, None], jnp.cos(ang), -jnp.sin(ang)], axis=-1)
    h = jnp.sin(freq[0].astype(f32) * (feats @ w1.astype(f32) + b1.astype(f32)))
    h = jnp.sin(freq[1].astype(f32) * (h @ w2.astype(f32) + b2.astype(f32)))
    h = (h @ w3.astype(f32)).reshape(n, HY_ORDER, 2, HY_CH)
    deltas = jnp.abs(jnp.linspace(HY_MIN_DECAY, HY_MAX_DECAY, HY_CH, dtype=f32))
    h = h * jnp.exp(-t[:, None, None, None] * deltas)
    kern = jnp.concatenate([h[:, :, 0], jnp.zeros((1, HY_ORDER, HY_CH), f32), jnp.flip(h[1:, :, 1], axis=0)], axis=0)
    kern = kern * lax.rsqrt(jnp.sum(kern * kern, axis=0, keepdims=True) + EPS)
    return jnp.fft.rfft(kern, axis=0)

def fft_long_conv(z, kf):
    n = z.shape[1]
    zf = jnp.fft.rfft(z.astype(jnp.float32), n=2 * n, axis=1)
    return jnp.fft.irfft(zf * kf[None], n=2 * n, axis=1)[:, :n].astype(z.dtype)

def hyena(u, conv_w, kf, bias):
    v, x1, x2 = jnp.split(dwconv(u, conv_w), 3, axis=-1)
    z = v
    for o, gate in enumerate((x1, x2)):
        z = gate * (fft_long_conv(z, kf[:, o]) + z * bias[o])
    return z

def mixer_ab(hx, hz, w_in, w_out, conv_w, a_log, dt_bias, gdn_g, lam_p, diff_g, lam_init, rope, with_ctx_out):
    b, n, _ = hx.shape
    nc = hz.shape[1]
    px = split_cols(hx @ w_in, AB_SPLITS)
    pz = split_cols(hz @ w_in, AB_SPLITS)
    qz, kz, vz, gz, bz = gdn_prep(pz[0], pz[2], pz[3], conv_w, a_log, dt_bias)
    qx, kx, vx, gx, bx = gdn_prep(px[0], px[2], px[3], conv_w, a_log, dt_bias)
    s0 = jnp.zeros((2, b, GDN_HEADS, GDN_DIM, GDN_DIM), jnp.float32)
    oaz, s_ctx = gdn_bidir(qz, kz, vz, gz, bz, s0)
    oax, _ = gdn_bidir(qx, kx, vx, gx, bx, s_ctx)
    lam = diff_lambda_value(lam_p, lam_init)
    dq_x = rope_pairs(px[4].reshape(b, n, DIFF_HEADS, 2, DIFF_DIM), rope)
    dk_x = rope_pairs(px[5].reshape(b, n, DIFF_HEADS, 2, DIFF_DIM), rope)
    dv_x = px[6].reshape(b, n, DIFF_HEADS, DIFF_VDIM)
    dk_z = pz[5].reshape(b, nc, DIFF_HEADS, 2, DIFF_DIM)
    dv_z = pz[6].reshape(b, nc, DIFF_HEADS, DIFF_VDIM)
    obx = diff_attention_blocks(dq_x, jnp.concatenate([dk_x, dk_z], axis=1), jnp.concatenate([dv_x, dv_z], axis=1), lam)
    out_x = jnp.concatenate([gdn_out(oax, px[1], gdn_g), diff_out(obx, diff_g, lam_init)], axis=-1) @ w_out
    if not with_ctx_out:
        return out_x, None
    dq_z = pz[4].reshape(b, nc, DIFF_HEADS, 2, DIFF_DIM)
    obz = diff_attention(dq_z, dk_z, dv_z, lam)
    out_z = jnp.concatenate([gdn_out(oaz, pz[1], gdn_g), diff_out(obz, diff_g, lam_init)], axis=-1) @ w_out
    return out_x, out_z

def mixer_cd(hx, hz, w_in, w_out, sink, hy_conv, hy_w1, hy_b1, hy_w2, hy_b2, hy_w3, hy_freq, hy_bias, rope, with_ctx_out):
    b, n, _ = hx.shape
    nc = hz.shape[1]
    qx, kx, vx, ux = split_cols(hx @ w_in, CD_SPLITS)
    qx = rope2d(qx.reshape(b, n, SWA_HEADS, HEAD_DIM), *rope)
    kx = rope2d(kx.reshape(b, n, SWA_KV_HEADS, HEAD_DIM), *rope)
    vx = vx.reshape(b, n, SWA_KV_HEADS, HEAD_DIM)
    if with_ctx_out:
        qz, kz, vz, uz = split_cols(hz @ w_in, CD_SPLITS)
    else:
        kv_lo = CD_SPLITS[0]
        kz, vz = split_cols(hz @ w_in[:, kv_lo:kv_lo + CD_SPLITS[1] + CD_SPLITS[2]], CD_SPLITS[1:3])
    kz = kz.reshape(b, nc, SWA_KV_HEADS, HEAD_DIM)
    vz = vz.reshape(b, nc, SWA_KV_HEADS, HEAD_DIM)
    ocx = swa_latent(qx, kx, vx, kz, vz, sink)
    odx = hyena(ux, hy_conv, hyena_filters(n, hy_w1, hy_b1, hy_w2, hy_b2, hy_w3, hy_freq), hy_bias)
    out_x = jnp.concatenate([ocx, odx], axis=-1) @ w_out
    if not with_ctx_out:
        return out_x, None
    ocz = swa_context(qz.reshape(b, nc, SWA_HEADS, HEAD_DIM), kz, vz, sink)
    odz = hyena(uz, hy_conv, hyena_filters(nc, hy_w1, hy_b1, hy_w2, hy_b2, hy_w3, hy_freq), hy_bias)
    out_z = jnp.concatenate([ocz, odz], axis=-1) @ w_out
    return out_x, out_z

def conv_ffn(h, w_up, conv_w, w_down):
    a, g = jnp.split(dwconv(h @ w_up, conv_w), 2, axis=-1)
    return (jax.nn.silu(g) * a) @ w_down

def setup_inputs(seed: int = 0) -> dict:
    key = jax.random.key(seed)
    ks = iter(jax.random.split(key, 40))
    f32 = jnp.float32
    nrm = lambda shape, scale: jax.random.normal(next(ks), shape, f32) * scale
    n_even, n_odd = (DEPTH + 1) // 2, DEPTH // 2
    d = D_MODEL
    p_ab, p_cd = sum(AB_SPLITS), sum(CD_SPLITS)
    dt = jnp.exp(jax.random.uniform(next(ks), (n_even, 2, GDN_HEADS), f32, minval=math.log(1e-3), maxval=math.log(1e-1)))
    return {
        'x': nrm((BATCH, SEQ, d), 1.0),
        'c': nrm((BATCH, d), 1.0),
        'ctx': nrm((BATCH, CTX_LEN, d), 1.0),
        'c_ctx': nrm((d,), 1.0),
        'w_mod': nrm((DEPTH, d, N_MOD * d), 0.5 * d ** -0.5),
        'b_mod': nrm((DEPTH, N_MOD * d), 0.02),
        'norm_g': 1.0 + nrm((DEPTH, 4, d), 0.02),
        'ffn_w_up': nrm((DEPTH, d, 2 * D_FF), d ** -0.5),
        'ffn_conv': nrm((DEPTH, FFN_CONV, 2 * D_FF), FFN_CONV ** -0.5),
        'ffn_w_down': nrm((DEPTH, D_FF, d), D_FF ** -0.5),
        'ab_w_in': nrm((n_even, d, p_ab), d ** -0.5),
        'ab_w_out': nrm((n_even, AB_OUT, d), AB_OUT ** -0.5),
        'gdn_conv': nrm((n_even, SHORT_CONV, 3 * GDN_HEADS * GDN_DIM), SHORT_CONV ** -0.5),
        'gdn_a_log': jnp.log(jax.random.uniform(next(ks), (n_even, 2, GDN_HEADS), f32, minval=1.0, maxval=16.0)),
        'gdn_dt_bias': dt + jnp.log(-jnp.expm1(-dt)),
        'gdn_norm_g': 1.0 + nrm((n_even, GDN_DIM), 0.02),
        'diff_lambda': nrm((n_even, 4, DIFF_DIM), 0.1),
        'diff_norm_g': 1.0 + nrm((n_even, DIFF_VDIM), 0.02),
        'cd_w_in': nrm((n_odd, d, p_cd), d ** -0.5),
        'cd_w_out': nrm((n_odd, CD_OUT, d), CD_OUT ** -0.5),
        'swa_sink': nrm((n_odd, SWA_HEADS), 1.0),
        'hy_conv': nrm((n_odd, SHORT_CONV, 3 * HY_CH), SHORT_CONV ** -0.5),
        'hy_w1': nrm((n_odd, HY_EMB, HY_HID), HY_EMB ** -0.5),
        'hy_b1': nrm((n_odd, HY_HID), 0.1),
        'hy_w2': nrm((n_odd, HY_HID, HY_HID), HY_HID ** -0.5),
        'hy_b2': nrm((n_odd, HY_HID), 0.1),
        'hy_w3': nrm((n_odd, HY_HID, HY_ORDER * 2 * HY_CH), HY_HID ** -0.5),
        'hy_freq': 1.0 + nrm((n_odd, 2, HY_HID), 0.1),
        'hy_bias': nrm((n_odd, HY_ORDER, HY_CH), 1.0),
    }

def reference(x, c, ctx, c_ctx, w_mod, b_mod, norm_g, ffn_w_up, ffn_conv, ffn_w_down,
              ab_w_in, ab_w_out, gdn_conv, gdn_a_log, gdn_dt_bias, gdn_norm_g, diff_lambda, diff_norm_g,
              cd_w_in, cd_w_out, swa_sink, hy_conv, hy_w1, hy_b1, hy_w2, hy_b2, hy_w3, hy_freq, hy_bias):
    b, n, d = x.shape
    rope = axial_rope_angles(n)
    z = ctx
    sc, scc = jax.nn.silu(c), jax.nn.silu(c_ctx)
    for l in range(DEPTH):
        last = l == DEPTH - 1
        i = l // 2
        mx = (sc @ w_mod[l] + b_mod[l]).reshape(b, 1, N_MOD, d)
        mz = (scc @ w_mod[l] + b_mod[l]).reshape(1, 1, N_MOD, d)
        hx = modulate(rmsnorm(x, norm_g[l, 0]), mx[:, :, 0], mx[:, :, 1])
        hz = modulate(rmsnorm(z, norm_g[l, 0]), mz[:, :, 0], mz[:, :, 1])
        if l % 2 == 0:
            lam_init = 0.8 - 0.6 * math.exp(-0.3 * l)
            ox, oz = mixer_ab(hx, hz, ab_w_in[i], ab_w_out[i], gdn_conv[i], gdn_a_log[i], gdn_dt_bias[i], gdn_norm_g[i],
                              diff_lambda[i], diff_norm_g[i], lam_init, rope, not last)
        else:
            ox, oz = mixer_cd(hx, hz, cd_w_in[i], cd_w_out[i], swa_sink[i], hy_conv[i], hy_w1[i], hy_b1[i], hy_w2[i],
                              hy_b2[i], hy_w3[i], hy_freq[i], hy_bias[i], rope, not last)
        x = x + mx[:, :, 2] * rmsnorm(ox, norm_g[l, 1])
        hx = modulate(rmsnorm(x, norm_g[l, 2]), mx[:, :, 3], mx[:, :, 4])
        x = x + mx[:, :, 5] * rmsnorm(conv_ffn(hx, ffn_w_up[l], ffn_conv[l], ffn_w_down[l]), norm_g[l, 3])
        if not last:
            z = z + mz[:, :, 2] * rmsnorm(oz, norm_g[l, 1])
            hz = modulate(rmsnorm(z, norm_g[l, 2]), mz[:, :, 3], mz[:, :, 4])
            z = z + mz[:, :, 5] * rmsnorm(conv_ffn(hz, ffn_w_up[l], ffn_conv[l], ffn_w_down[l]), norm_g[l, 3])
    return x


_drawn_inputs = setup_inputs


def setup_inputs(seed=0):
    import zlib

    import numpy as np

    out = dict(_drawn_inputs(seed))
    spreads = {}
    factors = {'norm_g': 2.788,
     'gdn_norm_g': 8.0,
     'diff_lambda': 3.67,
     'diff_norm_g': 8.0,
     'swa_sink': 8.0}
    for name, (base, spread) in spreads.items():
        noise = np.random.default_rng([zlib.crc32(name.encode()), seed]).standard_normal(out[name].shape)
        drawn = base * np.exp(spread * noise) if base else spread * noise
        out[name] = jnp.asarray(drawn.astype(out[name].dtype))
    for name, factor in factors.items():
        out[name] = (out[name] * factor).astype(out[name].dtype)
    return out
```

```python
import math
from contextlib import ExitStack

import numpy as np

import concourse.bass as bass
from concourse import mybir

F32 = mybir.dt.float32
ALU = mybir.AluOpType
ACT = mybir.ActivationFunctionType
AX = mybir.AxisListType

D = 1024
KT = D // 128
N_X, N_Z = 512, 256
N_ALL = N_X + N_Z
TX, TZ = N_X // 128, N_Z // 128
TT = TX + TZ
D_FF = 2816
FT = D_FF // 128
EPS = 1e-6
HEAD = 64
CHUNK = 64
GH = 8
PAIRS = GH // 2
GW = 512
CX, CZ = N_X // CHUNK, N_Z // CHUNK
STEPS = CX + CZ
NEG = -1e30
LAM_INIT = 0.2
N_FREQ = 512
RING = 4
SLOT = 2048
LEVELS = (1, 2, 4, 8, 16, 32)

_TABLE = {}
_at = 0
for _name, _n in (("ident", 128), ("rot", 128), ("heads", 128), ("ones", 128), ("cos", 512), ("sin", 512),
                  ("tri", 128), ("tri2", 256), ("mask_a", 128), ("mask_q", 128), ("m1", 128), ("mt", 768),
                  ("eye", 64), ("win_l", 128), ("win_r", 128), ("pick", 32), ("row_of", 256), ("nonzero", 1),
                  ("feats", 512)):
    _TABLE[_name] = (_at, _n)
    _at += _n
TABLE_COLS = _at


def constant_tables():
    f = np.float32
    t = np.zeros((128, TABLE_COLS), f)

    def put(name, a, rows=128):
        o, n = _TABLE[name]
        t[:rows, o:o + n] = np.asarray(a, f).reshape(rows, n)

    put("ident", np.eye(128))
    rot = np.zeros((128, 128))
    for d in range(128):
        if d % 32 < 16:
            rot[d + 16, d] = -1
        else:
            rot[d - 16, d] = 1
    put("rot", rot)
    put("heads", np.kron(np.eye(2), np.ones((64, 64))))
    put("ones", np.ones((128, 128)))
    inv = (f(10000.0) ** (-np.arange(0, 32, 2, dtype=f) / f(32))).astype(f)
    tok = np.arange(N_X)
    ang = np.zeros((128, N_X), f)
    for d in range(128):
        pos = (tok // 64 if d % 64 < 32 else tok % 64).astype(f)
        ang[d] = pos * inv[d % 16]
    put("cos", np.cos(ang))
    put("sin", np.sin(ang))
    i, j = np.arange(64)[:, None], np.arange(64)[None, :]
    both = lambda a: np.tile(a, (2, 1))
    two = lambda fwd, bwd: both(np.concatenate([fwd, bwd], axis=1))
    put("tri", two(i <= j, i >= j))
    put("tri2", np.concatenate([np.kron(np.eye(2), i <= j), np.kron(np.eye(2), i >= j)], axis=1))
    put("mask_a", two(np.where(i > j, 0, NEG), np.where(i < j, 0, NEG)))
    put("mask_q", two(np.where(i <= j, 0, NEG), np.where(i >= j, 0, NEG)))
    level = lambda b: (i // (2 * b) == j // (2 * b)) & ((i // b) % 2 == 1) & ((j // b) % 2 == 0)
    put("m1", two(level(1), level(1).T))
    put("mt", np.concatenate([two(level(b).T, level(b)) for b in LEVELS], axis=1))
    put("eye", both(np.eye(64)))
    q, m = np.arange(128)[:, None], np.arange(128)[None, :]
    put("win_l", np.where(m >= q, 0, NEG))
    put("win_r", np.where(m <= q, 0, NEG))
    pick = np.zeros((32, 2, 2, 2, PAIRS))
    for direction in range(2):
        for hh in range(2):
            for what in range(2):
                for p in range(PAIRS):
                    pick[what * 16 + direction * 8 + 2 * p + hh, direction, hh, what, p] = 1
    put("pick", pick, 32)
    row_of = np.zeros((2, 2, 128))
    row_of[0, 0] = row_of[1, 1] = 1
    put("row_of", row_of, 2)
    nz = np.ones(128)
    nz[0] = 0
    put("nonzero", nz)
    n = N_X
    pos = np.arange(n, dtype=f)
    tt = pos / f(n - 1)
    fa = (f(2.0 * math.pi) * pos / f(n))[:, None] * np.linspace(1e-4, 15, 16, dtype=f)[None, :]
    feats = np.concatenate([tt[:, None], np.cos(fa), -np.sin(fa)], axis=-1)
    put("feats", feats.T, 33)
    lo, hi = math.log(1e-2) / 1.5, math.log(1e-2) / 0.3
    decay = np.exp(-tt[:, None] * np.abs(np.linspace(lo, hi, 512, dtype=f))[None, :]).astype(f)
    w = 2 * np.pi * (np.arange(N_FREQ) + 0.5) / (2 * N_FREQ)
    ph = np.arange(n)[:, None] * w[None, :]
    fwd = np.stack([np.cos(ph), np.sin(ph)]).astype(f)
    back = (np.stack([np.cos(ph.T), np.sin(ph.T)]) / N_FREQ).astype(f)
    return {"t_table": t, "t_decay": decay, "t_fwd": fwd, "t_back": back}


class Core:

    def __init__(self, nc, a, ctx):
        self.nc, self.a, self.ctx = nc, a, ctx
        self.at = 0
        self.mem = ctx.enter_context(nc.sbuf_tensor("mem", [128, 53200], F32))
        self.ps = ctx.enter_context(nc.psum_tensor("banks", [128, 8, 512], F32))
        self.table, self.tab = self.room(TABLE_COLS), {}
        for name, (o, n) in _TABLE.items():
            self.tab[name] = self.table[:, o:o + n]
        self.x = self.room(TX * D).rearrange("p (t d) -> p t d", d=D)
        self.z = self.room(TZ * D).rearrange("p (t d) -> p t d", d=D)
        self.cols = self.room(512).rearrange("p (j c) -> p j c", j=4)
        self.sc = self.room(16).rearrange("p (k u) -> p k u", u=2)
        self.modc = self.room(64).rearrange("p (v k u) -> p v k u", v=4, u=2)
        self.coef = self.room(64).rearrange("p (m v u k) -> p m v u k", m=2, v=2, u=2)
        self.stat = self.room(256)
        self.gates = self.room(4 * D).rearrange("p (v u d) -> p v u d", v=2, u=2)
        self.ht = self.room(KT * N_ALL)
        self.ring = self.room(RING * SLOT)
        self.small = self.room(12 * 96 + 16)
        self.arena = self.mem[:, self.at:53200]
        self.arena_size = 53200 - self.at
        self.loads, self.range_of, self.issued = [], {}, 0
        self.slot_in = [ctx.enter_context(nc.semaphore(f"weights_in_{i}")) for i in range(RING)]
        self.stored = ctx.enter_context(nc.semaphore("stored"))
        self.stage_n, self.spent = 0, []

    def room(self, n):
        self.at += n
        return self.mem[:, self.at - n:self.at]

    def plan(self, name, views):
        self.range_of[name] = (len(self.loads), len(self.loads) + len(views))
        self.loads += views

    def slot(self, n, k, cols):
        o = (n % RING) * SLOT
        return self.ring[:, o:o + k * cols].rearrange("p (k n) -> p k n", k=k)

    def issue(self, sp, stage, done, freed):
        lo, hi = self.range_of[stage]
        for n in range(self.issued, min(hi + RING, len(self.loads))):
            if n - RING >= lo:
                sp.wait_ge(done, freed(n - RING - lo))
            src = self.loads[n]
            sp.dma_start(self.slot(n, src.shape[1], src.shape[2]), src).then_inc(self.slot_in[n % RING], 16)
            self.issued = n + 1

    def arrived(self, pe, n):
        pe.wait_ge(self.slot_in[n % RING], 16 * (n // RING + 1))


def chain(eng, sem):
    count = [0]

    def link(ins):
        count[0] += 1
        ins.then_inc(sem, 1)
        eng.wait_ge(sem, count[0])
    return link


def stage(c):
    c.stage_n += 1
    n = c.stage_n
    if len(c.spent) > 100:
        c.nc.clear_and_free_semaphores(c.spent)
        c.nc.all_engine_barrier()
        c.spent = []

    def sem(name):
        c.spent.append(c.nc.alloc_semaphore(f"{name}_{n}"))
        return c.spent[-1]
    return ExitStack(), sem


def rows_of(ap):
    return ap.rearrange("(u c) -> u c", c=128)


def load_inputs(c):
    nc, a = c.nc, c.a
    st, sem = stage(c)
    rows = c.arena[:, 0:512].rearrange("p (j c) -> p j c", j=4)
    taps = [a["ffn_conv"][l].rearrange("t (u c) -> t u c", c=128) for l in range(2)]
    batches = [
        [a["norm_g"].rearrange("l g (k c) -> (l g k) c", c=128), rows_of(a["c"][0]), rows_of(a["c_ctx"][0]),
         a["gdn_conv"][0].rearrange("t (u c) -> (t u) c", c=128)],
        [taps[0][0], taps[0][1], a["hy_conv"][0].rearrange("t (u c) -> (t u) c", c=128)],
        [taps[0][2], taps[1][0], rows_of(a["hy_bias"][0, 1])],
        [taps[1][1], taps[1][2]],
    ]
    sizes = [sum(v.shape[0] for v in b) for b in batches]
    with st, nc.Block() as block:
        table_in, rows_in, x_in, z_in = sem("table_in"), sem("rows_in"), sem("x_in"), sem("z_in")
        turned, columns = sem("turned"), sem("columns")
        n_rows = sum(len(b) for b in batches)

        @block.sync
        def _(sp):
            sp.dma_start(c.table, a["t_table"]).then_inc(table_in, 16)
            for j, views in enumerate(batches):
                r = 0
                for v in views:
                    sp.dma_start(rows[r:r + v.shape[0], j, :], v).then_inc(rows_in, 16)
                    r += v.shape[0]
            c.issue(sp, "start", None, None)

        @block.scalar
        def _(act):
            act.dma_start(c.x, a["x"][0].rearrange("(t p) d -> p t d", p=128)).then_inc(x_in, 16)
            act.dma_start(c.z, a["ctx"][0].rearrange("(t p) d -> p t d", p=128)).then_inc(z_in, 16)
            act.wait_ge(columns, 4)
            nc.scalar.activation(c.sc.rearrange("p k u -> p u k"),
                                 c.cols[:, 0, 64:80].rearrange("p (u k) -> p u k", u=2), ACT.Silu)
            act.wait_ge(x_in, 16)
            act.wait_ge(z_in, 16)

        @block.tensor
        def _(pe):
            pe.wait_ge(table_in, 16)
            pe.wait_ge(rows_in, 16 * n_rows)
            for j, n in enumerate(sizes):
                last = nc.tensor.transpose(c.ps[:, j, 0:n], rows[0:n, j, :], c.tab["ident"][0:n, 0:n])
                last.then_inc(turned, 1)

        @block.vector
        def _(dve):
            for j, n in enumerate(sizes):
                dve.wait_ge(turned, j + 1)
                nc.vector.tensor_copy(c.cols[:, j, 0:n], c.ps[:, j, 0:n]).then_inc(columns, 1)


def norm_col(c, l, g):
    o = (l * 4 + g) * 8
    return c.cols[:, 0, o:o + 8]


def gdn_tap(c, t, tile):
    return c.cols[:, 0, 80 + 12 * t + tile:81 + 12 * t + tile]


def hy_tap(c, t, tile):
    return c.cols[:, 1, 88 + 12 * t + tile:89 + 12 * t + tile]


def hy_bias_col(c, tile):
    return c.cols[:, 2, 88 + tile:89 + tile]


def ffn_tap(c, l, t, tile):
    j, o = {(0, 0): (1, 0), (0, 1): (1, 44), (0, 2): (2, 0), (1, 0): (2, 44), (1, 1): (3, 0), (1, 2): (3, 44)}[l, t]
    return c.cols[:, j, o + tile:o + tile + 1]


def modulation(c, l):
    nc, a = c.nc, c.a
    st, sem = stage(c)
    n6 = 6 * D
    mod = c.arena[:, 0:n6]
    bias = c.arena[:, n6:2 * n6]
    gain = c.arena[:, 2 * n6:2 * n6 + 2 * D].rearrange("p (v d) -> p v d", v=2)
    lo, _ = c.range_of[f"mod{l}"]
    n_chunks = n6 // 256
    columns_of = (0, 1, 3, 4)
    with st, nc.Block() as block:
        rows_in, product, drained = sem("rows_in"), sem("product"), sem("drained")
        gate_rows, turned, columns = sem("gate_rows"), sem("turned"), sem("columns")
        gate, spread = sem("gate"), sem("spread")

        @block.sync
        def _(sp):
            for r in range(2):
                sp.dma_start(bias[r:r + 1, :], a["b_mod"][l:l + 1, :]).then_inc(rows_in, 16)
                for w in range(2):
                    sp.dma_start(gain[r:r + 1, w, :], a["norm_g"][l, 1 + 2 * w:2 + 2 * w, :]).then_inc(rows_in, 16)
            c.issue(sp, f"mod{l}", product, lambda j: j + 1)

        @block.tensor
        def _(pe):
            for j in range(n_chunks):
                if j >= 4:
                    pe.wait_ge(drained, j - 3)
                c.arrived(pe, lo + j)
                w = c.slot(lo + j, KT, 256)
                for k in range(KT):
                    last = nc.tensor.matmul(c.ps[0:2, j % 4, 0:256], c.sc[:, k, :], w[:, k, :],
                                            start=k == 0, stop=k == KT - 1)
                last.then_inc(product, 1)
            pe.wait_ge(drained, n_chunks)
            for w, six in enumerate(columns_of):
                for k in range(KT):
                    last = nc.tensor.matmul(c.ps[:, 4, (w * KT + k) * 2:(w * KT + k) * 2 + 2],
                                            mod[0:2, six * D + k * 128:six * D + (k + 1) * 128], c.tab["ident"][0:2, 0:2],
                                            start=True, stop=True)
            last.then_inc(turned, 1)
            pe.wait_ge(gate_rows, 2)
            for n in range(8):
                w, r, half = n // 4, n // 2 % 2, n % 2
                if n >= 4:
                    pe.wait_ge(spread, n - 3)
                nc.tensor.matmul(c.ps[:, n % 4, :], c.tab["row_of"][0:2, r * 128:(r + 1) * 128],
                                 mod[0:2, (2, 5)[w] * D + half * 512:(2, 5)[w] * D + half * 512 + 512],
                                 start=True, stop=True).then_inc(gate, 1)

        @block.vector
        def _(dve):
            dve.wait_ge(rows_in, 96)
            for j in range(n_chunks):
                dve.wait_ge(product, j + 1)
                nc.vector.tensor_tensor(mod[0:2, j * 256:(j + 1) * 256], c.ps[0:2, j % 4, 0:256],
                                        bias[0:2, j * 256:(j + 1) * 256], ALU.add).then_inc(drained, 1)
            dve.wait_ge(drained, n_chunks)
            for w, six in enumerate((2, 5)):
                nc.vector.tensor_tensor(mod[0:2, six * D:(six + 1) * D], mod[0:2, six * D:(six + 1) * D],
                                        gain[0:2, w, :], ALU.mult).then_inc(gate_rows, 1)
            dve.wait_ge(turned, 1)
            nc.vector.tensor_copy(c.modc.rearrange("p v k u -> p (v k u)"), c.ps[:, 4, 0:64]).then_inc(columns, 1)
            dve.wait_ge(columns, 1)
            for m in range(2):
                for r in range(2):
                    nc.vector.scalar_tensor_tensor(c.coef[:, m, 0, r, :], c.modc[:, 2 * m + 1, :, r], 1.0,
                                                   norm_col(c, l, 2 * m), ALU.add, ALU.mult)
                    nc.vector.tensor_copy(c.coef[:, m, 1, r, :], c.modc[:, 2 * m, :, r])
            for n in range(8):
                w, r, half = n // 4, n // 2 % 2, n % 2
                dve.wait_ge(gate, n + 1)
                nc.vector.tensor_copy(c.gates[:, w, r, half * 512:half * 512 + 512], c.ps[:, n % 4, :]).then_inc(spread, 1)


def ht_view(c):
    return c.ht.rearrange("p (k t) -> p k t", k=KT)


def token_tile(c, t):
    return c.x[:, t, :] if t < TX else c.z[:, t - TX, :]


def norm_to_features(c, m, tiles):
    nc = c.nc
    st, sem = stage(c)
    junk = c.arena[:, 0:D]
    y = c.arena[:, D:3 * D].rearrange("p (b d) -> p b d", b=2)
    rstd = c.stat[:, 0:TT]
    ht = ht_view(c)
    with st, nc.Block() as block:
        act_chain, stats, scaled = sem("act_chain"), sem("stats"), sem("scaled")
        turned, act_out, dve_out = sem("turned"), sem("act_out"), sem("dve_out")

        @block.scalar
        def _(act):
            link = chain(act, act_chain)
            for t in tiles:
                link(nc.scalar.activation(junk, token_tile(c, t), ACT.Square, accum_out=rstd[:, t:t + 1]))
            n = len(tiles)
            link(nc.scalar.activation(rstd[:, 0:n], rstd[:, 0:n], ACT.Ln, bias=EPS, scale=1.0 / D))
            nc.scalar.activation(rstd[:, 0:n], rstd[:, 0:n], ACT.Exp, scale=-0.5).then_inc(stats, 1)
            for t in tiles:
                act.wait_ge(turned, 2 * t + 1)
                r = int(t >= TX)
                for k in range(4):
                    nc.scalar.activation(ht[:, k, t * 128:(t + 1) * 128], c.ps[:, (t % 4) * 2, k * 128:(k + 1) * 128],
                                         ACT.Identity, scale=c.coef[:, m, 0, r, k:k + 1],
                                         bias=c.coef[:, m, 1, r, k:k + 1]).then_inc(act_out, 1)

        @block.vector
        def _(dve):
            dve.wait_ge(stats, 1)
            for i in range(len(tiles) + 1):
                if i < len(tiles):
                    if i >= 2:
                        dve.wait_ge(turned, 2 * (i - 1))
                    nc.vector.tensor_scalar(y[:, i % 2, :], token_tile(c, tiles[i]), rstd[:, i:i + 1], None,
                                            ALU.mult).then_inc(scaled, 1)
                if i:
                    t = tiles[i - 1]
                    r = int(t >= TX)
                    dve.wait_ge(turned, 2 * i)
                    for k in range(4, KT):
                        nc.vector.tensor_scalar(ht[:, k, t * 128:(t + 1) * 128],
                                                c.ps[:, (t % 4) * 2 + 1, (k - 4) * 128:(k - 3) * 128],
                                                c.coef[:, m, 0, r, k:k + 1], c.coef[:, m, 1, r, k:k + 1],
                                                ALU.mult, ALU.add).then_inc(dve_out, 1)

        @block.tensor
        def _(pe):
            for t in tiles:
                if t >= 4:
                    pe.wait_ge(act_out, 4 * (t - 3))
                    pe.wait_ge(dve_out, 4 * (t - 3))
                pe.wait_ge(scaled, t + 1)
                for k in range(KT):
                    last = nc.tensor.transpose(c.ps[:, (t % 4) * 2 + k // 4, (k % 4) * 128:(k % 4 + 1) * 128],
                                               y[:, t % 2, k * 128:(k + 1) * 128], c.tab["ident"])
                    if k % 4 == 3:
                        last.then_inc(turned, 1)


def plan_all(c):
    a = c.a
    ktiles = lambda w: w.rearrange("(k p) n -> p k n", p=128)
    chunks = lambda w, n=256: [ktiles(w)[:, :, i:i + n] for i in range(0, w.shape[1], n)]
    down = lambda w: [ktiles(w)[:, h * 11:(h + 1) * 11, i:i + 128] for i in range(0, D, 128) for h in range(2)]

    def up(w):
        both = chunks(w)
        return [both[i] for j in range(11) for i in (j, 11 + j)]

    c.range_of["start"] = (0, 0)
    ab, cd = a["ab_w_in"][0], a["cd_w_in"][0]
    c.plan("mod0", chunks(a["w_mod"][0]))
    c.plan("diff_qk", chunks(ab[:, 2080:3104]))
    c.plan("diff_v", chunks(ab[:, 3104:3616]))
    c.plan("gdn_gates", chunks(ab[:, 2048:2080], 32))
    c.plan("gdn_gate", chunks(ab[:, 1536:2048]))
    c.plan("gdn_qkv", chunks(ab[:, 0:1536]))
    c.plan("ab_out", chunks(a["ab_w_out"][0]))
    c.plan("up0", up(a["ffn_w_up"][0]))
    c.plan("down0", down(a["ffn_w_down"][0]))
    c.plan("mod1", chunks(a["w_mod"][1]))
    c.plan("swa_q", chunks(cd[:, 0:512]))
    c.plan("swa_k", chunks(cd[:, 512:640], 128))
    c.plan("swa_v", chunks(cd[:, 640:768], 128))
    c.plan("hy_in", chunks(cd[:, 768:2304]))
    c.plan("cd_out", chunks(a["cd_w_out"][0]))
    c.plan("up1", up(a["ffn_w_up"][1]))
    c.plan("down1", down(a["ffn_w_down"][1]))


def project_features(c, name, n_tiles, dst, kind, z=N_Z, taps=None, x=N_X, cols=256):
    nc = c.nc
    st, sem = stage(c)
    lo, _ = c.range_of[name]
    ht = ht_view(c)
    per = cols // 128
    slots = 3
    work = c.arena[:, c.arena_size - 3072:].rearrange("p (n b t) -> p n b t", n=3, b=2)
    raw, turned_cos, turned_sin = work[:, 0], work[:, 1], work[:, 2]
    conv = kind.startswith("conv")
    per_tile = 2 if z else 1
    with st, nc.Block() as block:
        product, drained, done, last_out = sem("product"), sem("drained"), sem("done"), sem("last_out")
        rotated, dve_chain = sem("rotated"), sem("dve_chain")

        @block.sync
        def _(sp):
            c.issue(sp, name, product, lambda j: per * (j + 1))

        @block.tensor
        def _(pe):
            def rotate(n):
                pe.wait_ge(drained, per_tile * n + 1)
                if n >= 2:
                    pe.wait_ge(done, n - 1)
                nc.tensor.matmul(c.ps[:, 6 + n % 2, :], c.tab["rot"], raw[:, n % 2, :],
                                 start=True, stop=True).then_inc(rotated, 1)

            for n in range(n_tiles):
                if n >= slots:
                    pe.wait_ge(drained, per_tile * (n - slots + 1))
                    if conv:
                        pe.wait_ge(done, n - slots + 1)
                if n % per == 0:
                    c.arrived(pe, lo + n // per)
                w = c.slot(lo + n // per, KT, cols)[:, :, n % per * 128:n % per * 128 + 128]
                for k in range(KT):
                    last = nc.tensor.matmul(c.ps[:, 2 * (n % slots), :], w[:, k, :], ht[:, k, 0:N_X],
                                            start=k == 0, stop=k == KT - 1)
                    if z:
                        last = nc.tensor.matmul(c.ps[:, 2 * (n % slots) + 1, 0:z], w[:, k, :],
                                                ht[:, k, N_X:N_X + z], start=k == 0, stop=k == KT - 1)
                last.then_inc(product, 1)
                if kind == "rope" and n:
                    rotate(n - 1)
            if kind == "rope":
                rotate(n_tiles - 1)

        @block.scalar
        def _(act):
            def finish(n):
                act.wait_ge(done, n + 1)
                nc.scalar.activation(dst[:, n, :], dst[:, n, :], ACT.Silu).then_inc(last_out, 1)

            for n in range(n_tiles):
                act.wait_ge(product, n + 1)
                px, pz = c.ps[:, 2 * (n % slots), :], c.ps[:, 2 * (n % slots) + 1, 0:z]
                if kind == "rope":
                    if n >= 2:
                        act.wait_ge(done, n - 1)
                    nc.scalar.activation(raw[:, n % 2, :], px, ACT.Copy).then_inc(drained, 1)
                elif conv:
                    nc.scalar.activation(dst[:, n, 0:N_X], px, ACT.Identity, scale=taps(1, n)).then_inc(drained, 1)
                else:
                    nc.scalar.activation(dst[:, n, 0:N_X], px, ACT.Silu if kind == "silu" else ACT.Copy)\
                        .then_inc(drained, 1)
                if z:
                    if conv:
                        nc.scalar.activation(dst[:, n, N_X:N_X + z], pz, ACT.Identity,
                                             scale=taps(1, n)).then_inc(drained, 1)
                    else:
                        nc.scalar.activation(dst[:, n, N_X:N_X + z], pz, ACT.Silu if kind == "silu" else ACT.Copy)\
                            .then_inc(drained, 1)
                if kind == "conv_silu" and n:
                    finish(n - 1)
            if kind == "conv_silu":
                finish(n_tiles - 1)

        @block.vector
        def _(dve):
            link = chain(dve, dve_chain)
            for n in range(n_tiles):
                if kind == "rope":
                    dve.wait_ge(drained, per_tile * n + 1)
                    nc.vector.tensor_tensor(turned_cos[:, n % 2, :], raw[:, n % 2, :], c.tab["cos"], ALU.mult)
                    dve.wait_ge(rotated, n + 1)
                    link(nc.vector.tensor_tensor(turned_sin[:, n % 2, :], c.ps[:, 6 + n % 2, :], c.tab["sin"], ALU.mult))
                    nc.vector.tensor_tensor(dst[:, n, 0:N_X], turned_cos[:, n % 2, :], turned_sin[:, n % 2, :],
                                            ALU.add).then_inc(done, 1)
                elif conv:
                    dve.wait_ge(drained, per_tile * (n + 1))
                    convolve(c, link, dst[:, n, :], c.ps[:, 2 * (n % slots), :], c.ps[:, 2 * (n % slots) + 1, :], z,
                             lambda t: taps(t, n)).then_inc(done, 1)


def convolve(c, link, y, px, pz, z, tap):
    v = c.nc.vector
    parts = [(y[:, 0:N_X], px, N_X)] + ([(y[:, N_X:N_X + z], pz, z)] if z else [])
    for out, src, n in parts:
        step = v.scalar_tensor_tensor(out[:, 1:n], src[:, 0:n - 1], tap(0), out[:, 1:n], ALU.mult, ALU.add)
        if n == parts[-1][2]:
            link(step)
    for out, src, n in parts:
        step = v.scalar_tensor_tensor(out[:, 0:n - 1], src[:, 1:n], tap(2), out[:, 0:n - 1], ALU.mult, ALU.add)
    return step


def project_tokens(c, name, src, k_tiles, loads_per, cols, tiles, dst):
    nc = c.nc
    st, sem = stage(c)
    lo, hi = c.range_of[name]
    n_chunks = (hi - lo) // loads_per
    k_per = k_tiles // loads_per
    units = [(j, t) for j in range(n_chunks) for t in tiles]
    with st, nc.Block() as block:
        product, act_out, dve_out = sem("product"), sem("act_out"), sem("dve_out")

        @block.sync
        def _(sp):
            c.issue(sp, name, product, lambda j: len(tiles) * (j // loads_per + 1))

        @block.tensor
        def _(pe):
            for n, (j, t) in enumerate(units):
                if n >= 8:
                    pe.wait_ge(dve_out if n % 2 else act_out, n // 2 - 3)
                if t == tiles[0]:
                    for m in range(loads_per):
                        c.arrived(pe, lo + j * loads_per + m)
                for k in range(k_tiles):
                    w = c.slot(lo + j * loads_per + k // k_per, k_per, cols)[:, k % k_per, :]
                    last = nc.tensor.matmul(c.ps[:, n % 8, 0:cols], src[:, k, t * 128:(t + 1) * 128], w,
                                            start=k == 0, stop=k == k_tiles - 1)
                last.then_inc(product, 1)

        @block.scalar
        def _(act):
            for n, (j, t) in enumerate(units):
                if n % 2 == 0:
                    act.wait_ge(product, n + 1)
                    nc.scalar.activation(dst(t, j), c.ps[:, n % 8, 0:cols], ACT.Copy).then_inc(act_out, 1)

        @block.vector
        def _(dve):
            for n, (j, t) in enumerate(units):
                if n % 2 == 1:
                    dve.wait_ge(product, n + 1)
                    nc.vector.tensor_copy(dst(t, j), c.ps[:, n % 8, 0:cols]).then_inc(dve_out, 1)


def outc(c):
    return c.arena[:, 0:KT * N_ALL].rearrange("p (k t) -> p k t", k=KT)


def diff_buffers(c):
    o = KT * N_ALL
    qk = c.arena[:, o:o + 8 * N_ALL].rearrange("p (k t) -> p k t", k=8)
    v = c.arena[:, o + 8 * N_ALL:o + 8 * N_ALL + TT * 512].rearrange("p (t e) -> p t e", t=TT)
    return qk, v, o + 8 * N_ALL + TT * 512


def lambda_value(c):
    nc, a = c.nc, c.a
    st, sem = stage(c)
    lam = c.small[:, 0:256].rearrange("p (u d) -> p u d", u=4)
    prod = c.small[:, 256:384].rearrange("p (u d) -> p u d", u=2)
    dots = c.stat[:, 200:202]
    with st, nc.Block() as block:
        rows_in, multiplied, summed, exps, link_sem = (sem(n) for n in ("rows_in", "multiplied", "summed", "exps", "link"))

        @block.sync
        def _(sp):
            sp.dma_start(lam, a["diff_lambda"][0].partition_broadcast(128)).then_inc(rows_in, 16)
            sp.dma_start(c.stat[:, 204:205], a["diff_norm_g"][0].unsqueeze(1)).then_inc(rows_in, 16)

        @block.vector
        def _(dve):
            link = chain(dve, link_sem)
            dve.wait_ge(rows_in, 32)
            link(nc.vector.tensor_tensor(prod, lam[:, 0:4:2, :], lam[:, 1:4:2, :], ALU.mult))
            nc.vector.tensor_reduce(dots, prod, AX.X, ALU.add).then_inc(summed, 1)
            dve.wait_ge(exps, 1)
            link(nc.vector.tensor_tensor(c.stat[:, 203:204], dots[:, 1:2], dots[:, 0:1], ALU.subtract))
            link(nc.vector.tensor_scalar(c.stat[:, 203:204], c.stat[:, 203:204], -LAM_INIT, None, ALU.add))
            link(nc.vector.tensor_scalar(c.stat[:, 204:205], c.stat[:, 204:205], 1.0 - LAM_INIT, None, ALU.mult))

        @block.scalar
        def _(act):
            act.wait_ge(summed, 1)
            nc.scalar.activation(dots, dots, ACT.Exp).then_inc(exps, 1)


def diff_attention(c):
    nc = c.nc
    st, sem = stage(c)
    qk, v, o = diff_buffers(c)
    out = outc(c)
    prob = c.arena[:, o:o + 4 * N_ALL].rearrange("p (b s m) -> p b s m", b=2, s=2)
    o += 4 * N_ALL
    turned = c.arena[:, o:o + 2 * N_ALL].rearrange("p (b m) -> p b m", b=2)
    o += 2 * N_ALL
    mixed = c.arena[:, o:o + 256].rearrange("p (b e) -> p b e", b=2)
    top, neg, total, sq = (c.stat[:, i * 4:i * 4 + 4].rearrange("p (b s) -> p b s", b=2) for i in range(4))
    rstd = c.stat[:, 16:18]
    junk = c.small[:, 0:128]
    units = [(q, h, 0) for h in range(4) for q in range(TX)] + [(q, h, N_X) for h in range(4) for q in (TX, TX + 1)]
    n_units = len(units)
    scale = HEAD ** -0.5
    flat = c.ps.rearrange("p b n -> p (b n)")
    score = lambda s: flat[:, s * 1024:s * 1024 + N_ALL]
    turn = flat[:, 2048:2048 + N_ALL]
    with st, nc.Block() as block:
        scored, maxed, exped, weighed = sem("scored"), sem("maxed"), sem("exped"), sem("weighed")
        turned_ps, turned_sb, valued, stats = sem("turned_ps"), sem("turned_sb"), sem("valued"), sem("stats")
        normed, back, written = sem("normed"), sem("back"), sem("written")
        dve_chain, act_chain = sem("dve_chain"), sem("act_chain")

        def keys(u):
            return range(units[u][2] // 128, TT)

        @block.tensor
        def _(pe):
            for i in range(n_units + 3):
                if i < n_units:
                    q, h, first = units[i]
                    for s in range(2):
                        if i:
                            pe.wait_ge(exped, 2 * (i - 1) + s + 1)
                        r = slice(64 * s, 64 * s + 64)
                        lhs = qk[r, h, q * 128:(q + 1) * 128]
                        if not first:
                            nc.tensor.matmul(score(s)[:, 0:N_X], lhs, qk[r, 4 + h, 0:N_X], start=True, stop=True)
                        nc.tensor.matmul(score(s)[:, N_X:N_ALL], lhs, qk[r, 4 + h, N_X:N_ALL],
                                         start=True, stop=True).then_inc(scored, 1)
                if 0 <= i - 1 < n_units:
                    u = i - 1
                    pe.wait_ge(weighed, u + 1)
                    if u:
                        pe.wait_ge(turned_sb, u)
                    for m in keys(u):
                        last = nc.tensor.transpose(turn[:, m * 128:(m + 1) * 128],
                                                   prob[:, u % 2, 0, m * 128:(m + 1) * 128], c.tab["ident"])
                    last.then_inc(turned_ps, 1)
                if 0 <= i - 2 < n_units:
                    u = i - 2
                    pe.wait_ge(turned_sb, u + 1)
                    if u:
                        pe.wait_ge(normed, u)
                    h = units[u][1]
                    for m in keys(u):
                        last = nc.tensor.matmul(c.ps[:, 6, 0:128], turned[:, u % 2, m * 128:(m + 1) * 128],
                                                v[:, m, h * 128:(h + 1) * 128], start=m == keys(u)[0], stop=m == TT - 1)
                    last.then_inc(valued, 1)
                if 0 <= i - 3 < n_units:
                    u = i - 3
                    pe.wait_ge(normed, u + 1)
                    if u:
                        pe.wait_ge(written, u)
                    nc.tensor.transpose(c.ps[:, 7, 0:128], mixed[:, u % 2, :], c.tab["ident"]).then_inc(back, 1)

        @block.scalar
        def _(act):
            link = chain(act, act_chain)
            for i in range(n_units + 2):
                if i < n_units:
                    first = units[i][2]
                    for s in range(2):
                        act.wait_ge(maxed, 2 * i + s + 1)
                        if i >= 2:
                            act.wait_ge(turned_ps, i - 1)
                        nc.scalar.activation(prob[:, i % 2, s, first:N_ALL], score(s)[:, first:N_ALL], ACT.Exp,
                                             bias=neg[:, i % 2, s:s + 1], scale=scale,
                                             accum_out=total[:, i % 2, s:s + 1]).then_inc(exped, 1)
                if 0 <= i - 1 < n_units:
                    u = i - 1
                    act.wait_ge(turned_ps, u + 1)
                    if u >= 2:
                        act.wait_ge(valued, u - 1)
                    first = units[u][2]
                    nc.scalar.activation(turned[:, u % 2, first:N_ALL], turn[:, first:N_ALL],
                                         ACT.Copy).then_inc(turned_sb, 1)
                if 0 <= i - 2 < n_units:
                    u = i - 2
                    act.wait_ge(valued, u + 1)
                    if u >= 2:
                        act.wait_ge(normed, u - 1)
                    link(nc.scalar.activation(junk, c.ps[:, 6, 0:128], ACT.Square, accum_out=rstd[:, u % 2:u % 2 + 1]))
                    link(nc.scalar.activation(rstd[:, u % 2:u % 2 + 1], rstd[:, u % 2:u % 2 + 1], ACT.Ln,
                                              bias=EPS, scale=1.0 / 128))
                    nc.scalar.activation(rstd[:, u % 2:u % 2 + 1], rstd[:, u % 2:u % 2 + 1], ACT.Exp,
                                         scale=-0.5).then_inc(stats, 1)

        @block.vector
        def _(dve):
            link = chain(dve, dve_chain)
            for i in range(n_units + 3):
                if i < n_units:
                    first = units[i][2]
                    for s in range(2):
                        dve.wait_ge(scored, 2 * i + s + 1)
                        link(nc.vector.reduce_max(top[:, i % 2, s:s + 1], score(s)[:, first:N_ALL], AX.X))
                        nc.vector.tensor_scalar(neg[:, i % 2, s:s + 1], top[:, i % 2, s:s + 1], -scale, None,
                                                ALU.mult).then_inc(maxed, 1)
                if 0 <= i - 1 < n_units:
                    u = i - 1
                    first = units[u][2]
                    b = u % 2
                    dve.wait_ge(exped, 2 * u + 2)
                    link(nc.vector.reciprocal(total[:, b, :], total[:, b, :]))
                    link(nc.vector.tensor_tensor(sq[:, b, 1:2], total[:, b, 1:2], c.stat[:, 203:204], ALU.mult))
                    link(nc.vector.tensor_scalar(prob[:, b, 1, first:N_ALL], prob[:, b, 1, first:N_ALL],
                                                 sq[:, b, 1:2], None, ALU.mult))
                    nc.vector.scalar_tensor_tensor(prob[:, b, 0, first:N_ALL], prob[:, b, 0, first:N_ALL],
                                                   total[:, b, 0:1], prob[:, b, 1, first:N_ALL],
                                                   ALU.mult, ALU.add).then_inc(weighed, 1)
                if 0 <= i - 2 < n_units:
                    u = i - 2
                    dve.wait_ge(stats, u + 1)
                    if u >= 2:
                        dve.wait_ge(back, u - 1)
                    nc.vector.tensor_scalar(mixed[:, u % 2, :], c.ps[:, 6, 0:128], rstd[:, u % 2:u % 2 + 1], None,
                                            ALU.mult).then_inc(normed, 1)
                if 0 <= i - 3 < n_units:
                    u = i - 3
                    q, h, _ = units[u]
                    dve.wait_ge(back, u + 1)
                    nc.vector.tensor_scalar(out[:, 4 + h, q * 128:(q + 1) * 128], c.ps[:, 7, 0:128],
                                            c.stat[:, 204:205], None, ALU.mult).then_inc(written, 1)


def gdn_buffers(c):
    o = KT * N_ALL
    qkv = c.arena[:, o:o + 12 * N_ALL].rearrange("p (k t) -> p k t", k=12)
    gate = c.arena[:, o + 12 * N_ALL:o + 16 * N_ALL].rearrange("p (k t) -> p k t", k=4)
    return qkv, gate, o + 16 * N_ALL


SMALL = ("g", "beta", "gc", "exp_gc", "exp_tail", "exp_last", "beta_exp_gc", "work")


def small(c, name):
    i = SMALL.index(name)
    return c.small[:, 96 * i:96 * i + 96]


def chunk_of(step, direction):
    if step < CZ:
        return N_X + CHUNK * (step if direction == 0 else CZ - 1 - step)
    return CHUNK * (step - CZ if direction == 0 else CX - 1 - (step - CZ))


def gdn_gates(c):
    nc, a = c.nc, c.a
    st, sem = stage(c)
    lo, _ = c.range_of["gdn_gates"]
    ht = ht_view(c)
    ba = gdn_buffers(c)[1][0:32, 0, :]
    raw = c.arena[:, c.arena_size - 192:].rearrange("p (s v) -> p s v", v=8)
    va = c.arena[:, c.arena_size - 400:c.arena_size - 384]
    rates = va[:, 0:16].rearrange("p (v s) -> p v s", v=2)
    by_head = c.arena[:, c.arena_size - 384:c.arena_size - 352].rearrange("p (i s) -> p i s", i=2)
    s24 = lambda n: small(c, n).rearrange("p (s v) -> p s v", v=4)
    by_dir = lambda ap, d: ap.rearrange("p (s u v) -> p s u v", u=2, v=4)[:, :, d, :]
    with st, nc.Block() as block:
        consts_in, product, drained, picked, summed = (sem(n) for n in ("consts_in", "product", "drained", "picked", "summed"))
        act_step, dve_step, rates_in = sem("act_step"), sem("dve_step"), sem("rates_in")

        @block.sync
        def _(sp):
            for i, name in enumerate(("gdn_a_log", "gdn_dt_bias")):
                sp.dma_start(by_head[:, i, :], a[name][0].rearrange("u h -> (u h)").partition_broadcast(128))\
                    .then_inc(consts_in, 16)
            c.issue(sp, "gdn_gates", product, lambda j: 1)

        @block.tensor
        def _(pe):
            c.arrived(pe, lo)
            w = c.slot(lo, KT, 32)
            for x, n, bank in ((0, N_X, 0), (N_X, N_Z, 1)):
                for k in range(KT):
                    last = nc.tensor.matmul(c.ps[0:32, bank, 0:n], w[:, k, :], ht[:, k, x:x + n],
                                            start=k == 0, stop=k == KT - 1)
            last.then_inc(product, 1)
            pe.wait_ge(drained, 1)
            pick = c.tab["pick"][0:32, :].rearrange("p (u h v) -> p u h v", u=2, h=2)
            for s in range(STEPS):
                for r in range(2):
                    t0 = chunk_of(s, r)
                    for hh in range(2):
                        last = nc.tensor.matmul(c.ps[64 * hh:64 * hh + 64, 2, (2 * s + r) * 8:(2 * s + r) * 8 + 8],
                                                ba[:, t0:t0 + CHUNK], pick[:, r, hh, :], start=True, stop=True)
            last.then_inc(picked, 1)
            pe.wait_ge(dve_step, 10)
            for r in range(2):
                nc.tensor.matmul(c.ps[:, 3 + r, 0:48], c.tab["tri2"][:, r * 128:(r + 1) * 128], by_dir(small(c, "g"), r),
                                 start=True, stop=True)
            nc.tensor.matmul(c.ps[:, 5, 0:96], c.tab["heads"], small(c, "g"), start=True, stop=True).then_inc(summed, 1)

        @block.vector
        def _(dve):
            v = nc.vector
            link = chain(dve, dve_step)
            dve.wait_ge(product, 1)
            v.tensor_copy(ba[:, 0:N_X], c.ps[0:32, 0, :])
            v.tensor_copy(ba[:, N_X:N_ALL], c.ps[0:32, 1, 0:N_Z]).then_inc(drained, 1)
            dve.wait_ge(picked, 1)
            link(v.tensor_copy(raw.rearrange("p s v -> p (s v)"), c.ps[:, 2, 0:192]))
            dve.wait_ge(consts_in, 32)
            for hh in range(2):
                half = slice(64 * hh, 64 * hh + 64)
                last = v.tensor_copy(rates[half], by_head[half, :, hh::2])
            last.then_inc(rates_in, 1)
            dve.wait_ge(rates_in, 1)
            alpha = raw[:, :, 4:8]
            dt = rates[:, 1, :].rearrange("p (u v) -> p u v", u=2).unsqueeze(1).to_broadcast([128, STEPS, 2, 4])
            link(v.tensor_tensor(alpha.rearrange("p (s u) v -> p s u v", u=2),
                                 alpha.rearrange("p (s u) v -> p s u v", u=2), dt, ALU.add))
            link(v.tensor_scalar(s24("work"), alpha, -1.0, None, ALU.mult))
            link(v.tensor_tensor(s24("work"), s24("work"), alpha, ALU.min))
            dve.wait_ge(act_step, 4)
            link(v.tensor_scalar(s24("beta"), s24("beta"), 1.0, None, ALU.add))
            link(v.reciprocal(s24("beta"), s24("beta")))
            link(v.tensor_scalar(s24("g"), alpha, 0.0, None, ALU.max))
            link(v.tensor_tensor(s24("g"), s24("g"), s24("work"), ALU.add))
            rate = rates[:, 0, :].rearrange("p (u v) -> p u v", u=2).unsqueeze(1).to_broadcast([128, STEPS, 2, 4])
            g4 = small(c, "g").rearrange("p (s u v) -> p s u v", u=2, v=4)
            link(v.tensor_tensor(g4, g4, rate, ALU.mult))
            link(v.tensor_scalar(s24("g"), s24("g"), -1.0, None, ALU.mult))
            dve.wait_ge(summed, 1)
            for r in range(2):
                link(v.tensor_copy(by_dir(small(c, "gc"), r), c.ps[:, 3 + r, 0:48].rearrange("p (s v) -> p s v", v=4)))
            link(v.tensor_copy(small(c, "exp_last"), c.ps[:, 5, 0:96]))
            link(v.tensor_tensor(small(c, "exp_tail"), small(c, "exp_last"), small(c, "gc"), ALU.subtract))
            dve.wait_ge(act_step, 7)
            link(v.tensor_tensor(small(c, "beta_exp_gc"), small(c, "beta"), small(c, "exp_gc"), ALU.mult))

        @block.scalar
        def _(act):
            link = chain(act, act_step)
            act.wait_ge(dve_step, 1)
            link(nc.scalar.activation(s24("beta"), raw[:, :, 0:4], ACT.Exp, scale=-1.0))
            act.wait_ge(dve_step, 4)
            link(nc.scalar.activation(s24("work"), s24("work"), ACT.Exp))
            link(nc.scalar.activation(rates[:, 0, :], rates[:, 0, :], ACT.Exp))
            link(nc.scalar.activation(s24("work"), s24("work"), ACT.Ln, bias=1.0))
            act.wait_ge(dve_step, 14)
            nc.scalar.activation(small(c, "exp_gc"), small(c, "gc"), ACT.Exp).then_inc(act_step, 1)
            nc.scalar.activation(small(c, "exp_last"), small(c, "exp_last"), ACT.Exp).then_inc(act_step, 1)
            nc.scalar.activation(small(c, "exp_tail"), small(c, "exp_tail"), ACT.Exp).then_inc(act_step, 1)


def head_norm(c, buf, tiles, n_sum, extra, finish, work_at):
    nc = c.nc
    st, sem = stage(c)
    sq = work_at[:, 0:2 * N_ALL].rearrange("p (b t) -> p b t", b=2)
    root = work_at[:, 2 * N_ALL:4 * N_ALL].rearrange("p (b t) -> p b t", b=2)
    flat = c.ps.rearrange("p b n -> p (b n)")
    with st, nc.Block() as block:
        squared, summed, rooted, act_chain, done, dve_chain = \
            (sem(n) for n in ("squared", "summed", "rooted", "act_chain", "done", "dve_chain"))

        @block.tensor
        def _(pe):
            for n in range(len(tiles)):
                pe.wait_ge(squared, n + 1)
                if n >= 4:
                    pe.wait_ge(rooted, n - 3)
                s = (n % 4) * 2
                nc.tensor.matmul(c.ps[:, s, :], c.tab["heads"], sq[:, n % 2, 0:N_X], start=True, stop=True)
                nc.tensor.matmul(c.ps[:, s + 1, 0:N_Z], c.tab["heads"], sq[:, n % 2, N_X:N_ALL],
                                 start=True, stop=True).then_inc(summed, 1)

        @block.scalar
        def _(act):
            link = chain(act, act_chain)

            def square(n):
                if n < len(tiles):
                    if n >= 2:
                        act.wait_ge(summed, n - 1)
                    nc.scalar.activation(sq[:, n % 2, :], buf[:, tiles[n], :], ACT.Square).then_inc(squared, 1)

            square(0)
            for n in range(len(tiles)):
                square(n + 1)
                act.wait_ge(summed, n + 1)
                if n >= 2:
                    act.wait_ge(done, n - 1)
                link(nc.scalar.activation(root[:, n % 2, :], flat[:, (n % 4) * 1024:(n % 4) * 1024 + N_ALL],
                                          ACT.Ln, bias=EPS, scale=1.0 / n_sum))
                nc.scalar.activation(root[:, n % 2, :], root[:, n % 2, :], ACT.Exp, bias=extra(n),
                                     scale=-0.5).then_inc(rooted, 1)

        @block.vector
        def _(dve):
            link = chain(dve, dve_chain)
            for n in range(len(tiles)):
                dve.wait_ge(rooted, n + 1)
                finish(link, buf[:, tiles[n], :], root[:, n % 2, :], n).then_inc(done, 1)


def delta_rule(c):
    nc = c.nc
    st, sem = stage(c)
    qkv, gate, o = gdn_buffers(c)
    out = outc(c)
    pool = [c.arena[:, o + 512 * i:o + 512 * i + 512] for i in range((c.arena_size - o) // 512)]
    pool += [c.ht[:, 512 * i:512 * i + 512] for i in range(KT * N_ALL // 512)]
    take = lambda: pool.pop()
    two = lambda: [take(), take()]
    inv_t, v_beta, w_neg, q_k, q_dec, k_tail = (two() for _ in range(6))
    A, k_beta, inv, T, v_new, S = (take() for _ in range(6))
    work, dist = inv, T
    four = lambda ap: ap.rearrange("p (u v e) -> p u v e", u=2, v=4)
    rows = lambda name, s: small(c, name)[:, 8 * s:8 * s + 8].unsqueeze(2).to_broadcast([128, 8, 64])
    eight = lambda ap: ap.rearrange("p (n e) -> p n e", n=8)
    table = lambda ap: ap.rearrange("p (u e) -> p u e", u=2).unsqueeze(2).to_broadcast([128, 2, 4, 64])
    eye = c.tab["eye"].unsqueeze(1).to_broadcast([128, 8, 64])
    mask_t = lambda n: table(c.tab["mt"][:, n * 128:(n + 1) * 128])
    NL = len(LEVELS)
    blocks = [(r, p, hh, slice(64 * hh, 64 * hh + 64), slice((r * 4 + p) * 64, (r * 4 + p) * 64 + 64))
              for r in range(2) for p in range(4) for hh in range(2)]
    B_GR, B_KK, B_QK, B_K, B_V, B_T, B_ZT, B_XT = range(8)

    with st, nc.Block() as block:
        names = ("projected", "masked_dist", "exps", "gathered", "a_ready", "first_t", "level_t", "level_masked",
                 "inv_ready", "inv_z", "w_ps", "w_ready", "v_ps", "v_ready", "out_ps", "state_ps", "state",
                 "out_added", "q_scaled", "dve_chain", "state_zero", "out_copied")
        s_ = {n: sem(n) for n in names}

        @block.tensor
        def _(pe):
            mm = nc.tensor.matmul

            def prepare(s):
                if s:
                    pe.wait_ge(s_["w_ready"], s)
                for r, p, hh, pa, fr in blocks:
                    g = small(c, "g")[pa, 8 * s + 4 * r + p:8 * s + 4 * r + p + 1].to_broadcast([64, 64])
                    last = mm(c.ps[pa, B_GR, fr], g, c.tab["tri"][pa, 64 * r:64 * r + 64], start=True, stop=True)
                last.then_inc(s_["projected"], 1)
                if s >= 2:
                    pe.wait_ge(s_["v_ready"], s - 1)
                for r, p, hh, pa, fr in blocks:
                    t0 = chunk_of(s, r)
                    k = qkv[pa, 4 + p, t0:t0 + 64]
                    last = mm(c.ps[pa, B_KK, fr], k, k, start=True, stop=True)
                last.then_inc(s_["projected"], 1)
                if s >= 2:
                    pe.wait_ge(s_["out_added"], s - 1)
                for r, p, hh, pa, fr in blocks:
                    t0 = chunk_of(s, r)
                    last = mm(c.ps[pa, B_QK, fr], qkv[pa, 4 + p, t0:t0 + 64], qkv[pa, p, t0:t0 + 64],
                              start=True, stop=True)
                last.then_inc(s_["projected"], 1)
                if s:
                    pe.wait_ge(s_["state"], s)
                for r, p, hh, pa, fr in blocks:
                    t0 = chunk_of(s, r)
                    last = mm(c.ps[pa, B_K, fr], qkv[pa, 4 + p, t0:t0 + 64], c.tab["ident"][pa, pa], start=True, stop=True)
                last.then_inc(s_["projected"], 1)
                for r, p, hh, pa, fr in blocks:
                    t0 = chunk_of(s, r)
                    last = mm(c.ps[pa, B_V, fr], qkv[pa, 8 + p, t0:t0 + 64], c.tab["ident"][pa, pa], start=True, stop=True)
                last.then_inc(s_["projected"], 1)

            def transposed_a(s, n):
                if n == 0:
                    pe.wait_ge(s_["a_ready"], s + 1)
                else:
                    pe.wait_ge(s_["inv_z"], NL * s + n)
                for r, p, hh, pa, fr in blocks:
                    rhs = c.tab["eye"][pa, :] if n == 0 else inv_t[s % 2][pa, fr]
                    last = mm(c.ps[pa, B_T, fr], A[pa, fr], rhs, start=True, stop=True)
                last.then_inc(s_["level_t"], 1)

            def products(s, n):
                pe.wait_ge(s_["level_masked"], NL * s + n + 1)
                for r, p, hh, pa, fr in blocks:
                    last = mm(c.ps[pa, B_ZT, fr], inv[pa, fr], T[pa, fr], start=True, stop=True)
                last.then_inc(s_["inv_ready"], 1)
                if n < NL - 1:
                    for r, p, hh, pa, fr in blocks:
                        last = mm(c.ps[pa, B_XT, fr], T[pa, fr], inv[pa, fr], start=True, stop=True)
                    last.then_inc(s_["inv_ready"], 1)

            def w_product(s):
                pe.wait_ge(s_["inv_z"], NL * (s + 1))
                pe.wait_ge(s_["gathered"], s + 1)
                for r, p, hh, pa, fr in blocks:
                    last = mm(c.ps[pa, B_GR, fr], k_beta[pa, fr], inv_t[s % 2][pa, fr], start=True, stop=True)
                last.then_inc(s_["w_ps"], 1)

            def new_values(s):
                pe.wait_ge(s_["w_ready"], s + 1)
                pe.wait_ge(s_["state"], s + 1)
                for r, p, hh, pa, fr in blocks:
                    mm(c.ps[pa, B_KK, fr], inv_t[s % 2][pa, fr], v_beta[s % 2][pa, fr], start=True, stop=False)
                    last = mm(c.ps[pa, B_KK, fr], w_neg[s % 2][pa, fr], S[pa, fr], start=False, stop=True)
                last.then_inc(s_["v_ps"], 1)

            def outputs(s):
                pe.wait_ge(s_["v_ready"], s + 1)
                pe.wait_ge(s_["q_scaled"], s + 1)
                for r, p, hh, pa, fr in blocks:
                    mm(c.ps[pa, B_QK, fr], S[pa, fr], q_dec[s % 2][pa, fr], start=True, stop=False)
                    last = mm(c.ps[pa, B_QK, fr], v_new[pa, fr], q_k[s % 2][pa, fr], start=False, stop=True)
                last.then_inc(s_["out_ps"], 1)
                for r, p, hh, pa, fr in blocks:
                    last = mm(c.ps[pa, B_K, fr], k_tail[s % 2][pa, fr], v_new[pa, fr], start=True, stop=True)
                last.then_inc(s_["state_ps"], 1)

            for s in range(STEPS + 1):
                if s < STEPS:
                    prepare(s)
                    for n in range(NL):
                        transposed_a(s, n)
                        if s and n == 1:
                            new_values(s - 1)
                        if s and n == 3:
                            outputs(s - 1)
                        if n:
                            products(s, n)
                    w_product(s)
                else:
                    new_values(s - 1)
                    outputs(s - 1)

        @block.scalar
        def _(act):
            for s in range(STEPS + 1):
                if s < STEPS:
                    act.wait_ge(s_["masked_dist"], 2 * s + 1)
                    nc.scalar.activation(A, A, ACT.Exp).then_inc(s_["exps"], 1)
                    if s >= 2:
                        act.wait_ge(s_["out_ps"], s - 1)
                    nc.scalar.activation(q_dec[s % 2], c.ps[:, B_GR, :], ACT.Exp).then_inc(s_["exps"], 1)
                    act.wait_ge(s_["masked_dist"], 2 * s + 2)
                    nc.scalar.activation(q_k[s % 2], q_k[s % 2], ACT.Exp).then_inc(s_["exps"], 1)
                if s:
                    act.wait_ge(s_["v_ps"], s)
                    nc.scalar.activation(v_new, c.ps[:, B_KK, :], ACT.Copy).then_inc(s_["v_ready"], 1)
                if s < STEPS:
                    act.wait_ge(s_["w_ps"], s + 1)
                    nc.scalar.activation(w_neg[s % 2], c.ps[:, B_GR, :], ACT.Copy, scale=-1.0).then_inc(s_["w_ready"], 1)

        @block.gpsimd
        def _(pool_):
            for s in range(STEPS):
                pool_.wait_ge(s_["exps"], 3 * s + 2)
                for r in range(2):
                    t0 = chunk_of(s, r)
                    last = nc.gpsimd.tensor_tensor(four(q_dec[s % 2])[:, r], four(q_dec[s % 2])[:, r],
                                                   qkv[:, 0:4, t0:t0 + 64], ALU.mult)
                last.then_inc(s_["q_scaled"], 1)

        @block.vector
        def _(dve):
            v = nc.vector
            link = chain(dve, s_["dve_chain"])
            v.memset(S, 0.0).then_inc(s_["state"], 1)

            def state(s):
                dve.wait_ge(s_["state_ps"], s + 1)
                link(v.tensor_tensor(eight(S), eight(S), rows("exp_last", s), ALU.mult))
                v.tensor_tensor(S, S, c.ps[:, B_K, :], ALU.add).then_inc(s_["state"], 1)
                first = s < CZ // 2 or CZ <= s < CZ + CX // 2
                for r in range(2):
                    t0 = chunk_of(s, r)
                    dst, src = out[:, 0:4, t0:t0 + 64], four(c.ps[:, B_QK, :])[:, r]
                    last = v.tensor_copy(dst, src) if first else v.tensor_tensor(dst, dst, src, ALU.add)
                last.then_inc(s_["out_added"], 1)

            for s in range(STEPS):
                b = s % 2
                dve.wait_ge(s_["projected"], 5 * s + 1)
                link(v.tensor_tensor(eight(dist), rows("gc", s), eight(c.ps[:, B_GR, :]), ALU.subtract))
                v.tensor_tensor(four(A), four(dist), table(c.tab["mask_a"]), ALU.add).then_inc(s_["masked_dist"], 1)
                if s >= 2:
                    dve.wait_ge(s_["out_ps"], s - 1)
                v.tensor_tensor(four(q_k[b]), table(c.tab["mask_q"]), four(dist), ALU.subtract).then_inc(s_["masked_dist"], 1)
                dve.wait_ge(s_["projected"], 5 * s + 2)
                link(v.tensor_tensor(eight(work), eight(c.ps[:, B_KK, :]), rows("beta", s), ALU.mult))
                dve.wait_ge(s_["exps"], 3 * s + 1)
                link(v.tensor_tensor(A, A, work, ALU.mult))
                link(v.tensor_tensor(four(work), four(A), table(c.tab["m1"]), ALU.mult))
                v.tensor_tensor(eight(inv), eye, eight(work), ALU.subtract).then_inc(s_["a_ready"], 1)
                dve.wait_ge(s_["level_t"], NL * s + 1)
                v.tensor_tensor(four(T), four(c.ps[:, B_T, :]), mask_t(0), ALU.mult).then_inc(s_["level_masked"], 1)
                dve.wait_ge(s_["level_masked"], NL * s + 1)
                v.tensor_tensor(eight(inv_t[b]), eye, eight(T), ALU.subtract).then_inc(s_["inv_z"], 1)
                dve.wait_ge(s_["projected"], 5 * s + 3)
                dve.wait_ge(s_["exps"], 3 * s + 3)
                v.tensor_tensor(q_k[b], q_k[b], c.ps[:, B_QK, :], ALU.mult)
                dve.wait_ge(s_["projected"], 5 * s + 5)
                v.tensor_tensor(eight(k_beta), eight(c.ps[:, B_K, :]), rows("beta_exp_gc", s), ALU.mult)
                v.tensor_tensor(eight(k_tail[b]), eight(c.ps[:, B_K, :]), rows("exp_tail", s), ALU.mult)
                v.tensor_tensor(eight(v_beta[b]), eight(c.ps[:, B_V, :]), rows("beta", s), ALU.mult).then_inc(s_["gathered"], 1)
                for n in range(1, NL):
                    dve.wait_ge(s_["level_t"], NL * s + n + 1)
                    v.tensor_tensor(four(T), four(c.ps[:, B_T, :]), mask_t(n), ALU.mult).then_inc(s_["level_masked"], 1)
                    if s and n == 4:
                        state(s - 1)
                    dve.wait_ge(s_["inv_ready"], (2 * (NL - 1) - 1) * s + 2 * n - 1)
                    v.tensor_tensor(inv_t[b], inv_t[b], c.ps[:, B_ZT, :], ALU.subtract).then_inc(s_["inv_z"], 1)
                    if n < NL - 1:
                        dve.wait_ge(s_["inv_ready"], (2 * (NL - 1) - 1) * s + 2 * n)
                        v.tensor_tensor(inv, inv, c.ps[:, B_XT, :], ALU.subtract).then_inc(s_["first_t"], 1)
            state(STEPS - 1)


def norm_qk(c):
    buf, _, o = gdn_buffers(c)
    head_norm(c, buf, range(8), 1, lambda n: math.log(GW // GH) * -0.5 if n < 4 else 0.0,
              lambda link, y, root, n: c.nc.vector.tensor_tensor(y, y, root, ALU.mult), c.arena[:, o:])


def gdn_output(c):
    nc, a = c.nc, c.a
    _, gate, o = gdn_buffers(c)
    gain = c.stat[:, 205:206]
    st, sem = stage(c)
    gain_in = sem("gain_in")
    with st:
        with nc.Block() as block:
            @block.sync
            def _(sp):
                for hh in range(2):
                    sp.dma_start(gain[64 * hh:64 * hh + 64, :], a["gdn_norm_g"][0].unsqueeze(1)).then_inc(gain_in, 16)
                sp.wait_ge(gain_in, 32)

    def finish(link, y, root, n):
        link(nc.vector.scalar_tensor_tensor(y, y, gain, root, ALU.mult, ALU.mult))
        return nc.vector.tensor_tensor(y, y, gate[:, n, :], ALU.mult)

    head_norm(c, outc(c), range(4), HEAD, lambda n: 0.0, finish, c.ht)


def mixed_rows(c):
    return c.ht.rearrange("p (t d) -> p t d", t=TT)


def add_branch(c, w, tiles):
    nc = c.nc
    st, sem = stage(c)
    y = mixed_rows(c)
    junk = c.arena[:, 0:D]
    rstd = c.stat[:, 0:TT]
    with st, nc.Block() as block:
        act_chain, stats, dve_chain = sem("act_chain"), sem("stats"), sem("dve_chain")

        @block.scalar
        def _(act):
            link = chain(act, act_chain)
            for t in tiles:
                link(nc.scalar.activation(junk, y[:, t, :], ACT.Square, accum_out=rstd[:, t:t + 1]))
            n = len(tiles)
            link(nc.scalar.activation(rstd[:, 0:n], rstd[:, 0:n], ACT.Ln, bias=EPS, scale=1.0 / D))
            nc.scalar.activation(rstd[:, 0:n], rstd[:, 0:n], ACT.Exp, scale=-0.5).then_inc(stats, 1)

        @block.vector
        def _(dve):
            link = chain(dve, dve_chain)
            dve.wait_ge(stats, 1)
            for t in tiles:
                link(nc.vector.scalar_tensor_tensor(y[:, t, :], y[:, t, :], rstd[:, t:t + 1],
                                                    c.gates[:, w, int(t >= TX), :], ALU.mult, ALU.mult))
                nc.vector.tensor_tensor(token_tile(c, t), token_tile(c, t), y[:, t, :], ALU.add)


def ffn_up(c, l, z):
    nc = c.nc
    st, sem = stage(c)
    name = f"up{l}"
    lo, _ = c.range_of[name]
    ht = ht_view(c)
    hidden, o = ffn_hidden(c)
    n_all = N_X + z
    gbuf = c.arena[:, o:o + 2 * N_ALL].rearrange("p (b t) -> p b t", b=2)
    with st, nc.Block() as block:
        product, drained, summed, gated, done, dve_chain = \
            (sem(n) for n in ("product", "drained", "summed", "gated", "done", "dve_chain"))

        @block.sync
        def _(sp):
            c.issue(sp, name, product, lambda j: 2 * (2 * (j // 2) + 2))

        @block.tensor
        def _(pe):
            for n in range(FT):
                for half in range(2):
                    chunk = lo + 2 * (n // 2) + half
                    if n % 2 == 0:
                        c.arrived(pe, chunk)
                    if n >= 2:
                        pe.wait_ge(summed, 2 * (n - 2) + half + 1)
                    w = c.slot(chunk, KT, 256)[:, :, n % 2 * 128:n % 2 * 128 + 128]
                    bank = 4 * (n % 2) + 2 * half
                    for k in range(KT):
                        last = nc.tensor.matmul(c.ps[:, bank, :], w[:, k, :], ht[:, k, 0:N_X],
                                                start=k == 0, stop=k == KT - 1)
                        if z:
                            last = nc.tensor.matmul(c.ps[:, bank + 1, 0:z], w[:, k, :], ht[:, k, N_X:N_X + z],
                                                    start=k == 0, stop=k == KT - 1)
                    last.then_inc(product, 1)

        def middle_tap(n, half):
            return ffn_tap(c, l, 1, n + half * FT)

        @block.scalar
        def _(act):
            def gate(n):
                act.wait_ge(summed, 2 * n + 2)
                nc.scalar.activation(gbuf[:, n % 2, 0:n_all], gbuf[:, n % 2, 0:n_all], ACT.Silu).then_inc(gated, 1)

            for n in range(FT):
                for half in range(2):
                    act.wait_ge(product, 2 * n + half + 1)
                    bank = 4 * (n % 2) + 2 * half
                    if half and n >= 2:
                        act.wait_ge(done, n - 1)
                    dst = gbuf[:, n % 2, :] if half else hidden[:, n, :]
                    nc.scalar.activation(dst[:, 0:N_X], c.ps[:, bank, :], ACT.Identity,
                                         scale=middle_tap(n, half)).then_inc(drained, 1)
                    if z:
                        nc.scalar.activation(dst[:, N_X:n_all], c.ps[:, bank + 1, 0:z], ACT.Identity,
                                             scale=middle_tap(n, half)).then_inc(drained, 1)
                    if half == 0 and n:
                        gate(n - 1)
            gate(FT - 1)

        @block.vector
        def _(dve):
            link = chain(dve, dve_chain)
            per = 2 if z else 1

            def multiply(n):
                dve.wait_ge(gated, n + 1)
                nc.vector.tensor_tensor(hidden[:, n, 0:n_all], hidden[:, n, 0:n_all], gbuf[:, n % 2, 0:n_all],
                                        ALU.mult).then_inc(done, 1)

            for n in range(FT):
                for half in range(2):
                    dve.wait_ge(drained, per * (2 * n + half + 1))
                    bank = 4 * (n % 2) + 2 * half
                    dst = gbuf[:, n % 2, :] if half else hidden[:, n, :]
                    convolve(c, link, dst, c.ps[:, bank, :], c.ps[:, bank + 1, :], z,
                             lambda t: ffn_tap(c, l, t, n + half * FT)).then_inc(summed, 1)
                    if half == 0 and n:
                        multiply(n - 1)
            multiply(FT - 1)


def ffn_hidden(c):
    return c.arena[:, 0:FT * N_ALL].rearrange("p (k t) -> p k t", k=FT), FT * N_ALL


def feed_forward(c, l, z, tiles):
    norm_to_features(c, 1, tiles)
    ffn_up(c, l, z)
    project_tokens(c, f"down{l}", ffn_hidden(c)[0], FT, 2, 128, tiles,
                   lambda t, j: mixed_rows(c)[:, t, j * 128:(j + 1) * 128])
    add_branch(c, 1, tiles)


def layer_ab(c):
    norm_to_features(c, 0, range(TT))
    project_features(c, "diff_qk", 8, diff_buffers(c)[0], "rope")
    project_tokens(c, "diff_v", ht_view(c), KT, 1, 256, range(TT),
                   lambda t, j: diff_buffers(c)[1][:, t, j * 256:(j + 1) * 256])
    lambda_value(c)
    diff_attention(c)
    gdn_gates(c)
    project_features(c, "gdn_gate", 4, gdn_buffers(c)[1], "silu")
    project_features(c, "gdn_qkv", 12, gdn_buffers(c)[0], "conv_silu", taps=lambda t, n: gdn_tap(c, t, n))
    norm_qk(c)
    delta_rule(c)
    gdn_output(c)
    project_tokens(c, "ab_out", outc(c), KT, 1, 256, range(TT),
                   lambda t, j: mixed_rows(c)[:, t, j * 256:(j + 1) * 256])
    add_branch(c, 0, range(TT))
    feed_forward(c, 0, N_Z, range(TT))


def cd_buffers(c):
    at = [0]

    def take(n):
        at[0] += n
        return c.arena[:, at[0] - n:at[0]]

    out = take(KT * N_X).rearrange("p (k t) -> p k t", k=KT)
    q = take(4 * N_X).rearrange("p (k t) -> p k t", k=4)
    k = take(N_ALL).rearrange("p (k t) -> p k t", k=1)
    k2 = take(2 * N_ALL).rearrange("p (g t) -> p g t", g=2)
    v = take(TT * 128).rearrange("p (t e) -> p t e", t=TT)
    prob = take(2 * 640).rearrange("p (b m) -> p b m", b=2)
    turned = take(2 * 640).rearrange("p (b m) -> p b m", b=2)
    u = take(12 * N_X).rearrange("p (k t) -> p k t", k=12)
    return out, q, k, k2, v, prob, turned, u


def window_attention(c):
    nc, a = c.nc, c.a
    st, sem = stage(c)
    out, q_, k_, k2, v_, prob, turned, _ = cd_buffers(c)
    top, neg, total, sink_exp = (c.stat[:, 2 * i:2 * i + 2] for i in range(4))
    sink, neg_sink = c.stat[:, 16:24], c.stat[:, 24:32]
    units = [(q, h) for q in range(TX) for h in range(8)]
    n_units = len(units)
    scale = HEAD ** -0.5
    flat = c.ps.rearrange("p b n -> p (b n)")
    score = lambda u: flat[:, (u % 2) * 1024:(u % 2) * 1024 + 640]
    turn = flat[:, 2048:2048 + 640]
    window = lambda q: range(max(0, q - 1), min(TX, q + 2))
    tiles = lambda q: [TX, TX + 1] + list(window(q))
    with st, nc.Block() as block:
        names = ("sink_in", "ready", "scored", "maxed", "exped", "sink_exped", "weighed", "turned_ps", "turned_sb",
                 "valued", "written", "dve_chain")
        sink_in, ready, scored, maxed, exped, sink_exped, weighed, turned_ps, turned_sb, valued, written, dve_chain = \
            (sem(n) for n in names)

        @block.sync
        def _(sp):
            sp.dma_start(sink, a["swa_sink"][0].partition_broadcast(128)).then_inc(sink_in, 16)

        @block.tensor
        def _(pe):
            pe.wait_ge(ready, 1)
            for i in range(n_units + 2):
                if i < n_units:
                    q, h = units[i]
                    if i >= 2:
                        pe.wait_ge(exped, i - 1)
                    pa = slice(64 * (h % 2), 64 * (h % 2) + 64)
                    lhs, keys, s = q_[pa, h // 2, q * 128:(q + 1) * 128], k2[pa, h // 4, :], score(i)
                    w = window(q)
                    first = w[0] * 128
                    nc.tensor.matmul(s[:, 0:N_Z], lhs, keys[:, N_X:N_ALL], start=True, stop=True)
                    last = nc.tensor.matmul(s[:, N_Z:512], lhs, keys[:, first:first + 256], start=True, stop=True)
                    if len(w) == 3:
                        last = nc.tensor.matmul(s[:, 512:640], lhs, keys[:, first + 256:first + 384],
                                                start=True, stop=True)
                    last.then_inc(scored, 1)
                if 0 <= i - 1 < n_units:
                    u = i - 1
                    q, h = units[u]
                    pe.wait_ge(weighed, u + 1)
                    if u:
                        pe.wait_ge(turned_sb, u)
                    for m in range(len(tiles(q))):
                        last = nc.tensor.transpose(turn[:, m * 128:(m + 1) * 128],
                                                   prob[:, u % 2, m * 128:(m + 1) * 128], c.tab["ident"])
                    last.then_inc(turned_ps, 1)
                if 0 <= i - 2 < n_units:
                    u = i - 2
                    q, h = units[u]
                    pe.wait_ge(turned_sb, u + 1)
                    if u >= 2:
                        pe.wait_ge(written, u - 1)
                    pa, g = slice(64 * (h % 2), 64 * (h % 2) + 64), h // 4
                    for m, t in enumerate(tiles(q)):
                        last = nc.tensor.matmul(c.ps[pa, 6 + u % 2, 0:128], v_[:, t, 64 * g:64 * g + 64],
                                                turned[:, u % 2, m * 128:(m + 1) * 128],
                                                start=m == 0, stop=m == len(tiles(q)) - 1)
                    last.then_inc(valued, 1)

        @block.scalar
        def _(act):
            for i in range(n_units + 1):
                if i < n_units:
                    q, h = units[i]
                    n = len(tiles(q)) * 128
                    act.wait_ge(maxed, i + 1)
                    if i >= 2:
                        act.wait_ge(turned_ps, i - 1)
                    nc.scalar.activation(prob[:, i % 2, 0:n], score(i)[:, 0:n], ACT.Exp, bias=neg[:, i % 2:i % 2 + 1],
                                         scale=scale, accum_out=total[:, i % 2:i % 2 + 1]).then_inc(exped, 1)
                    nc.scalar.activation(sink_exp[:, i % 2:i % 2 + 1], sink[:, h:h + 1], ACT.Exp,
                                         bias=neg[:, i % 2:i % 2 + 1]).then_inc(sink_exped, 1)
                if 0 <= i - 1 < n_units:
                    u = i - 1
                    n = len(tiles(units[u][0])) * 128
                    act.wait_ge(turned_ps, u + 1)
                    if u >= 2:
                        act.wait_ge(valued, u - 1)
                    nc.scalar.activation(turned[:, u % 2, 0:n], turn[:, 0:n], ACT.Copy).then_inc(turned_sb, 1)

        @block.vector
        def _(dve):
            v = nc.vector
            link = chain(dve, dve_chain)
            dve.wait_ge(sink_in, 16)
            for g in range(2):
                for hh in range(2):
                    v.tensor_copy(k2[64 * hh:64 * hh + 64, g, :], k_[64 * g:64 * g + 64, 0, :])
            v.tensor_scalar(neg_sink, sink, -1.0, None, ALU.mult).then_inc(ready, 1)
            dve.wait_ge(ready, 1)
            for i in range(n_units + 3):
                if i < n_units:
                    q, h = units[i]
                    w = window(q)
                    b = slice(i % 2, i % 2 + 1)
                    n = len(tiles(q)) * 128
                    dve.wait_ge(scored, i + 1)
                    if w[0] == q - 1:
                        link(v.tensor_tensor(score(i)[:, 256:384], score(i)[:, 256:384], c.tab["win_l"], ALU.add))
                    if w[-1] == q + 1:
                        link(v.tensor_tensor(score(i)[:, n - 128:n], score(i)[:, n - 128:n], c.tab["win_r"], ALU.add))
                    link(v.reduce_max(top[:, b], score(i)[:, 0:n], AX.X))
                    if i >= 2:
                        dve.wait_ge(sink_exped, i - 1)
                    v.tensor_scalar(neg[:, b], top[:, b], -scale, neg_sink[:, h:h + 1], ALU.mult, ALU.min)\
                        .then_inc(maxed, 1)
                if 0 <= i - 1 < n_units:
                    u = i - 1
                    b = slice(u % 2, u % 2 + 1)
                    n = len(tiles(units[u][0])) * 128
                    dve.wait_ge(sink_exped, u + 1)
                    link(v.tensor_tensor(total[:, b], total[:, b], sink_exp[:, b], ALU.add))
                    link(v.reciprocal(total[:, b], total[:, b]))
                    v.tensor_scalar(prob[:, u % 2, 0:n], prob[:, u % 2, 0:n], total[:, b], None, ALU.mult)\
                        .then_inc(weighed, 1)
                if 0 <= i - 3 < n_units:
                    u = i - 3
                    q, h = units[u]
                    pa = slice(64 * (h % 2), 64 * (h % 2) + 64)
                    dve.wait_ge(valued, u + 1)
                    v.tensor_copy(out[pa, h // 2, q * 128:(q + 1) * 128], c.ps[pa, 6 + u % 2, 0:128]).then_inc(written, 1)


class Hyena:

    def __init__(self, c):
        at = [KT * N_X]

        def take(n):
            at[0] += n
            return c.arena[:, at[0] - n:at[0]]

        self.out = c.arena[:, 0:KT * N_X].rearrange("p (k t) -> p k t", k=KT)
        four = lambda ap: ap.rearrange("p (s t n) -> p s t n", s=2, t=4)
        self.fwd, self.back, self.kern, self.lags = (four(take(4096)) for _ in range(4))
        self.spec = self.lags
        self.tmp = take(1536).rearrange("p (n c) -> p n c", n=3)
        ht = lambda i: c.ht[:, i * 2048:i * 2048 + 2048].rearrange("p (t n) -> p t n", t=4)
        self.v, self.x1, self.x2t = ht(0), ht(1), ht(2)
        self.z1t = self.x1
        self.decay = c.z.rearrange("p t d -> p (t d)").rearrange("p (t n) -> p t n", t=4)
        self.w3 = c.arena[0:HEAD, 4 * N_X:8 * N_X]
        spare = c.gates[:, :, 1, :].rearrange("p v (h n) -> p v h n", h=2)
        self.root, self.bias0, self.h1, self.h2 = spare[:, 0, 0], spare[:, 0, 1], spare[0:64, 1, 0], spare[0:64, 1, 1]
        self.small = c.small[:, 0:256]


def turn_tiles(c, jobs, copies=()):
    nc = c.nc
    st, sem = stage(c)
    with st, nc.Block() as block:
        turned, act_out, dve_out, copied = sem("turned"), sem("act_out"), sem("dve_out"), sem("copied")

        @block.tensor
        def _(pe):
            for n, (_, blocks) in enumerate(jobs):
                if n >= 8:
                    pe.wait_ge(dve_out if n % 2 else act_out, (n - 8) // 2 + 1)
                for i, b in enumerate(blocks):
                    last = nc.tensor.transpose(c.ps[:, n % 8, i * 128:(i + 1) * 128], b, c.tab["ident"])
                last.then_inc(turned, 1)

        @block.scalar
        def _(act):
            for n, (dst, _) in enumerate(jobs):
                if n % 2 == 0:
                    act.wait_ge(turned, n + 1)
                    nc.scalar.activation(dst, c.ps[:, n % 8, :], ACT.Copy).then_inc(act_out, 1)

        @block.vector
        def _(dve):
            for n, (dst, _) in enumerate(jobs):
                if n % 2:
                    dve.wait_ge(turned, n + 1)
                    nc.vector.tensor_copy(dst, c.ps[:, n % 8, :]).then_inc(dve_out, 1)

        @block.gpsimd
        def _(pool):
            for dst, src in copies:
                nc.gpsimd.tensor_copy(dst, src).then_inc(copied, 1)


def filter_features(c, hy):
    nc, a = c.nc, c.a
    st, sem = stage(c)
    w1, w2 = hy.small[0:33, 0:64], hy.small[0:64, 64:128]
    cols = hy.small[0:64, 128:132]
    n_, r_ = hy.tmp[0:64, 0, :], hy.tmp[0:64, 1, :]
    hi = float(np.float32(6.28125))
    lo = 2 * math.pi - hi
    magic = 12582912.0
    with st, nc.Block() as block:
        w_in, tables_in, product, chained, sined = (sem(n) for n in ("w_in", "tables_in", "product", "chained", "sined"))

        @block.sync
        def _(sp):
            sp.dma_start(w1, a["hy_w1"][0]).then_inc(w_in, 16)
            sp.dma_start(w2, a["hy_w2"][0]).then_inc(w_in, 16)
            for i, v in enumerate((a["hy_b1"][0], a["hy_b2"][0], a["hy_freq"][0, 0], a["hy_freq"][0, 1])):
                sp.dma_start(cols[:, i:i + 1], v.unsqueeze(1)).then_inc(w_in, 16)
            sp.dma_start(hy.w3, a["hy_w3"][0]).then_inc(tables_in, 16)
            sp.dma_start(hy.decay, a["t_decay"].rearrange("(t p) n -> p t n", p=128)).then_inc(tables_in, 16)
            sp.dma_start(hy.bias0, a["hy_bias"][0, 0].partition_broadcast(128)).then_inc(tables_in, 16)
            for s in range(2):
                sp.dma_start(hy.fwd[:, s], a["t_fwd"][s].rearrange("(t p) n -> p t n", p=128)).then_inc(tables_in, 16)
                sp.dma_start(hy.back[:, s], a["t_back"][s].rearrange("(t p) n -> p t n", p=128)).then_inc(tables_in, 16)
            sp.wait_ge(tables_in, 112)

        @block.tensor
        def _(pe):
            pe.wait_ge(w_in, 96)
            nc.tensor.matmul(c.ps[0:64, 0, :], w1, c.tab["feats"][0:33, :], start=True, stop=True).then_inc(product, 1)
            pe.wait_ge(sined, 1)
            nc.tensor.matmul(c.ps[0:64, 1, :], w2, hy.h1, start=True, stop=True).then_inc(product, 1)

        @block.vector
        def _(dve):
            v = nc.vector
            link = chain(dve, chained)
            for i, h in enumerate((hy.h1, hy.h2)):
                dve.wait_ge(product, i + 1)
                link(v.tensor_scalar(h, c.ps[0:64, i, :], cols[:, i:i + 1], cols[:, 2 + i:3 + i], ALU.add, ALU.mult))
                link(v.tensor_scalar(n_, h, 1 / (2 * math.pi), magic, ALU.mult, ALU.add))
                link(v.tensor_scalar(n_, n_, -magic, None, ALU.add))
                link(v.scalar_tensor_tensor(h, n_, -hi, h, ALU.mult, ALU.add))
                link(v.scalar_tensor_tensor(h, n_, -lo, h, ALU.mult, ALU.add))
                link(v.tensor_scalar(h, h, 3.1415925, -3.1415925, ALU.min, ALU.max))

        @block.scalar
        def _(act):
            for i, h in enumerate((hy.h1, hy.h2)):
                act.wait_ge(chained, 6 * (i + 1))
                nc.scalar.activation(h, h, ACT.Sin).then_inc(sined, 1)


def filter_lags(c, hy, order):
    nc = c.nc
    st, sem = stage(c)
    sq = hy.tmp
    with st, nc.Block() as block:
        product, decayed, squared, used, summed, act_chain, combined = \
            (sem(n) for n in ("product", "decayed", "squared", "used", "summed", "act_chain", "combined"))

        @block.tensor
        def _(pe):
            def square_sum(t):
                for side in range(2):
                    n = 2 * t + side
                    pe.wait_ge(squared, n + 1)
                    nc.tensor.matmul(c.ps[:, 7, :], c.tab["ones"], sq[:, n % 3, :], start=n == 0, stop=n == 7,
                                     ).then_inc(used, 1)

            for t in range(4):
                for side in range(2):
                    n = 2 * t + side
                    if n >= 6:
                        pe.wait_ge(decayed, n - 5)
                    col = (order * 2 + side) * 512
                    nc.tensor.matmul(c.ps[:, n % 6, :], hy.h2[:, t * 128:(t + 1) * 128], hy.w3[:, col:col + 512],
                                     start=True, stop=True).then_inc(product, 1)
                if t:
                    square_sum(t - 1)
            square_sum(3)

        @block.vector
        def _(dve):
            v = nc.vector
            for t in range(4):
                for side in range(2):
                    n = 2 * t + side
                    dve.wait_ge(product, n + 1)
                    dst = hy.lags[:, side, t, :]
                    if side and t == 0:
                        v.scalar_tensor_tensor(dst, c.ps[:, n % 6, :], c.tab["nonzero"], hy.decay[:, t, :],
                                               ALU.mult, ALU.mult).then_inc(decayed, 1)
                    else:
                        v.tensor_tensor(dst, c.ps[:, n % 6, :], hy.decay[:, t, :], ALU.mult).then_inc(decayed, 1)
                dve.wait_ge(squared, 2 * t + 2)
                v.tensor_tensor(hy.lags[:, 0, t, :], hy.lags[:, 0, t, :], hy.lags[:, 1, t, :], ALU.add)\
                    .then_inc(combined, 1)
                dve.wait_ge(combined, 2 * t + 1)
                v.scalar_tensor_tensor(hy.lags[:, 1, t, :], hy.lags[:, 1, t, :], -2.0, hy.lags[:, 0, t, :],
                                       ALU.mult, ALU.add).then_inc(combined, 1)

        @block.scalar
        def _(act):
            link = chain(act, act_chain)
            for n in range(8):
                act.wait_ge(decayed, n + 1)
                if n >= 3:
                    act.wait_ge(used, n - 2)
                nc.scalar.activation(sq[:, n % 3, :], hy.lags[:, n % 2, n // 2, :], ACT.Square).then_inc(squared, 1)
            act.wait_ge(used, 8)
            link(nc.scalar.activation(hy.root, c.ps[:, 7, :], ACT.Ln, bias=EPS))
            link(nc.scalar.activation(hy.root, hy.root, ACT.Exp, scale=-0.5))


def transform(c, src, hy, finish):
    nc = c.nc
    st, sem = stage(c)
    with st, nc.Block() as block:
        product, chained = sem("product"), sem("chained")

        @block.tensor
        def _(pe):
            for f in range(4):
                for s in range(2):
                    n = 2 * f + s
                    for t in range(4):
                        last = nc.tensor.matmul(c.ps[:, n, :], hy.fwd[:, s, t, f * 128:(f + 1) * 128], src(s)[:, t, :],
                                                start=t == 0, stop=t == 3)
                    last.then_inc(product, 1)

        @block.vector
        def _(dve):
            link = chain(dve, chained)
            for f in range(4):
                dve.wait_ge(product, 2 * f + 2)
                finish(link, f, c.ps[:, 2 * f, :], c.ps[:, 2 * f + 1, :])


def inverse(c, hy, by_token, finish):
    nc = c.nc
    st, sem = stage(c)
    with st, nc.Block() as block:
        product, chained = sem("product"), sem("chained")

        @block.tensor
        def _(pe):
            for i in range(4):
                for n in range(8):
                    s, f = n // 4, n % 4
                    table, spec = hy.back[:, s, f, :], hy.spec[:, s, f, :]
                    cut = slice(i * 128, (i + 1) * 128)
                    lhs, rhs = (table[:, cut], spec) if by_token else (spec[:, cut], table)
                    last = nc.tensor.matmul(c.ps[:, i, :], lhs, rhs, start=n == 0, stop=n == 7)
                last.then_inc(product, 1)

        @block.vector
        def _(dve):
            link = chain(dve, chained)
            for i in range(4):
                dve.wait_ge(product, i + 1)
                finish(link, i, c.ps[:, i, :])


def hyena(c):
    nc = c.nc
    v = nc.vector
    hy = Hyena(c)
    u = cd_buffers(c)[7]
    block_of = lambda buf, i, j: buf[:, i, j * 128:(j + 1) * 128]
    turn_tiles(c, [(hy.v[:, t, :], [block_of(u, k, t) for k in range(4)]) for t in range(4)]
               + [(hy.x1[:, t, :], [block_of(u, 4 + k, t) for k in range(4)]) for t in range(4)],
               [(hy.x2t[:, k, :], u[:, 8 + k, :]) for k in range(4)])
    filter_features(c, hy)
    root = hy.root

    def scaled(link, f, cos, sin):
        v.tensor_tensor(hy.kern[:, 0, f, :], cos, root, ALU.mult)
        v.tensor_tensor(hy.kern[:, 1, f, :], sin, root, ALU.mult)

    def complex_product(link, f, cos, sin):
        hc, hs, t0, t1, t2 = hy.kern[:, 0, f, :], hy.kern[:, 1, f, :], hy.tmp[:, 0, :], hy.tmp[:, 1, :], hy.tmp[:, 2, :]
        v.tensor_tensor(t0, cos, hc, ALU.mult)
        link(v.tensor_tensor(t1, sin, hs, ALU.mult))
        v.tensor_tensor(hy.spec[:, 0, f, :], t0, t1, ALU.subtract)
        link(v.tensor_tensor(t2, cos, hs, ALU.mult))
        link(v.tensor_tensor(t0, sin, hc, ALU.mult))
        link(v.tensor_tensor(hy.spec[:, 1, f, :], t2, t0, ALU.add))

    def gate_tokens(link, t, conv):
        z = hy.v[:, t, :]
        link(v.tensor_tensor(z, z, hy.bias0, ALU.mult))
        link(v.tensor_tensor(z, z, conv, ALU.add))
        link(v.tensor_tensor(z, z, hy.x1[:, t, :], ALU.mult))

    def gate_features(link, k, conv):
        t0 = hy.tmp[:, 0, :]
        link(v.scalar_tensor_tensor(t0, hy.z1t[:, k, :], hy_bias_col(c, k), conv, ALU.mult, ALU.add))
        link(v.tensor_tensor(hy.out[:, 4 + k, :], t0, hy.x2t[:, k, :], ALU.mult))

    for order in range(2):
        filter_lags(c, hy, order)
        transform(c, lambda s: hy.lags[:, s], hy, scaled)
        transform(c, lambda s: hy.v, hy, complex_product)
        if order == 0:
            inverse(c, hy, True, gate_tokens)
            turn_tiles(c, [(hy.z1t[:, k, :], [block_of(hy.v, t, k) for t in range(4)]) for k in range(4)])
        else:
            inverse(c, hy, False, gate_features)


def layer_cd(c):
    norm_to_features(c, 0, range(TT))
    out, q, k, _, v, _, _, u = cd_buffers(c)
    project_features(c, "swa_q", 4, q, "rope", z=0)
    project_features(c, "swa_k", 1, k, "rope", cols=128)
    project_tokens(c, "swa_v", ht_view(c), KT, 1, 128, range(TT), lambda t, j: v[:, t, :])
    project_features(c, "hy_in", 12, u, "conv", z=0, taps=lambda t, n: hy_tap(c, t, n))
    window_attention(c)
    hyena(c)
    project_tokens(c, "cd_out", out, KT, 1, 256, range(TX), lambda t, j: mixed_rows(c)[:, t, j * 256:(j + 1) * 256])
    add_branch(c, 0, range(TX))
    feed_forward(c, 1, 0, range(TX))


def store(c):
    with c.nc.Block() as block:
        @block.sync
        def _(sp):
            sp.dma_start(c.a["out"][0].rearrange("(t p) d -> p t d", p=128), c.x).then_inc(c.stored, 16)
            sp.wait_ge(c.stored, 16)


def build_program(nc, a):
    with ExitStack() as ctx:
        c = Core(nc, a, ctx)
        plan_all(c)
        load_inputs(c)
        modulation(c, 0)
        layer_ab(c)
        modulation(c, 1)
        layer_cd(c)
        store(c)


_INS = ("x", "c", "ctx", "c_ctx", "w_mod", "b_mod", "norm_g", "ffn_w_up", "ffn_conv", "ffn_w_down", "ab_w_in",
        "ab_w_out", "gdn_conv", "gdn_a_log", "gdn_dt_bias", "gdn_norm_g", "diff_lambda", "diff_norm_g", "cd_w_in",
        "cd_w_out", "swa_sink", "hy_conv", "hy_w1", "hy_b1", "hy_w2", "hy_b2", "hy_w3", "hy_freq", "hy_bias")


def kernel(**inputs):
    import concourse.bacc as bacc
    from concourse.bass_utils import run_bass_kernel_spmd

    nc = bacc.Bacc("TRN2", target_bir_lowering=False, num_devices=1)
    arrays = {f"in_{name}": np.ascontiguousarray(inputs[name]) for name in _INS}
    arrays["in_c_ctx"] = arrays["in_c_ctx"].reshape(1, D)
    arrays.update({f"in_{name}": table for name, table in constant_tables().items()})
    a = {name[3:]: nc.dram_tensor(name, v.shape, mybir.dt.from_np(v.dtype), kind="ExternalInput").ap()
         for name, v in arrays.items()}
    a["out"] = nc.dram_tensor("out", (1, N_X, D), F32, kind="ExternalOutput").ap()
    build_program(nc, a)
    r = run_bass_kernel_spmd(nc, [arrays], core_ids=[0])
    return r.results[0]["out"]
```

```python
import math
from contextlib import ExitStack

import numpy as np

import concourse.bass as bass
from concourse import mybir

F32 = mybir.dt.float32
ALU = mybir.AluOpType
ACT = mybir.ActivationFunctionType
AX = mybir.AxisListType

D = 1024
KT = D // 128
N_X, N_Z = 512, 256
N_ALL = N_X + N_Z
TX, TZ = N_X // 128, N_Z // 128
TT = TX + TZ
D_FF = 2816
FT = D_FF // 128
EPS = 1e-6
HEAD = 64
CHUNK = 64
GH = 8
PAIRS = GH // 2
GW = 512
CX, CZ = N_X // CHUNK, N_Z // CHUNK
STEPS = CX + CZ
NEG = -1e30
LAM_INIT = 0.2
N_FREQ = 512
RING = 4
SLOT = 2048
LEVELS = (1, 2, 4, 8, 16, 32)

_TABLE = {}
_at = 0
for _name, _n in (("ident", 128), ("rot", 128), ("heads", 128), ("ones", 128), ("cos", 512), ("sin", 512),
                  ("tri", 128), ("tri2", 256), ("mask_a", 128), ("mask_q", 128), ("m1", 128), ("mt", 768),
                  ("eye", 64), ("win_l", 128), ("win_r", 128), ("pick", 32), ("row_of", 256), ("nonzero", 1),
                  ("feats", 512)):
    _TABLE[_name] = (_at, _n)
    _at += _n
TABLE_COLS = _at


def constant_tables():
    f = np.float32
    t = np.zeros((128, TABLE_COLS), f)

    def put(name, a, rows=128):
        o, n = _TABLE[name]
        t[:rows, o:o + n] = np.asarray(a, f).reshape(rows, n)

    put("ident", np.eye(128))
    rot = np.zeros((128, 128))
    for d in range(128):
        if d % 32 < 16:
            rot[d + 16, d] = -1
        else:
            rot[d - 16, d] = 1
    put("rot", rot)
    put("heads", np.kron(np.eye(2), np.ones((64, 64))))
    put("ones", np.ones((128, 128)))
    inv = (f(10000.0) ** (-np.arange(0, 32, 2, dtype=f) / f(32))).astype(f)
    tok = np.arange(N_X)
    ang = np.zeros((128, N_X), f)
    for d in range(128):
        pos = (tok // 64 if d % 64 < 32 else tok % 64).astype(f)
        ang[d] = pos * inv[d % 16]
    put("cos", np.cos(ang))
    put("sin", np.sin(ang))
    i, j = np.arange(64)[:, None], np.arange(64)[None, :]
    both = lambda a: np.tile(a, (2, 1))
    two = lambda fwd, bwd: both(np.concatenate([fwd, bwd], axis=1))
    put("tri", two(i <= j, i >= j))
    put("tri2", np.concatenate([np.kron(np.eye(2), i <= j), np.kron(np.eye(2), i >= j)], axis=1))
    put("mask_a", two(np.where(i > j, 0, NEG), np.where(i < j, 0, NEG)))
    put("mask_q", two(np.where(i <= j, 0, NEG), np.where(i >= j, 0, NEG)))
    level = lambda b: (i // (2 * b) == j // (2 * b)) & ((i // b) % 2 == 1) & ((j // b) % 2 == 0)
    put("m1", two(level(1), level(1).T))
    put("mt", np.concatenate([two(level(b).T, level(b)) for b in LEVELS], axis=1))
    put("eye", both(np.eye(64)))
    q, m = np.arange(128)[:, None], np.arange(128)[None, :]
    put("win_l", np.where(m >= q, 0, NEG))
    put("win_r", np.where(m <= q, 0, NEG))
    pick = np.zeros((32, 2, 2, 2, PAIRS))
    for direction in range(2):
        for hh in range(2):
            for what in range(2):
                for p in range(PAIRS):
                    pick[what * 16 + direction * 8 + 2 * p + hh, direction, hh, what, p] = 1
    put("pick", pick, 32)
    row_of = np.zeros((4, 32, 2, 128))
    row_of[:, 0, 0] = row_of[:, 1, 1] = 1
    put("row_of", row_of)
    nz = np.ones(128)
    nz[0] = 0
    put("nonzero", nz)
    n = N_X
    pos = np.arange(n, dtype=f)
    tt = pos / f(n - 1)
    fa = (f(2.0 * math.pi) * pos / f(n))[:, None] * np.linspace(1e-4, 15, 16, dtype=f)[None, :]
    feats = np.concatenate([tt[:, None], np.cos(fa), -np.sin(fa)], axis=-1)
    put("feats", feats.T, 33)
    lo, hi = math.log(1e-2) / 1.5, math.log(1e-2) / 0.3
    decay = np.exp(-tt[:, None] * np.abs(np.linspace(lo, hi, 512, dtype=f))[None, :]).astype(f)
    w = 2 * np.pi * (np.arange(N_FREQ) + 0.5) / (2 * N_FREQ)
    ph = np.arange(n)[:, None] * w[None, :]
    fwd = np.stack([np.cos(ph), np.sin(ph)]).astype(f)
    back = (np.stack([np.cos(ph.T), np.sin(ph.T)]) / N_FREQ).astype(f)
    return {"t_table": t, "t_decay": decay, "t_fwd": fwd, "t_back": back}


class Core:

    def __init__(self, nc, a, ctx):
        self.nc, self.a, self.ctx = nc, a, ctx
        self.at = 0
        self.mem = ctx.enter_context(nc.sbuf_tensor("mem", [128, 53200], F32))
        self.ps = ctx.enter_context(nc.psum_tensor("banks", [128, 8, 512], F32))
        self.table, self.tab = self.room(TABLE_COLS), {}
        for name, (o, n) in _TABLE.items():
            self.tab[name] = self.table[:, o:o + n]
        self.x = self.room(TX * D).rearrange("p (t d) -> p t d", d=D)
        self.z = self.room(TZ * D).rearrange("p (t d) -> p t d", d=D)
        self.cols = self.room(512).rearrange("p (j c) -> p j c", j=4)
        self.sc = self.room(16).rearrange("p (k u) -> p k u", u=2)
        self.modc = self.room(64).rearrange("p (v k u) -> p v k u", v=4, u=2)
        self.coef = self.room(64).rearrange("p (m v u k) -> p m v u k", m=2, v=2, u=2)
        self.stat = self.room(256)
        self.gates = self.room(4 * D).rearrange("p (v u d) -> p v u d", v=2, u=2)
        self.ht = self.room(KT * N_ALL)
        self.ring = self.room(RING * SLOT)
        self.small = self.room(12 * 96 + 16)
        self.arena = self.mem[:, self.at:53200]
        self.arena_size = 53200 - self.at
        self.loads, self.range_of, self.issued = [], {}, 0
        self.slot_in = [ctx.enter_context(nc.semaphore(f"weights_in_{i}")) for i in range(RING)]
        self.tables_back = ctx.enter_context(nc.semaphore("tables_back"))
        self.stored = ctx.enter_context(nc.semaphore("stored"))
        self.stage_n, self.spent = 0, []

    def room(self, n):
        self.at += n
        return self.mem[:, self.at - n:self.at]

    def plan(self, name, views):
        self.range_of[name] = (len(self.loads), len(self.loads) + len(views))
        self.loads += views

    def slot(self, n, k, cols):
        o = (n % RING) * SLOT
        return self.ring[:, o:o + k * cols].rearrange("p (k n) -> p k n", k=k)

    def issue(self, sp, stage, freed, ahead=RING):
        lo, hi = self.range_of[stage]
        for n in range(self.issued, min(hi + ahead, len(self.loads))):
            if n - RING >= lo:
                sp.wait_ge(*freed(n - RING - lo))
            src = self.loads[n]
            sp.dma_start(self.slot(n, src.shape[1], src.shape[2]), src).then_inc(self.slot_in[n % RING], 16)
            self.issued = n + 1

    def prefetch(self, sp, stage):
        lo = self.range_of[stage][0]
        for n in range(lo, lo + RING):
            src = self.loads[n]
            sp.dma_start(self.slot(n, src.shape[1], src.shape[2]), src).then_inc(self.slot_in[n % RING], 16)
            self.issued = n + 1

    def arrived(self, pe, n):
        pe.wait_ge(self.slot_in[n % RING], 16 * (n // RING + 1))


def chain(eng, sem):
    count = [0]

    def link(ins):
        count[0] += 1
        ins.then_inc(sem, 1)
        eng.wait_ge(sem, count[0])
    return link


def stage(c):
    c.stage_n += 1
    n = c.stage_n
    if len(c.spent) > 100:
        c.nc.clear_and_free_semaphores(c.spent)
        c.nc.all_engine_barrier()
        c.spent = []

    def sem(name):
        c.spent.append(c.nc.alloc_semaphore(f"{name}_{n}"))
        return c.spent[-1]
    return ExitStack(), sem


def rows_of(ap):
    return ap.rearrange("(u c) -> u c", c=128)


def load_inputs(c):
    nc, a = c.nc, c.a
    st, sem = stage(c)
    rows = c.arena[:, 0:512].rearrange("p (j c) -> p j c", j=4)
    taps = [a["ffn_conv"][l].rearrange("t (u c) -> t u c", c=128) for l in range(2)]
    batches = [
        [a["norm_g"].rearrange("l g (k c) -> (l g k) c", c=128), rows_of(a["c"][0]), rows_of(a["c_ctx"][0]),
         a["gdn_conv"][0].rearrange("t (u c) -> (t u) c", c=128)],
        [taps[0][0], taps[0][1], a["hy_conv"][0].rearrange("t (u c) -> (t u) c", c=128)],
        [taps[0][2], taps[1][0], rows_of(a["hy_bias"][0, 1])],
        [taps[1][1], taps[1][2]],
    ]
    sizes = [sum(v.shape[0] for v in b) for b in batches]
    with st, nc.Block() as block:
        table_in, rows_in, x_in, z_in = sem("table_in"), sem("rows_in"), sem("x_in"), sem("z_in")
        turned, columns = sem("turned"), sem("columns")
        n_rows = sum(len(b) for b in batches)

        @block.sync
        def _(sp):
            sp.dma_start(c.table, a["t_table"]).then_inc(table_in, 16)
            for j, views in enumerate(batches):
                r = 0
                for v in views:
                    sp.dma_start(rows[r:r + v.shape[0], j, :], v).then_inc(rows_in, 16)
                    r += v.shape[0]
            c.issue(sp, "start", None)

        @block.scalar
        def _(act):
            act.dma_start(c.x, a["x"][0].rearrange("(t p) d -> p t d", p=128)).then_inc(x_in, 16)
            act.dma_start(c.z, a["ctx"][0].rearrange("(t p) d -> p t d", p=128)).then_inc(z_in, 16)
            act.wait_ge(columns, 4)
            nc.scalar.activation(c.sc.rearrange("p k u -> p u k"),
                                 c.cols[:, 0, 64:80].rearrange("p (u k) -> p u k", u=2), ACT.Silu)
            act.wait_ge(x_in, 16)
            act.wait_ge(z_in, 16)

        @block.tensor
        def _(pe):
            pe.wait_ge(table_in, 16)
            pe.wait_ge(rows_in, 16 * n_rows)
            for j, n in enumerate(sizes):
                last = nc.tensor.transpose(c.ps[:, j, 0:n], rows[0:n, j, :], c.tab["ident"][0:n, 0:n])
                last.then_inc(turned, 1)

        @block.vector
        def _(dve):
            for j, n in enumerate(sizes):
                dve.wait_ge(turned, j + 1)
                nc.vector.tensor_copy(c.cols[:, j, 0:n], c.ps[:, j, 0:n]).then_inc(columns, 1)


def norm_col(c, l, g):
    o = (l * 4 + g) * 8
    return c.cols[:, 0, o:o + 8]


def gdn_tap(c, t, tile):
    return c.cols[:, 0, 80 + 12 * t + tile:81 + 12 * t + tile]


def hy_tap(c, t, tile):
    return c.cols[:, 1, 88 + 12 * t + tile:89 + 12 * t + tile]


def hy_bias_col(c, tile):
    return c.cols[:, 2, 88 + tile:89 + tile]


def ffn_tap(c, l, t, tile):
    j, o = {(0, 0): (1, 0), (0, 1): (1, 44), (0, 2): (2, 0), (1, 0): (2, 44), (1, 1): (3, 0), (1, 2): (3, 44)}[l, t]
    return c.cols[:, j, o + tile:o + tile + 1]


class Modulation:

    LOADS = 6 * 4

    def __init__(self, c, l):
        self.c, self.l = c, l
        o = c.arena_size - 3072
        self.mod, self.bias = c.arena[:, o:o + 1536], c.arena[:, o + 1536:o + 3072]
        self.gain = c.small[:, 0:512]
        self.weights = c.arena[:, o - 2048:o].rearrange("p (k n) -> p k n", k=2)

    def load_rows(self, eng, rows_in):
        a, l = self.c.a, self.l
        for g in range(4):
            for r in range(2):
                p = slice(32 * g + r, 32 * g + r + 1)
                eng.dma_start(self.bias[p, :].rearrange("p (i n) -> p i n", i=6),
                              a["b_mod"][l:l + 1, :].rearrange("a (i g n) -> a i g n", i=6, g=4)[:, :, g, :])\
                    .then_inc(rows_in, 16)
                for w in range(2):
                    eng.dma_start(self.gain[p, 256 * w:256 * w + 256],
                                  a["norm_g"][l, 1 + 2 * w:2 + 2 * w, 256 * g:256 * g + 256]).then_inc(rows_in, 16)

    ROWS_IN = 16 * 24

    def product(self, n, w, bank):
        c = self.c
        for kk in range(2):
            k = 2 * (n % 4) + kk
            for g in range(4):
                last = c.nc.tensor.matmul(c.ps[32 * g:32 * g + 2, bank, 0:256], c.sc[:, k, :],
                                          w[:, kk, 256 * g:256 * g + 256], start=k == 0, stop=k == KT - 1)
        return last

    def drain(self, i, bank):
        c = self.c
        for g in range(4):
            p = slice(32 * g, 32 * g + 2)
            last = c.nc.vector.tensor_tensor(self.mod[p, 256 * i:256 * i + 256], c.ps[p, bank, 0:256],
                                             self.bias[p, 256 * i:256 * i + 256], ALU.add)
        return last


def modulation(c, l):
    st, sem = stage(c)
    m = Modulation(c, l)
    name = f"mod{l}"
    lo, _ = c.range_of[name]
    with st, c.nc.Block() as block:
        rows_in, product, drained = sem("rows_in"), sem("product"), sem("drained")

        @block.sync
        def _(sp):
            c.issue(sp, name, lambda j: (product, j + 1))

        @block.scalar
        def _(act):
            m.load_rows(act, rows_in)

        @block.tensor
        def _(pe):
            for n in range(m.LOADS):
                if n % 4 == 0 and n >= 8:
                    pe.wait_ge(drained, n // 4 - 1)
                c.arrived(pe, lo + n)
                m.product(n, c.slot(lo + n, 2, D), n // 4 % 2).then_inc(product, 1)

        @block.vector
        def _(dve):
            dve.wait_ge(rows_in, m.ROWS_IN)
            for i in range(6):
                dve.wait_ge(product, 4 * (i + 1))
                m.drain(i, i % 2).then_inc(drained, 1)


def spread_modulation(c, l):
    nc = c.nc
    st, sem = stage(c)
    m = Modulation(c, l)
    mod, gain = m.mod, m.gain
    columns_of = (0, 1, 3, 4)
    with st, nc.Block() as block:
        gate_rows, turned, columns = sem("gate_rows"), sem("turned"), sem("columns")
        gate, spread = sem("gate"), sem("spread")

        @block.tensor
        def _(pe):
            for w, i in enumerate(columns_of):
                for k in range(KT):
                    g, kk = k // 2, k % 2
                    p = slice(32 * g, 32 * g + 2)
                    last = nc.tensor.matmul(c.ps[:, 4 + g, 4 * w + 2 * kk:4 * w + 2 * kk + 2],
                                            mod[p, 256 * i + 128 * kk:256 * i + 128 * kk + 128],
                                            c.tab["ident"][p, p], start=True, stop=True)
            last.then_inc(turned, 1)
            pe.wait_ge(gate_rows, 8)
            for n in range(4):
                w, r = n // 2, n % 2
                if n == 1:
                    pe.wait_ge(columns, 4)
                elif n >= 2:
                    pe.wait_ge(spread, 4 * (n - 1))
                for g in range(4):
                    p = slice(32 * g, 32 * g + 2)
                    last = nc.tensor.matmul(c.ps[:, 4 * (n % 2) + g, 0:256], c.tab["row_of"][p, r * 128:(r + 1) * 128],
                                            mod[p, 256 * (2, 5)[w]:256 * (2, 5)[w] + 256], start=True, stop=True)
                last.then_inc(gate, 1)

        @block.vector
        def _(dve):
            for w, i in enumerate((2, 5)):
                for g in range(4):
                    p = slice(32 * g, 32 * g + 2)
                    nc.vector.tensor_tensor(mod[p, 256 * i:256 * i + 256], mod[p, 256 * i:256 * i + 256],
                                            gain[p, 256 * w:256 * w + 256], ALU.mult).then_inc(gate_rows, 1)
            dve.wait_ge(turned, 1)
            for g in range(4):
                nc.vector.tensor_copy(c.modc[:, :, 2 * g:2 * g + 2, :],
                                      c.ps[:, 4 + g, 0:16].rearrange("p (v k u) -> p v k u", v=4, k=2)).then_inc(columns, 1)
            dve.wait_ge(columns, 4)
            for m_ in range(2):
                for r in range(2):
                    nc.vector.scalar_tensor_tensor(c.coef[:, m_, 0, r, :], c.modc[:, 2 * m_ + 1, :, r], 1.0,
                                                   norm_col(c, l, 2 * m_), ALU.add, ALU.mult)
                    nc.vector.tensor_copy(c.coef[:, m_, 1, r, :], c.modc[:, 2 * m_, :, r])
            for n in range(4):
                w, r = n // 2, n % 2
                dve.wait_ge(gate, n + 1)
                for g in range(4):
                    nc.vector.tensor_copy(c.gates[:, w, r, 256 * g:256 * g + 256],
                                          c.ps[:, 4 * (n % 2) + g, 0:256]).then_inc(spread, 1)


def ht_view(c):
    return c.ht.rearrange("p (k t) -> p k t", k=KT)


def token_tile(c, t):
    return c.x[:, t, :] if t < TX else c.z[:, t - TX, :]


def norm_to_features(c, m, tiles):
    nc = c.nc
    st, sem = stage(c)
    junk = c.arena[:, 0:D]
    y = c.arena[:, D:3 * D].rearrange("p (b d) -> p b d", b=2)
    rstd = c.stat[:, 0:TT]
    ht = ht_view(c)
    with st, nc.Block() as block:
        act_chain, stats, scaled = sem("act_chain"), sem("stats"), sem("scaled")
        turned, act_out, dve_out = sem("turned"), sem("act_out"), sem("dve_out")

        @block.scalar
        def _(act):
            link = chain(act, act_chain)
            for t in tiles:
                link(nc.scalar.activation(junk, token_tile(c, t), ACT.Square, accum_out=rstd[:, t:t + 1]))
            n = len(tiles)
            link(nc.scalar.activation(rstd[:, 0:n], rstd[:, 0:n], ACT.Ln, bias=EPS, scale=1.0 / D))
            nc.scalar.activation(rstd[:, 0:n], rstd[:, 0:n], ACT.Exp, scale=-0.5).then_inc(stats, 1)
            for t in tiles:
                act.wait_ge(turned, 2 * t + 1)
                r = int(t >= TX)
                for k in range(4):
                    nc.scalar.activation(ht[:, k, t * 128:(t + 1) * 128], c.ps[:, (t % 4) * 2, k * 128:(k + 1) * 128],
                                         ACT.Identity, scale=c.coef[:, m, 0, r, k:k + 1],
                                         bias=c.coef[:, m, 1, r, k:k + 1]).then_inc(act_out, 1)

        @block.vector
        def _(dve):
            dve.wait_ge(stats, 1)
            for i in range(len(tiles) + 1):
                if i < len(tiles):
                    if i >= 2:
                        dve.wait_ge(turned, 2 * (i - 1))
                    nc.vector.tensor_scalar(y[:, i % 2, :], token_tile(c, tiles[i]), rstd[:, i:i + 1], None,
                                            ALU.mult).then_inc(scaled, 1)
                if i:
                    t = tiles[i - 1]
                    r = int(t >= TX)
                    dve.wait_ge(turned, 2 * i)
                    for k in range(4, KT):
                        nc.vector.tensor_scalar(ht[:, k, t * 128:(t + 1) * 128],
                                                c.ps[:, (t % 4) * 2 + 1, (k - 4) * 128:(k - 3) * 128],
                                                c.coef[:, m, 0, r, k:k + 1], c.coef[:, m, 1, r, k:k + 1],
                                                ALU.mult, ALU.add).then_inc(dve_out, 1)

        @block.tensor
        def _(pe):
            for t in tiles:
                if t >= 4:
                    pe.wait_ge(act_out, 4 * (t - 3))
                    pe.wait_ge(dve_out, 4 * (t - 3))
                pe.wait_ge(scaled, t + 1)
                for k in range(KT):
                    last = nc.tensor.transpose(c.ps[:, (t % 4) * 2 + k // 4, (k % 4) * 128:(k % 4 + 1) * 128],
                                               y[:, t % 2, k * 128:(k + 1) * 128], c.tab["ident"])
                    if k % 4 == 3:
                        last.then_inc(turned, 1)


def plan_all(c):
    a = c.a
    ktiles = lambda w: w.rearrange("(k p) n -> p k n", p=128)
    chunks = lambda w, n=256: [ktiles(w)[:, :, i:i + n] for i in range(0, w.shape[1], n)]
    down = lambda w: [ktiles(w)[:, h * 11:(h + 1) * 11, i:i + 128] for i in range(0, D, 128) for h in range(2)]

    def up(w):
        both = chunks(w)
        return [both[i] for j in range(11) for i in (j, 11 + j)]

    mods = lambda w: [ktiles(w)[:, k:k + 2, i * D:(i + 1) * D] for i in range(6) for k in range(0, KT, 2)]
    c.range_of["start"] = (0, 0)
    ab, cd = a["ab_w_in"][0], a["cd_w_in"][0]
    c.plan("mod0", mods(a["w_mod"][0]))
    c.plan("diff_qk", chunks(ab[:, 2080:3104]))
    c.plan("diff_v", chunks(ab[:, 3104:3616]))
    c.plan("gdn_gates", chunks(ab[:, 2048:2080], 32))
    c.plan("gdn_gate", chunks(ab[:, 1536:2048]))
    c.plan("gdn_qkv", chunks(ab[:, 0:1536]))
    c.plan("ab_out", chunks(a["ab_w_out"][0]))
    c.plan("up0", up(a["ffn_w_up"][0]))
    c.plan("down0", down(a["ffn_w_down"][0]))
    c.plan("swa_q", chunks(cd[:, 0:512]))
    c.plan("swa_k", chunks(cd[:, 512:640], 128))
    c.plan("swa_v", chunks(cd[:, 640:768], 128))
    c.plan("hy_in", chunks(cd[:, 768:2304]))
    c.plan("cd_out", chunks(a["cd_w_out"][0]))
    c.plan("up1", up(a["ffn_w_up"][1]))
    c.plan("down1", down(a["ffn_w_down"][1]))


def project_features(c, name, n_tiles, dst, kind, z=N_Z, taps=None, cols=256, ahead=RING):
    nc = c.nc
    st, sem = stage(c)
    lo, _ = c.range_of[name]
    ht = ht_view(c)
    per = cols // 128
    slots = 3
    work = c.arena[:, c.arena_size - 3072:].rearrange("p (n b t) -> p n b t", n=3, b=2)
    raw, turned_cos, turned_sin = work[:, 0], work[:, 1], work[:, 2]
    conv = kind.startswith("conv")
    per_tile = 2 if z else 1
    with st, nc.Block() as block:
        product, drained, done, last_out = sem("product"), sem("drained"), sem("done"), sem("last_out")
        rotated, dve_chain = sem("rotated"), sem("dve_chain")

        @block.sync
        def _(sp):
            c.issue(sp, name, lambda j: (product, per * (j + 1)), ahead)

        @block.tensor
        def _(pe):
            def rotate(n):
                pe.wait_ge(drained, per_tile * n + 1)
                if n >= 2:
                    pe.wait_ge(done, n - 1)
                nc.tensor.matmul(c.ps[:, 6 + n % 2, :], c.tab["rot"], raw[:, n % 2, :],
                                 start=True, stop=True).then_inc(rotated, 1)

            for n in range(n_tiles):
                if n >= slots:
                    pe.wait_ge(drained, per_tile * (n - slots + 1))
                    if conv:
                        pe.wait_ge(done, n - slots + 1)
                if n % per == 0:
                    c.arrived(pe, lo + n // per)
                w = c.slot(lo + n // per, KT, cols)[:, :, n % per * 128:n % per * 128 + 128]
                for k in range(KT):
                    last = nc.tensor.matmul(c.ps[:, 2 * (n % slots), :], w[:, k, :], ht[:, k, 0:N_X],
                                            start=k == 0, stop=k == KT - 1)
                    if z:
                        last = nc.tensor.matmul(c.ps[:, 2 * (n % slots) + 1, 0:z], w[:, k, :],
                                                ht[:, k, N_X:N_X + z], start=k == 0, stop=k == KT - 1)
                last.then_inc(product, 1)
                if kind == "rope" and n:
                    rotate(n - 1)
            if kind == "rope":
                rotate(n_tiles - 1)

        @block.scalar
        def _(act):
            def finish(n):
                act.wait_ge(done, n + 1)
                nc.scalar.activation(dst[:, n, :], dst[:, n, :], ACT.Silu).then_inc(last_out, 1)

            for n in range(n_tiles):
                act.wait_ge(product, n + 1)
                px, pz = c.ps[:, 2 * (n % slots), :], c.ps[:, 2 * (n % slots) + 1, 0:z]
                if kind == "rope":
                    if n >= 2:
                        act.wait_ge(done, n - 1)
                    nc.scalar.activation(raw[:, n % 2, :], px, ACT.Copy).then_inc(drained, 1)
                elif conv:
                    nc.scalar.activation(dst[:, n, 0:N_X], px, ACT.Identity, scale=taps(1, n)).then_inc(drained, 1)
                else:
                    nc.scalar.activation(dst[:, n, 0:N_X], px, ACT.Silu if kind == "silu" else ACT.Copy)\
                        .then_inc(drained, 1)
                if z:
                    if conv:
                        nc.scalar.activation(dst[:, n, N_X:N_X + z], pz, ACT.Identity,
                                             scale=taps(1, n)).then_inc(drained, 1)
                    else:
                        nc.scalar.activation(dst[:, n, N_X:N_X + z], pz, ACT.Silu if kind == "silu" else ACT.Copy)\
                            .then_inc(drained, 1)
                if kind == "conv_silu" and n:
                    finish(n - 1)
            if kind == "conv_silu":
                finish(n_tiles - 1)

        @block.vector
        def _(dve):
            link = chain(dve, dve_chain)
            for n in range(n_tiles):
                if kind == "rope":
                    dve.wait_ge(drained, per_tile * n + 1)
                    nc.vector.tensor_tensor(turned_cos[:, n % 2, :], raw[:, n % 2, :], c.tab["cos"], ALU.mult)
                    dve.wait_ge(rotated, n + 1)
                    link(nc.vector.tensor_tensor(turned_sin[:, n % 2, :], c.ps[:, 6 + n % 2, :], c.tab["sin"], ALU.mult))
                    nc.vector.tensor_tensor(dst[:, n, 0:N_X], turned_cos[:, n % 2, :], turned_sin[:, n % 2, :],
                                            ALU.add).then_inc(done, 1)
                elif conv:
                    dve.wait_ge(drained, per_tile * (n + 1))
                    convolve(c, link, dst[:, n, :], c.ps[:, 2 * (n % slots), :], c.ps[:, 2 * (n % slots) + 1, :], z,
                             lambda t: taps(t, n)).then_inc(done, 1)


def convolve(c, link, y, px, pz, z, tap):
    v = c.nc.vector
    parts = [(y[:, 0:N_X], px, N_X)] + ([(y[:, N_X:N_X + z], pz, z)] if z else [])
    for out, src, n in parts:
        step = v.scalar_tensor_tensor(out[:, 1:n], src[:, 0:n - 1], tap(0), out[:, 1:n], ALU.mult, ALU.add)
        if n == parts[-1][2]:
            link(step)
    for out, src, n in parts:
        step = v.scalar_tensor_tensor(out[:, 0:n - 1], src[:, 1:n], tap(2), out[:, 0:n - 1], ALU.mult, ALU.add)
    return step


def project_tokens(c, name, src, k_tiles, loads_per, cols, tiles, dst, mod_layer=None):
    nc = c.nc
    st, sem = stage(c)
    lo, hi = c.range_of[name]
    n_chunks = (hi - lo) // loads_per
    k_per = k_tiles // loads_per
    side = mod_layer is not None
    n_banks = 6 if side else 8
    units = [(j, t) for j in range(n_chunks) for t in tiles]
    m = Modulation(c, mod_layer)
    assert not side or m.LOADS == len(units) // 2
    with st, nc.Block() as block:
        product, act_out, dve_out = sem("product"), sem("act_out"), sem("dve_out")
        mod_in, mod_used, mod_drained, rows_in = sem("mod_in"), sem("mod_used"), sem("mod_drained"), sem("rows_in")

        @block.sync
        def _(sp):
            c.issue(sp, name, lambda j: (product, len(tiles) * (j // loads_per + 1)))

        if side:
            @block.gpsimd
            def _(pool):
                weights = c.a["w_mod"][mod_layer].rearrange("(k p) n -> p k n", p=128)
                for q in range(m.LOADS):
                    if q:
                        pool.wait_ge(mod_used, q)
                    k, i = 2 * (q % 4), q // 4
                    pool.dma_start(m.weights, weights[:, k:k + 2, i * D:(i + 1) * D]).then_inc(mod_in, 16)

        @block.tensor
        def _(pe):
            for n, (j, t) in enumerate(units):
                if n >= n_banks:
                    pe.wait_ge(dve_out if n % 2 else act_out, (n - n_banks) // 2 + 1)
                if t == tiles[0]:
                    for i in range(loads_per):
                        c.arrived(pe, lo + j * loads_per + i)
                for k in range(k_tiles):
                    w = c.slot(lo + j * loads_per + k // k_per, k_per, cols)[:, k % k_per, :]
                    last = nc.tensor.matmul(c.ps[:, n % n_banks, 0:cols], src[:, k, t * 128:(t + 1) * 128], w,
                                            start=k == 0, stop=k == k_tiles - 1)
                last.then_inc(product, 1)
                if side and n % 2:
                    q = n // 2
                    if q % 4 == 0 and q >= 8:
                        pe.wait_ge(mod_drained, q // 4 - 1)
                    pe.wait_ge(mod_in, 16 * (q + 1))
                    m.product(q, m.weights, 6 + q // 4 % 2).then_inc(mod_used, 1)

        @block.scalar
        def _(act):
            if side:
                m.load_rows(act, rows_in)
            for n, (j, t) in enumerate(units):
                if n % 2 == 0:
                    act.wait_ge(product, n + 1)
                    nc.scalar.activation(dst(t, j), c.ps[:, n % n_banks, 0:cols], ACT.Copy).then_inc(act_out, 1)

        @block.vector
        def _(dve):
            for n, (j, t) in enumerate(units):
                if n % 2 == 1:
                    dve.wait_ge(product, n + 1)
                    nc.vector.tensor_copy(dst(t, j), c.ps[:, n % n_banks, 0:cols]).then_inc(dve_out, 1)
                if side and n % 8 == 7:
                    part = n // 8
                    if part == 0:
                        dve.wait_ge(rows_in, m.ROWS_IN)
                    dve.wait_ge(mod_used, 4 * (part + 1))
                    m.drain(part, 6 + part % 2).then_inc(mod_drained, 1)


def outc(c):
    return c.arena[:, 0:KT * N_ALL].rearrange("p (k t) -> p k t", k=KT)


def diff_buffers(c):
    o = KT * N_ALL
    qk = c.arena[:, o:o + 8 * N_ALL].rearrange("p (k t) -> p k t", k=8)
    v = c.arena[:, o + 8 * N_ALL:o + 8 * N_ALL + TT * 512].rearrange("p (t e) -> p t e", t=TT)
    return qk, v, o + 8 * N_ALL + TT * 512


def lambda_value(c):
    nc, a = c.nc, c.a
    st, sem = stage(c)
    lam = c.small[:, 0:256].rearrange("p (u d) -> p u d", u=4)
    prod = c.small[:, 256:384].rearrange("p (u d) -> p u d", u=2)
    dots = c.stat[:, 200:202]
    with st, nc.Block() as block:
        rows_in, multiplied, summed, exps, link_sem = (sem(n) for n in ("rows_in", "multiplied", "summed", "exps", "link"))

        @block.sync
        def _(sp):
            sp.dma_start(lam, a["diff_lambda"][0].partition_broadcast(128)).then_inc(rows_in, 16)
            sp.dma_start(c.stat[:, 204:205], a["diff_norm_g"][0].unsqueeze(1)).then_inc(rows_in, 16)

        @block.vector
        def _(dve):
            link = chain(dve, link_sem)
            dve.wait_ge(rows_in, 32)
            link(nc.vector.tensor_tensor(prod, lam[:, 0:4:2, :], lam[:, 1:4:2, :], ALU.mult))
            nc.vector.tensor_reduce(dots, prod, AX.X, ALU.add).then_inc(summed, 1)
            dve.wait_ge(exps, 1)
            link(nc.vector.tensor_tensor(c.stat[:, 203:204], dots[:, 1:2], dots[:, 0:1], ALU.subtract))
            link(nc.vector.tensor_scalar(c.stat[:, 203:204], c.stat[:, 203:204], -LAM_INIT, None, ALU.add))
            link(nc.vector.tensor_scalar(c.stat[:, 204:205], c.stat[:, 204:205], 1.0 - LAM_INIT, None, ALU.mult))

        @block.scalar
        def _(act):
            act.wait_ge(summed, 1)
            nc.scalar.activation(dots, dots, ACT.Exp).then_inc(exps, 1)


def diff_attention(c):
    nc = c.nc
    st, sem = stage(c)
    qk, v, o = diff_buffers(c)
    out = outc(c)
    prob = c.arena[:, o:o + 4 * N_ALL].rearrange("p (b s m) -> p b s m", b=2, s=2)
    o += 4 * N_ALL
    turned = c.arena[:, o:o + 2 * N_ALL].rearrange("p (b m) -> p b m", b=2)
    o += 2 * N_ALL
    mixed = c.arena[:, o:o + 256].rearrange("p (b e) -> p b e", b=2)
    top, neg, total, sq = (c.stat[:, i * 4:i * 4 + 4].rearrange("p (b s) -> p b s", b=2) for i in range(4))
    rstd = c.stat[:, 16:18]
    junk = c.small[:, 0:128]
    units = [(q, h, 0) for h in range(4) for q in range(TX)] + [(q, h, N_X) for h in range(4) for q in (TX, TX + 1)]
    n_units = len(units)
    scale = HEAD ** -0.5
    flat = c.ps.rearrange("p b n -> p (b n)")
    score = lambda s: flat[:, s * 1024:s * 1024 + N_ALL]
    turn = flat[:, 2048:2048 + N_ALL]
    with st, nc.Block() as block:
        scored, maxed, exped, weighed = sem("scored"), sem("maxed"), sem("exped"), sem("weighed")
        turned_ps, turned_sb, valued, stats = sem("turned_ps"), sem("turned_sb"), sem("valued"), sem("stats")
        normed, back, written = sem("normed"), sem("back"), sem("written")
        dve_chain, act_chain = sem("dve_chain"), sem("act_chain")

        def keys(u):
            return range(units[u][2] // 128, TT)

        @block.tensor
        def _(pe):
            for i in range(n_units + 3):
                if i < n_units:
                    q, h, first = units[i]
                    for s in range(2):
                        if i:
                            pe.wait_ge(exped, 2 * (i - 1) + s + 1)
                        r = slice(64 * s, 64 * s + 64)
                        lhs = qk[r, h, q * 128:(q + 1) * 128]
                        if not first:
                            nc.tensor.matmul(score(s)[:, 0:N_X], lhs, qk[r, 4 + h, 0:N_X], start=True, stop=True)
                        nc.tensor.matmul(score(s)[:, N_X:N_ALL], lhs, qk[r, 4 + h, N_X:N_ALL],
                                         start=True, stop=True).then_inc(scored, 1)
                if 0 <= i - 1 < n_units:
                    u = i - 1
                    pe.wait_ge(weighed, u + 1)
                    if u:
                        pe.wait_ge(turned_sb, u)
                    for m in keys(u):
                        last = nc.tensor.transpose(turn[:, m * 128:(m + 1) * 128],
                                                   prob[:, u % 2, 0, m * 128:(m + 1) * 128], c.tab["ident"])
                    last.then_inc(turned_ps, 1)
                if 0 <= i - 2 < n_units:
                    u = i - 2
                    pe.wait_ge(turned_sb, u + 1)
                    if u:
                        pe.wait_ge(normed, u)
                    h = units[u][1]
                    for m in keys(u):
                        last = nc.tensor.matmul(c.ps[:, 6, 0:128], turned[:, u % 2, m * 128:(m + 1) * 128],
                                                v[:, m, h * 128:(h + 1) * 128], start=m == keys(u)[0], stop=m == TT - 1)
                    last.then_inc(valued, 1)
                if 0 <= i - 3 < n_units:
                    u = i - 3
                    pe.wait_ge(normed, u + 1)
                    if u:
                        pe.wait_ge(written, u)
                    nc.tensor.transpose(c.ps[:, 7, 0:128], mixed[:, u % 2, :], c.tab["ident"]).then_inc(back, 1)

        @block.scalar
        def _(act):
            link = chain(act, act_chain)
            for i in range(n_units + 2):
                if i < n_units:
                    first = units[i][2]
                    for s in range(2):
                        act.wait_ge(maxed, 2 * i + s + 1)
                        if i >= 2:
                            act.wait_ge(turned_ps, i - 1)
                        nc.scalar.activation(prob[:, i % 2, s, first:N_ALL], score(s)[:, first:N_ALL], ACT.Exp,
                                             bias=neg[:, i % 2, s:s + 1], scale=scale,
                                             accum_out=total[:, i % 2, s:s + 1]).then_inc(exped, 1)
                if 0 <= i - 1 < n_units:
                    u = i - 1
                    act.wait_ge(turned_ps, u + 1)
                    if u >= 2:
                        act.wait_ge(valued, u - 1)
                    first = units[u][2]
                    nc.scalar.activation(turned[:, u % 2, first:N_ALL], turn[:, first:N_ALL],
                                         ACT.Copy).then_inc(turned_sb, 1)
                if 0 <= i - 2 < n_units:
                    u = i - 2
                    act.wait_ge(valued, u + 1)
                    if u >= 2:
                        act.wait_ge(normed, u - 1)
                    link(nc.scalar.activation(junk, c.ps[:, 6, 0:128], ACT.Square, accum_out=rstd[:, u % 2:u % 2 + 1]))
                    link(nc.scalar.activation(rstd[:, u % 2:u % 2 + 1], rstd[:, u % 2:u % 2 + 1], ACT.Ln,
                                              bias=EPS, scale=1.0 / 128))
                    nc.scalar.activation(rstd[:, u % 2:u % 2 + 1], rstd[:, u % 2:u % 2 + 1], ACT.Exp,
                                         scale=-0.5).then_inc(stats, 1)

        @block.vector
        def _(dve):
            link = chain(dve, dve_chain)
            for i in range(n_units + 3):
                if i < n_units:
                    first = units[i][2]
                    for s in range(2):
                        dve.wait_ge(scored, 2 * i + s + 1)
                        link(nc.vector.reduce_max(top[:, i % 2, s:s + 1], score(s)[:, first:N_ALL], AX.X))
                        nc.vector.tensor_scalar(neg[:, i % 2, s:s + 1], top[:, i % 2, s:s + 1], -scale, None,
                                                ALU.mult).then_inc(maxed, 1)
                if 0 <= i - 1 < n_units:
                    u = i - 1
                    first = units[u][2]
                    b = u % 2
                    dve.wait_ge(exped, 2 * u + 2)
                    link(nc.vector.reciprocal(total[:, b, :], total[:, b, :]))
                    link(nc.vector.tensor_tensor(sq[:, b, 1:2], total[:, b, 1:2], c.stat[:, 203:204], ALU.mult))
                    link(nc.vector.tensor_scalar(prob[:, b, 1, first:N_ALL], prob[:, b, 1, first:N_ALL],
                                                 sq[:, b, 1:2], None, ALU.mult))
                    nc.vector.scalar_tensor_tensor(prob[:, b, 0, first:N_ALL], prob[:, b, 0, first:N_ALL],
                                                   total[:, b, 0:1], prob[:, b, 1, first:N_ALL],
                                                   ALU.mult, ALU.add).then_inc(weighed, 1)
                if 0 <= i - 2 < n_units:
                    u = i - 2
                    dve.wait_ge(stats, u + 1)
                    if u >= 2:
                        dve.wait_ge(back, u - 1)
                    nc.vector.tensor_scalar(mixed[:, u % 2, :], c.ps[:, 6, 0:128], rstd[:, u % 2:u % 2 + 1], None,
                                            ALU.mult).then_inc(normed, 1)
                if 0 <= i - 3 < n_units:
                    u = i - 3
                    q, h, _ = units[u]
                    dve.wait_ge(back, u + 1)
                    nc.vector.tensor_scalar(out[:, 4 + h, q * 128:(q + 1) * 128], c.ps[:, 7, 0:128],
                                            c.stat[:, 204:205], None, ALU.mult).then_inc(written, 1)


def gdn_buffers(c):
    o = KT * N_ALL
    qkv = c.arena[:, o:o + 12 * N_ALL].rearrange("p (k t) -> p k t", k=12)
    gate = c.arena[:, o + 12 * N_ALL:o + 16 * N_ALL].rearrange("p (k t) -> p k t", k=4)
    return qkv, gate, o + 16 * N_ALL


SMALL = ("g", "beta", "gc", "exp_gc", "exp_tail", "exp_last", "beta_exp_gc", "work")


def small(c, name):
    i = SMALL.index(name)
    return c.small[:, 96 * i:96 * i + 96]


def chunk_of(step, direction):
    if step < CZ:
        return N_X + CHUNK * (step if direction == 0 else CZ - 1 - step)
    return CHUNK * (step - CZ if direction == 0 else CX - 1 - (step - CZ))


def gdn_gates(c):
    nc, a = c.nc, c.a
    st, sem = stage(c)
    lo, _ = c.range_of["gdn_gates"]
    ht = ht_view(c)
    ba = gdn_buffers(c)[1][0:32, 0, :]
    raw = c.arena[:, c.arena_size - 192:].rearrange("p (s v) -> p s v", v=8)
    va = c.arena[:, c.arena_size - 400:c.arena_size - 384]
    rates = va[:, 0:16].rearrange("p (v s) -> p v s", v=2)
    by_head = c.arena[:, c.arena_size - 384:c.arena_size - 352].rearrange("p (i s) -> p i s", i=2)
    s24 = lambda n: small(c, n).rearrange("p (s v) -> p s v", v=4)
    by_dir = lambda ap, d: ap.rearrange("p (s u v) -> p s u v", u=2, v=4)[:, :, d, :]
    with st, nc.Block() as block:
        consts_in, product, drained, picked, summed = (sem(n) for n in ("consts_in", "product", "drained", "picked", "summed"))
        act_step, dve_step, rates_in = sem("act_step"), sem("dve_step"), sem("rates_in")

        @block.sync
        def _(sp):
            for i, name in enumerate(("gdn_a_log", "gdn_dt_bias")):
                sp.dma_start(by_head[:, i, :], a[name][0].rearrange("u h -> (u h)").partition_broadcast(128))\
                    .then_inc(consts_in, 16)
            c.issue(sp, "gdn_gates", lambda j: (product, 1))

        @block.tensor
        def _(pe):
            c.arrived(pe, lo)
            w = c.slot(lo, KT, 32)
            for x, n, bank in ((0, N_X, 0), (N_X, N_Z, 1)):
                for k in range(KT):
                    last = nc.tensor.matmul(c.ps[0:32, bank, 0:n], w[:, k, :], ht[:, k, x:x + n],
                                            start=k == 0, stop=k == KT - 1)
            last.then_inc(product, 1)
            pe.wait_ge(drained, 1)
            pick = c.tab["pick"][0:32, :].rearrange("p (u h v) -> p u h v", u=2, h=2)
            for s in range(STEPS):
                for r in range(2):
                    t0 = chunk_of(s, r)
                    for hh in range(2):
                        last = nc.tensor.matmul(c.ps[64 * hh:64 * hh + 64, 2, (2 * s + r) * 8:(2 * s + r) * 8 + 8],
                                                ba[:, t0:t0 + CHUNK], pick[:, r, hh, :], start=True, stop=True)
            last.then_inc(picked, 1)
            pe.wait_ge(dve_step, 10)
            for r in range(2):
                nc.tensor.matmul(c.ps[:, 3 + r, 0:48], c.tab["tri2"][:, r * 128:(r + 1) * 128], by_dir(small(c, "g"), r),
                                 start=True, stop=True)
            nc.tensor.matmul(c.ps[:, 5, 0:96], c.tab["heads"], small(c, "g"), start=True, stop=True).then_inc(summed, 1)

        @block.vector
        def _(dve):
            v = nc.vector
            link = chain(dve, dve_step)
            dve.wait_ge(product, 1)
            v.tensor_copy(ba[:, 0:N_X], c.ps[0:32, 0, :])
            v.tensor_copy(ba[:, N_X:N_ALL], c.ps[0:32, 1, 0:N_Z]).then_inc(drained, 1)
            dve.wait_ge(picked, 1)
            link(v.tensor_copy(raw.rearrange("p s v -> p (s v)"), c.ps[:, 2, 0:192]))
            dve.wait_ge(consts_in, 32)
            for hh in range(2):
                half = slice(64 * hh, 64 * hh + 64)
                last = v.tensor_copy(rates[half], by_head[half, :, hh::2])
            last.then_inc(rates_in, 1)
            dve.wait_ge(rates_in, 1)
            alpha = raw[:, :, 4:8]
            dt = rates[:, 1, :].rearrange("p (u v) -> p u v", u=2).unsqueeze(1).to_broadcast([128, STEPS, 2, 4])
            link(v.tensor_tensor(alpha.rearrange("p (s u) v -> p s u v", u=2),
                                 alpha.rearrange("p (s u) v -> p s u v", u=2), dt, ALU.add))
            link(v.tensor_scalar(s24("work"), alpha, -1.0, None, ALU.mult))
            link(v.tensor_tensor(s24("work"), s24("work"), alpha, ALU.min))
            dve.wait_ge(act_step, 4)
            link(v.tensor_scalar(s24("beta"), s24("beta"), 1.0, None, ALU.add))
            link(v.reciprocal(s24("beta"), s24("beta")))
            link(v.tensor_scalar(s24("g"), alpha, 0.0, None, ALU.max))
            link(v.tensor_tensor(s24("g"), s24("g"), s24("work"), ALU.add))
            rate = rates[:, 0, :].rearrange("p (u v) -> p u v", u=2).unsqueeze(1).to_broadcast([128, STEPS, 2, 4])
            g4 = small(c, "g").rearrange("p (s u v) -> p s u v", u=2, v=4)
            link(v.tensor_tensor(g4, g4, rate, ALU.mult))
            link(v.tensor_scalar(s24("g"), s24("g"), -1.0, None, ALU.mult))
            dve.wait_ge(summed, 1)
            for r in range(2):
                link(v.tensor_copy(by_dir(small(c, "gc"), r), c.ps[:, 3 + r, 0:48].rearrange("p (s v) -> p s v", v=4)))
            link(v.tensor_copy(small(c, "exp_last"), c.ps[:, 5, 0:96]))
            link(v.tensor_tensor(small(c, "exp_tail"), small(c, "exp_last"), small(c, "gc"), ALU.subtract))
            dve.wait_ge(act_step, 7)
            link(v.tensor_tensor(small(c, "beta_exp_gc"), small(c, "beta"), small(c, "exp_gc"), ALU.mult))

        @block.scalar
        def _(act):
            link = chain(act, act_step)
            act.wait_ge(dve_step, 1)
            link(nc.scalar.activation(s24("beta"), raw[:, :, 0:4], ACT.Exp, scale=-1.0))
            act.wait_ge(dve_step, 4)
            link(nc.scalar.activation(s24("work"), s24("work"), ACT.Exp))
            link(nc.scalar.activation(rates[:, 0, :], rates[:, 0, :], ACT.Exp))
            link(nc.scalar.activation(s24("work"), s24("work"), ACT.Ln, bias=1.0))
            act.wait_ge(dve_step, 14)
            nc.scalar.activation(small(c, "exp_gc"), small(c, "gc"), ACT.Exp).then_inc(act_step, 1)
            nc.scalar.activation(small(c, "exp_last"), small(c, "exp_last"), ACT.Exp).then_inc(act_step, 1)
            nc.scalar.activation(small(c, "exp_tail"), small(c, "exp_tail"), ACT.Exp).then_inc(act_step, 1)


def head_norm(c, buf, tiles, n_sum, extra, finish, work_at):
    nc = c.nc
    st, sem = stage(c)
    sq = work_at[:, 0:2 * N_ALL].rearrange("p (b t) -> p b t", b=2)
    root = work_at[:, 2 * N_ALL:4 * N_ALL].rearrange("p (b t) -> p b t", b=2)
    flat = c.ps.rearrange("p b n -> p (b n)")
    with st, nc.Block() as block:
        squared, summed, rooted, act_chain, done, dve_chain = \
            (sem(n) for n in ("squared", "summed", "rooted", "act_chain", "done", "dve_chain"))

        @block.tensor
        def _(pe):
            for n in range(len(tiles)):
                pe.wait_ge(squared, n + 1)
                if n >= 4:
                    pe.wait_ge(rooted, n - 3)
                s = (n % 4) * 2
                nc.tensor.matmul(c.ps[:, s, :], c.tab["heads"], sq[:, n % 2, 0:N_X], start=True, stop=True)
                nc.tensor.matmul(c.ps[:, s + 1, 0:N_Z], c.tab["heads"], sq[:, n % 2, N_X:N_ALL],
                                 start=True, stop=True).then_inc(summed, 1)

        @block.scalar
        def _(act):
            link = chain(act, act_chain)

            def square(n):
                if n < len(tiles):
                    if n >= 2:
                        act.wait_ge(summed, n - 1)
                    nc.scalar.activation(sq[:, n % 2, :], buf[:, tiles[n], :], ACT.Square).then_inc(squared, 1)

            square(0)
            for n in range(len(tiles)):
                square(n + 1)
                act.wait_ge(summed, n + 1)
                if n >= 2:
                    act.wait_ge(done, n - 1)
                link(nc.scalar.activation(root[:, n % 2, :], flat[:, (n % 4) * 1024:(n % 4) * 1024 + N_ALL],
                                          ACT.Ln, bias=EPS, scale=1.0 / n_sum))
                nc.scalar.activation(root[:, n % 2, :], root[:, n % 2, :], ACT.Exp, bias=extra(n),
                                     scale=-0.5).then_inc(rooted, 1)

        @block.vector
        def _(dve):
            link = chain(dve, dve_chain)
            for n in range(len(tiles)):
                dve.wait_ge(rooted, n + 1)
                finish(link, buf[:, tiles[n], :], root[:, n % 2, :], n).then_inc(done, 1)


def chunk_tables(c):
    view = lambda ap: ap.rearrange("p (k t) -> p k t", k=4)
    n = 4 * N_ALL
    return view(c.ring[:, 0:n]), view(c.ht[:, 0:n]), view(c.ht[:, n:2 * n])


def idle_tables(c):
    o = _TABLE["win_l"][0]
    return [c.table[:, o + 512 * i:o + 512 * i + 512] for i in range((TABLE_COLS - o) // 512)]


def reload_tables(c, sp, loaded):
    for o, n in ((_TABLE["cos"][0], 1024), (_TABLE["win_l"][0], TABLE_COLS - _TABLE["win_l"][0])):
        sp.dma_start(c.table[:, o:o + n], c.a["t_table"][:, o:o + n]).then_inc(loaded, 16)


def chunk_products(c):
    nc = c.nc
    st, sem = stage(c)
    qkv, _, _ = gdn_buffers(c)
    q, k, v = (qkv[:, 4 * i:4 * i + 4, :] for i in range(3))
    k_rows, k_k, k_q = chunk_tables(c)
    banks = lambda g, what: c.ps[:, 4 * (g % 2) + what, :].rearrange("p (u t) -> p u t", u=4)
    groups = N_ALL // 128

    with st, nc.Block() as block:
        turned, multiplied, dve_drained, act_drained = (sem(n) for n in ("turned", "multiplied", "dve_drained", "act_drained"))

        @block.tensor
        def _(pe):
            for g in range(groups):
                if g >= 2:
                    pe.wait_ge(act_drained, g - 1)
                for what, last_of in ((0, None), (1, turned), (2, None), (3, multiplied)):
                    if what == 2 and g >= 2:
                        pe.wait_ge(dve_drained, g - 1)
                    for half in range(2):
                        t = slice(128 * g + 64 * half, 128 * g + 64 * half + 64)
                        for p in range(4):
                            for hh in range(2):
                                pa = slice(64 * hh, 64 * hh + 64)
                                unit = c.tab["ident"][pa, pa]
                                left, right = ((k, unit), (v, unit), (k, k[pa, p, t]), (k, q[pa, p, t]))[what]
                                last = nc.tensor.matmul(banks(g, what)[pa, p, 64 * half:64 * half + 64],
                                                        left[pa, p, t], right, start=True, stop=True)
                    if last_of is not None:
                        last.then_inc(last_of, 1)

        @block.scalar
        def _(act):
            for g in range(groups):
                t = slice(128 * g, 128 * g + 128)
                act.wait_ge(turned, g + 1)
                nc.scalar.activation(k_rows[:, :, t], banks(g, 0), ACT.Copy)
                nc.scalar.activation(v[:, :, t], banks(g, 1), ACT.Copy).then_inc(act_drained, 1)

        @block.vector
        def _(dve):
            for g in range(groups):
                t = slice(128 * g, 128 * g + 128)
                dve.wait_ge(multiplied, g + 1)
                nc.vector.tensor_copy(k_k[:, :, t], banks(g, 2))
                nc.vector.tensor_copy(k_q[:, :, t], banks(g, 3)).then_inc(dve_drained, 1)


def delta_rule(c):
    nc = c.nc
    st, sem = stage(c)
    qkv, gate, o = gdn_buffers(c)
    k_rows, k_k, k_q = chunk_tables(c)
    out = outc(c)
    pool = [c.arena[:, o + 512 * i:o + 512 * i + 512] for i in range((c.arena_size - o) // 512)]
    pool += [c.ring[:, 4 * N_ALL + 512 * i:4 * N_ALL + 512 * i + 512] for i in range((RING * SLOT - 4 * N_ALL) // 512)]
    pool += [c.tab["cos"], c.tab["sin"]] + idle_tables(c)
    take = lambda: pool.pop()
    two = lambda: [take(), take()]
    q_k, q_dec, X_t = (two() for _ in range(3))
    decay, dist, v_beta, v_new, S, S_kept, g_tri = (take() for _ in range(7))
    by_heads = lambda ap: ap.rearrange("p (v h e) -> p v h e", v=4, h=2)
    A, X, T, k_tail = ([by_heads(take()) for r in range(2)] for _ in range(4))
    parts = (slice(0, 64), slice(64, 128))
    tail_by_heads = c.arena[:, c.arena_size - 192:].rearrange("p (n h) -> p n h", h=2)
    half = lambda ap, r: ap[:, 256 * r:256 * r + 256]
    four = lambda ap: ap.rearrange("p (u v e) -> p u v e", u=2, v=4)
    rows = lambda name, s: small(c, name)[:, 8 * s:8 * s + 8].unsqueeze(2).to_broadcast([128, 8, 64])
    rows_r = lambda name, s, r: small(c, name)[:, 8 * s + 4 * r:8 * s + 4 * r + 4].unsqueeze(2).to_broadcast([128, 4, 64])
    eight = lambda ap: ap.rearrange("p (n e) -> p n e", n=8)
    pairs = lambda ap: ap.rearrange("p (v e) -> p v e", v=4)
    table = lambda ap: ap.rearrange("p (u e) -> p u e", u=2).unsqueeze(2).to_broadcast([128, 2, 4, 64])
    table_r = lambda ap, r: ap[:, 64 * r:64 * r + 64].unsqueeze(1).to_broadcast([128, 4, 64])
    eye = c.tab["eye"].unsqueeze(1).to_broadcast([128, 4, 64])
    mask_t = lambda n, r: table_r(c.tab["mt"][:, n * 128:(n + 1) * 128], r)
    chunk = lambda buf, s, r: buf[:, 0:4, chunk_of(s, r):chunk_of(s, r) + 64]
    NL = len(LEVELS)
    heads = [(p, slice(64 * hh, 64 * hh + 64), slice(p * 64, p * 64 + 64)) for p in range(4) for hh in range(2)]
    blocks = [(r, p, pa, slice(256 * r + 64 * p, 256 * r + 64 * p + 64)) for r in range(2) for p, pa, _ in heads]
    B_GR, B_X, B_XT, B_REC, B_OUT, B_STATE = 0, 1, 3, 5, 6, 7

    with st, nc.Block() as block:
        names = ("g_spread", "decays", "dist_read", "masked_dist", "exps", "q_dec_exps", "q_scaled", "a_ready",
                 "v_scaled", "k_scaled", "state_read", "residual", "v_ps", "v_ready", "out_ps", "state_ps",
                 "state", "out_added", "dve_chain", "inverse_set", "zeroed",
                 "tail_placed", "k_k_scaled", "lowered", "block_masked", "state_kept")
        s_ = {n: sem(n) for n in names}
        level_t, level_masked, grown, inverse_t, inverse = ([sem(f"{n}{r}") for r in range(2)]
                                                 for n in ("level_t", "level_masked", "grown", "inverse_t", "inverse"))

        @block.tensor
        def _(pe):
            mm = nc.tensor.matmul

            def decays(s):
                pe.wait_ge(s_["g_spread"], s + 1)
                if s:
                    pe.wait_ge(s_["dist_read"], s)
                    pe.wait_ge(s_["q_dec_exps"], s)
                mm(c.ps[:, B_GR, :], c.tab["heads"], g_tri, start=True, stop=True).then_inc(s_["decays"], 1)

            def transposed_a(s, n, r):
                if n == 0:
                    pe.wait_ge(s_["a_ready"], s + 1)
                else:
                    pe.wait_ge(inverse_t[r], NL * s + n)
                for p in range(4):
                    fr = slice(64 * p, 64 * p + 64)
                    rhs = c.tab["eye"] if n == 0 else half(X_t[s % 2], r)[:, fr]
                    last = mm(c.ps[:, (B_XT if n else B_X) + r, fr], A[r][:, p].rearrange("p h e -> p (h e)"), rhs, start=True, stop=True)
                last.then_inc(level_t[r], 1)

            def products(s, n, r):
                if n == 1:
                    pe.wait_ge(s_["inverse_set"], s + 1)
                else:
                    pe.wait_ge(inverse[r], (NL - 2) * s + n - 1)
                pe.wait_ge(level_masked[r], NL * s + n + 1)
                whole = lambda m, p: m[r][:, p].rearrange("p h e -> p (h e)")
                for p in range(4):
                    last = mm(c.ps[:, B_XT + r, 128 * p:128 * p + 128], whole(X, p), whole(T, p), start=True, stop=True)
                if n < NL - 1:
                    for p in range(4):
                        last = mm(c.ps[:, B_X + r, 128 * p:128 * p + 128], whole(T, p), whole(X, p), start=True, stop=True)
                last.then_inc(grown[r], 1)

            def read_state(s):
                pe.wait_ge(s_["state"], s + 1)
                for r, p, pa, fr in blocks:
                    t0 = chunk_of(s, r)
                    last = mm(c.ps[pa, B_REC, fr], qkv[pa, 4 + p, t0:t0 + 64], S[pa, fr], start=True, stop=True)
                last.then_inc(s_["state_read"], 1)

            def new_values(s):
                for r in range(2):
                    pe.wait_ge(inverse_t[r], NL * (s + 1))
                pe.wait_ge(s_["residual"], s + 1)
                for r, p, pa, fr in blocks:
                    last = mm(c.ps[pa, B_REC, fr], X_t[s % 2][pa, fr], v_beta[pa, fr],
                              start=True, stop=True)
                last.then_inc(s_["v_ps"], 1)

            def outputs(s):
                pe.wait_ge(s_["v_ready"], s + 1)
                pe.wait_ge(s_["k_scaled"], s + 1)
                for r in range(2):
                    for p in range(4):
                        fr = slice(256 * r + 64 * p, 256 * r + 64 * p + 64)
                        last = mm(c.ps[:, B_STATE, fr], k_tail[r][:, p].rearrange("p h e -> p (h e)"), v_new[:, fr],
                                  start=True, stop=True)
                last.then_inc(s_["state_ps"], 1)
                pe.wait_ge(s_["q_scaled"], s + 1)
                if s:
                    pe.wait_ge(s_["out_added"], s)
                for r, p, pa, fr in blocks:
                    mm(c.ps[pa, B_OUT, fr], S[pa, fr], q_dec[s % 2][pa, fr], start=True, stop=False)
                    last = mm(c.ps[pa, B_OUT, fr], v_new[pa, fr], q_k[s % 2][pa, fr], start=False, stop=True)
                last.then_inc(s_["out_ps"], 1)

            decays(0)
            for s in range(STEPS):
                for r in range(2):
                    transposed_a(s, 0, r)
                if s:
                    read_state(s - 1)
                if s + 1 < STEPS:
                    decays(s + 1)
                for n in range(1, NL):
                    for r in range(2):
                        transposed_a(s, n, r)
                    for r in range(2):
                        products(s, n, r)
                    if s and n == 1:
                        new_values(s - 1)
                    if s and n == 2:
                        outputs(s - 1)
            read_state(STEPS - 1)
            new_values(STEPS - 1)
            outputs(STEPS - 1)

        @block.scalar
        def _(act):
            def decay_exps(s):
                act.wait_ge(s_["masked_dist"], 2 * s + 1)
                nc.scalar.activation(decay, decay, ACT.Exp).then_inc(s_["exps"], 1)
                if s >= 2:
                    act.wait_ge(s_["out_ps"], s - 1)
                act.wait_ge(s_["dist_read"], s + 1)
                nc.scalar.activation(q_dec[s % 2], c.ps[:, B_GR, :], ACT.Exp).then_inc(s_["q_dec_exps"], 1)
                act.wait_ge(s_["masked_dist"], 2 * s + 2)
                nc.scalar.activation(q_k[s % 2], q_k[s % 2], ACT.Exp).then_inc(s_["exps"], 1)

            def place_lower(s):
                act.wait_ge(s_["lowered"], s + 1)
                for r in range(2):
                    if s:
                        act.wait_ge(level_t[r], NL * s)
                    else:
                        act.wait_ge(s_["zeroed"], 1)
                    for hh, pa in enumerate(parts):
                        last = nc.scalar.activation(A[r][pa, :, hh], pairs(half(decay, r))[pa], ACT.Copy)
                last.then_inc(s_["a_ready"], 1)

            decay_exps(0)
            place_lower(0)
            for s in range(STEPS + 1):
                if s:
                    act.wait_ge(s_["v_ps"], s)
                    nc.scalar.activation(v_new, c.ps[:, B_REC, :], ACT.Copy).then_inc(s_["v_ready"], 1)
                if s + 1 < STEPS:
                    decay_exps(s + 1)
                    place_lower(s + 1)

        @block.gpsimd
        def _(pool_):
            tt = nc.gpsimd.tensor_tensor

            def spread(s):
                if s:
                    pool_.wait_ge(s_["decays"], s)
                tt(four(g_tri), rows("g", s).rearrange("p (u v) e -> p u v e", u=2), table(c.tab["tri"]),
                   ALU.mult).then_inc(s_["g_spread"], 1)

            def mask(s):
                pool_.wait_ge(s_["dist_read"], s + 1)
                tt(four(decay), four(dist), table(c.tab["mask_a"]), ALU.add).then_inc(s_["masked_dist"], 1)
                if s >= 2:
                    pool_.wait_ge(s_["out_ps"], s - 1)
                tt(four(q_k[s % 2]), table(c.tab["mask_q"]), four(dist), ALU.subtract).then_inc(s_["masked_dist"], 1)
                pool_.wait_ge(s_["masked_dist"], 2 * s + 2)
                for r in range(2):
                    last = tt(pairs(half(dist, r)), chunk(k_k, s, r), rows_r("beta", s, r), ALU.mult)
                last.then_inc(s_["k_k_scaled"], 1)

            def block_mask(s):
                pool_.wait_ge(s_["a_ready"], s + 1)
                for r in range(2):
                    last = tt(pairs(half(decay, r)), pairs(half(decay, r)), table_r(c.tab["m1"], r), ALU.mult)
                last.then_inc(s_["block_masked"], 1)

            def keep_state(s):
                pool_.wait_ge(s_["state"], s + 1)
                tt(eight(S_kept), eight(S), rows("exp_last", s), ALU.mult).then_inc(s_["state_kept"], 1)

            def scale_queries(s):
                pool_.wait_ge(s_["q_dec_exps"], s + 1)
                for r in range(2):
                    tt(four(q_dec[s % 2])[:, r], four(q_dec[s % 2])[:, r], chunk(qkv, s, r), ALU.mult)
                pool_.wait_ge(s_["exps"], 2 * s + 2)
                for r in range(2):
                    last = tt(four(q_k[s % 2])[:, r], four(q_k[s % 2])[:, r], chunk(k_q, s, r), ALU.mult)
                last.then_inc(s_["q_scaled"], 1)

            for m in (*X, *T, *A):
                last = nc.gpsimd.memset(m, 0.0)
            last.then_inc(s_["zeroed"], 1)
            spread(0)
            mask(0)
            scale_queries(0)
            block_mask(0)
            for s in range(STEPS):
                if s + 1 < STEPS:
                    spread(s + 1)
                    mask(s + 1)
                if s:
                    pool_.wait_ge(s_["v_ps"], s)
                for r in range(2):
                    last = tt(pairs(half(v_beta, r)), chunk(qkv[:, 8:12, :], s, r), rows_r("beta", s, r), ALU.mult)
                last.then_inc(s_["v_scaled"], 1)
                if s:
                    pool_.wait_ge(s_["state_ps"], s)
                else:
                    pool_.wait_ge(s_["tail_placed"], 1)
                for r in range(2):
                    k = chunk(k_rows, s, r).unsqueeze(2).to_broadcast([128, 4, 2, 64])
                    tail = tail_by_heads[:, 8 * s + 4 * r:8 * s + 4 * r + 4, :].unsqueeze(3).to_broadcast([128, 4, 2, 64])
                    last = tt(k_tail[r], k, tail, ALU.mult)
                last.then_inc(s_["k_scaled"], 1)
                if s + 1 < STEPS:
                    scale_queries(s + 1)
                keep_state(s)
                if s + 1 < STEPS:
                    block_mask(s + 1)

        @block.vector
        def _(dve):
            v = nc.vector
            link = chain(dve, s_["dve_chain"])

            def residual(s):
                dve.wait_ge(s_["state_read"], s + 1)
                link(v.tensor_tensor(eight(dist), eight(c.ps[:, B_REC, :]), rows("beta_exp_gc", s), ALU.mult))
                dve.wait_ge(s_["v_scaled"], s + 1)
                v.tensor_tensor(v_beta, v_beta, dist, ALU.subtract).then_inc(s_["residual"], 1)

            def state(s):
                dve.wait_ge(s_["out_ps"], s + 1)
                dve.wait_ge(s_["state_kept"], s + 1)
                v.tensor_tensor(S, S_kept, c.ps[:, B_STATE, :], ALU.add).then_inc(s_["state"], 1)
                first = s < CZ // 2 or CZ <= s < CZ + CX // 2
                for r in range(2):
                    dst, src = chunk(out, s, r), four(c.ps[:, B_OUT, :])[:, r]
                    last = v.tensor_copy(dst, src) if first else v.tensor_tensor(dst, dst, src, ALU.add)
                last.then_inc(s_["out_added"], 1)

            def distances(s):
                dve.wait_ge(s_["decays"], s + 1)
                v.tensor_tensor(eight(dist), rows("gc", s), eight(c.ps[:, B_GR, :]), ALU.subtract)\
                    .then_inc(s_["dist_read"], 1)

            def lower(s):
                dve.wait_ge(s_["k_k_scaled"], s + 1)
                dve.wait_ge(s_["exps"], 2 * s + 1)
                v.tensor_tensor(decay, decay, dist, ALU.mult).then_inc(s_["lowered"], 1)

            def first_inverse(s):
                dve.wait_ge(s_["block_masked"], s + 1)
                for r in range(2):
                    for hh, pa in enumerate(parts):
                        last = v.tensor_tensor(X[r][pa, :, hh], eye[pa], pairs(half(decay, r))[pa], ALU.subtract)
                last.then_inc(s_["inverse_set"], 1)

            def mask_level(s, n, r):
                dve.wait_ge(level_t[r], NL * s + n + 1)
                for hh, pa in enumerate(parts):
                    last = v.tensor_tensor(T[r][pa, :, hh], pairs(c.ps[pa, (B_XT if n else B_X) + r, 0:256]), mask_t(n, r)[pa], ALU.mult)
                last.then_inc(level_masked[r], 1)

            v.memset(S, 0.0).then_inc(s_["state"], 1)
            link(v.memset(tail_by_heads, 0.0))
            for hh, pa in enumerate(parts):
                last = v.tensor_copy(tail_by_heads[pa, :, hh], small(c, "exp_tail")[pa])
            last.then_inc(s_["tail_placed"], 1)
            dve.wait_ge(s_["zeroed"], 1)
            def grow(s, n, r):
                whole = X[r].rearrange("p v h e -> p (v h e)")
                v.tensor_tensor(whole, whole, c.ps[:, B_X + r, :], ALU.subtract).then_inc(inverse[r], 1)

            def grow_t(s, n, r):
                if n:
                    dve.wait_ge(grown[r], (NL - 1) * s + n)
                else:
                    dve.wait_ge(level_masked[r], NL * s + 1)
                for hh, pa in enumerate(parts):
                    dst = pairs(half(X_t[s % 2], r))[pa]
                    more = by_heads(c.ps[:, B_XT + r, :])[pa, :, hh] if n else T[r][pa, :, hh]
                    last = v.tensor_tensor(dst, dst if n else eye[pa], more, ALU.subtract)
                last.then_inc(inverse_t[r], 1)

            distances(0)
            lower(0)
            for s in range(STEPS):
                mask_level(s, 0, 0)
                mask_level(s, 0, 1)
                grow_t(s, 0, 0)
                grow_t(s, 0, 1)
                first_inverse(s)
                for n in range(1, NL):
                    mask_level(s, n, 0)
                    if n > 1:
                        grow(s, n - 1, 1)
                    mask_level(s, n, 1)
                    if s and n == 1:
                        residual(s - 1)
                    if s and n == 3:
                        state(s - 1)
                    if s + 1 < STEPS:
                        if n == 2:
                            distances(s + 1)
                        if n == 4:
                            lower(s + 1)
                    grow_t(s, n, 0)
                    if n < NL - 1:
                        grow(s, n, 0)
                    grow_t(s, n, 1)
            residual(STEPS - 1)
            state(STEPS - 1)


def norm_qk(c):
    buf, _, o = gdn_buffers(c)
    head_norm(c, buf, range(8), 1, lambda n: math.log(GW // GH) * -0.5 if n < 4 else 0.0,
              lambda link, y, root, n: c.nc.vector.tensor_tensor(y, y, root, ALU.mult), c.arena[:, o:])


def gdn_output(c):
    nc, a = c.nc, c.a
    _, gate, o = gdn_buffers(c)
    gain = c.stat[:, 205:206]
    st, sem = stage(c)
    gain_in = sem("gain_in")
    with st:
        with nc.Block() as block:
            @block.sync
            def _(sp):
                for hh in range(2):
                    sp.dma_start(gain[64 * hh:64 * hh + 64, :], a["gdn_norm_g"][0].unsqueeze(1)).then_inc(gain_in, 16)
                c.prefetch(sp, "ab_out")
                reload_tables(c, sp, c.tables_back)
                sp.wait_ge(gain_in, 32)

    def finish(link, y, root, n):
        link(nc.vector.scalar_tensor_tensor(y, y, gain, root, ALU.mult, ALU.mult))
        return nc.vector.tensor_tensor(y, y, gate[:, n, :], ALU.mult)

    head_norm(c, outc(c), range(4), HEAD, lambda n: 0.0, finish, c.ht)


def mixed_rows(c):
    return c.ht.rearrange("p (t d) -> p t d", t=TT)


def add_branch(c, w, tiles):
    nc = c.nc
    st, sem = stage(c)
    y = mixed_rows(c)
    junk = c.arena[:, 0:D]
    rstd = c.stat[:, 0:TT]
    with st, nc.Block() as block:
        act_chain, stats, dve_chain = sem("act_chain"), sem("stats"), sem("dve_chain")

        @block.scalar
        def _(act):
            link = chain(act, act_chain)
            for t in tiles:
                link(nc.scalar.activation(junk, y[:, t, :], ACT.Square, accum_out=rstd[:, t:t + 1]))
            n = len(tiles)
            link(nc.scalar.activation(rstd[:, 0:n], rstd[:, 0:n], ACT.Ln, bias=EPS, scale=1.0 / D))
            nc.scalar.activation(rstd[:, 0:n], rstd[:, 0:n], ACT.Exp, scale=-0.5).then_inc(stats, 1)

        @block.vector
        def _(dve):
            link = chain(dve, dve_chain)
            dve.wait_ge(stats, 1)
            for t in tiles:
                link(nc.vector.scalar_tensor_tensor(y[:, t, :], y[:, t, :], rstd[:, t:t + 1],
                                                    c.gates[:, w, int(t >= TX), :], ALU.mult, ALU.mult))
                nc.vector.tensor_tensor(token_tile(c, t), token_tile(c, t), y[:, t, :], ALU.add)


def ffn_up(c, l, z):
    nc = c.nc
    st, sem = stage(c)
    name = f"up{l}"
    lo, _ = c.range_of[name]
    ht = ht_view(c)
    hidden, o = ffn_hidden(c)
    n_all = N_X + z
    gbuf = c.arena[:, o:o + 2 * N_ALL].rearrange("p (b t) -> p b t", b=2)
    with st, nc.Block() as block:
        product, drained, summed, gated, done, dve_chain = \
            (sem(n) for n in ("product", "drained", "summed", "gated", "done", "dve_chain"))

        @block.sync
        def _(sp):
            c.issue(sp, name, lambda j: (product, 2 * (2 * (j // 2) + 2)))

        @block.tensor
        def _(pe):
            for n in range(FT):
                for half in range(2):
                    chunk = lo + 2 * (n // 2) + half
                    if n % 2 == 0:
                        c.arrived(pe, chunk)
                    if n >= 2:
                        pe.wait_ge(summed, 2 * (n - 2) + half + 1)
                    w = c.slot(chunk, KT, 256)[:, :, n % 2 * 128:n % 2 * 128 + 128]
                    bank = 4 * (n % 2) + 2 * half
                    for k in range(KT):
                        last = nc.tensor.matmul(c.ps[:, bank, :], w[:, k, :], ht[:, k, 0:N_X],
                                                start=k == 0, stop=k == KT - 1)
                        if z:
                            last = nc.tensor.matmul(c.ps[:, bank + 1, 0:z], w[:, k, :], ht[:, k, N_X:N_X + z],
                                                    start=k == 0, stop=k == KT - 1)
                    last.then_inc(product, 1)

        def middle_tap(n, half):
            return ffn_tap(c, l, 1, n + half * FT)

        @block.scalar
        def _(act):
            def gate(n):
                act.wait_ge(summed, 2 * n + 2)
                nc.scalar.activation(gbuf[:, n % 2, 0:n_all], gbuf[:, n % 2, 0:n_all], ACT.Silu).then_inc(gated, 1)

            for n in range(FT):
                for half in range(2):
                    act.wait_ge(product, 2 * n + half + 1)
                    bank = 4 * (n % 2) + 2 * half
                    if half and n >= 2:
                        act.wait_ge(done, n - 1)
                    dst = gbuf[:, n % 2, :] if half else hidden[:, n, :]
                    nc.scalar.activation(dst[:, 0:N_X], c.ps[:, bank, :], ACT.Identity,
                                         scale=middle_tap(n, half)).then_inc(drained, 1)
                    if z:
                        nc.scalar.activation(dst[:, N_X:n_all], c.ps[:, bank + 1, 0:z], ACT.Identity,
                                             scale=middle_tap(n, half)).then_inc(drained, 1)
                    if half == 0 and n:
                        gate(n - 1)
            gate(FT - 1)

        @block.vector
        def _(dve):
            link = chain(dve, dve_chain)
            per = 2 if z else 1

            def multiply(n):
                dve.wait_ge(gated, n + 1)
                nc.vector.tensor_tensor(hidden[:, n, 0:n_all], hidden[:, n, 0:n_all], gbuf[:, n % 2, 0:n_all],
                                        ALU.mult).then_inc(done, 1)

            for n in range(FT):
                for half in range(2):
                    dve.wait_ge(drained, per * (2 * n + half + 1))
                    bank = 4 * (n % 2) + 2 * half
                    dst = gbuf[:, n % 2, :] if half else hidden[:, n, :]
                    convolve(c, link, dst, c.ps[:, bank, :], c.ps[:, bank + 1, :], z,
                             lambda t: ffn_tap(c, l, t, n + half * FT)).then_inc(summed, 1)
                    if half == 0 and n:
                        multiply(n - 1)
            multiply(FT - 1)


def ffn_hidden(c):
    return c.arena[:, 0:FT * N_ALL].rearrange("p (k t) -> p k t", k=FT), FT * N_ALL


def feed_forward(c, l, z, tiles):
    norm_to_features(c, 1, tiles)
    ffn_up(c, l, z)
    project_tokens(c, f"down{l}", ffn_hidden(c)[0], FT, 2, 128, tiles,
                   lambda t, j: mixed_rows(c)[:, t, j * 128:(j + 1) * 128], mod_layer=1 if l == 0 else None)
    add_branch(c, 1, tiles)


def layer_ab(c):
    spread_modulation(c, 0)
    norm_to_features(c, 0, range(TT))
    project_features(c, "diff_qk", 8, diff_buffers(c)[0], "rope")
    project_tokens(c, "diff_v", ht_view(c), KT, 1, 256, range(TT),
                   lambda t, j: diff_buffers(c)[1][:, t, j * 256:(j + 1) * 256])
    lambda_value(c)
    diff_attention(c)
    gdn_gates(c)
    project_features(c, "gdn_gate", 4, gdn_buffers(c)[1], "silu")
    project_features(c, "gdn_qkv", 12, gdn_buffers(c)[0], "conv_silu", taps=lambda t, n: gdn_tap(c, t, n),
                     ahead=0)
    norm_qk(c)
    chunk_products(c)
    delta_rule(c)
    gdn_output(c)
    project_tokens(c, "ab_out", outc(c), KT, 1, 256, range(TT),
                   lambda t, j: mixed_rows(c)[:, t, j * 256:(j + 1) * 256])
    add_branch(c, 0, range(TT))
    feed_forward(c, 0, N_Z, range(TT))


def cd_buffers(c):
    at = [0]

    def take(n):
        at[0] += n
        return c.arena[:, at[0] - n:at[0]]

    out = take(KT * N_X).rearrange("p (k t) -> p k t", k=KT)
    q = take(4 * N_X).rearrange("p (k t) -> p k t", k=4)
    k = take(N_ALL).rearrange("p (k t) -> p k t", k=1)
    k2 = take(2 * N_ALL).rearrange("p (g t) -> p g t", g=2)
    v = take(TT * 128).rearrange("p (t e) -> p t e", t=TT)
    prob = take(2 * 640).rearrange("p (b m) -> p b m", b=2)
    turned = take(2 * 640).rearrange("p (b m) -> p b m", b=2)
    u = take(12 * N_X).rearrange("p (k t) -> p k t", k=12)
    return out, q, k, k2, v, prob, turned, u


def window_attention(c):
    nc, a = c.nc, c.a
    st, sem = stage(c)
    out, q_, k_, k2, v_, prob, turned, _ = cd_buffers(c)
    top, neg, total, sink_exp = (c.stat[:, 2 * i:2 * i + 2] for i in range(4))
    sink, neg_sink = c.stat[:, 16:24], c.stat[:, 24:32]
    units = [(q, h) for q in range(TX) for h in range(8)]
    n_units = len(units)
    scale = HEAD ** -0.5
    flat = c.ps.rearrange("p b n -> p (b n)")
    score = lambda u: flat[:, (u % 2) * 1024:(u % 2) * 1024 + 640]
    turn = flat[:, 2048:2048 + 640]
    window = lambda q: range(max(0, q - 1), min(TX, q + 2))
    tiles = lambda q: [TX, TX + 1] + list(window(q))
    with st, nc.Block() as block:
        names = ("sink_in", "ready", "scored", "maxed", "exped", "sink_exped", "weighed", "turned_ps", "turned_sb",
                 "valued", "written", "dve_chain")
        sink_in, ready, scored, maxed, exped, sink_exped, weighed, turned_ps, turned_sb, valued, written, dve_chain = \
            (sem(n) for n in names)

        @block.sync
        def _(sp):
            sp.dma_start(sink, a["swa_sink"][0].partition_broadcast(128)).then_inc(sink_in, 16)

        @block.tensor
        def _(pe):
            pe.wait_ge(ready, 1)
            for i in range(n_units + 2):
                if i < n_units:
                    q, h = units[i]
                    if i >= 2:
                        pe.wait_ge(exped, i - 1)
                    pa = slice(64 * (h % 2), 64 * (h % 2) + 64)
                    lhs, keys, s = q_[pa, h // 2, q * 128:(q + 1) * 128], k2[pa, h // 4, :], score(i)
                    w = window(q)
                    first = w[0] * 128
                    nc.tensor.matmul(s[:, 0:N_Z], lhs, keys[:, N_X:N_ALL], start=True, stop=True)
                    last = nc.tensor.matmul(s[:, N_Z:512], lhs, keys[:, first:first + 256], start=True, stop=True)
                    if len(w) == 3:
                        last = nc.tensor.matmul(s[:, 512:640], lhs, keys[:, first + 256:first + 384],
                                                start=True, stop=True)
                    last.then_inc(scored, 1)
                if 0 <= i - 1 < n_units:
                    u = i - 1
                    q, h = units[u]
                    pe.wait_ge(weighed, u + 1)
                    if u:
                        pe.wait_ge(turned_sb, u)
                    for m in range(len(tiles(q))):
                        last = nc.tensor.transpose(turn[:, m * 128:(m + 1) * 128],
                                                   prob[:, u % 2, m * 128:(m + 1) * 128], c.tab["ident"])
                    last.then_inc(turned_ps, 1)
                if 0 <= i - 2 < n_units:
                    u = i - 2
                    q, h = units[u]
                    pe.wait_ge(turned_sb, u + 1)
                    if u >= 2:
                        pe.wait_ge(written, u - 1)
                    pa, g = slice(64 * (h % 2), 64 * (h % 2) + 64), h // 4
                    for m, t in enumerate(tiles(q)):
                        last = nc.tensor.matmul(c.ps[pa, 6 + u % 2, 0:128], v_[:, t, 64 * g:64 * g + 64],
                                                turned[:, u % 2, m * 128:(m + 1) * 128],
                                                start=m == 0, stop=m == len(tiles(q)) - 1)
                    last.then_inc(valued, 1)

        @block.scalar
        def _(act):
            for i in range(n_units + 1):
                if i < n_units:
                    q, h = units[i]
                    n = len(tiles(q)) * 128
                    act.wait_ge(maxed, i + 1)
                    if i >= 2:
                        act.wait_ge(turned_ps, i - 1)
                    nc.scalar.activation(prob[:, i % 2, 0:n], score(i)[:, 0:n], ACT.Exp, bias=neg[:, i % 2:i % 2 + 1],
                                         scale=scale, accum_out=total[:, i % 2:i % 2 + 1]).then_inc(exped, 1)
                    nc.scalar.activation(sink_exp[:, i % 2:i % 2 + 1], sink[:, h:h + 1], ACT.Exp,
                                         bias=neg[:, i % 2:i % 2 + 1]).then_inc(sink_exped, 1)
                if 0 <= i - 1 < n_units:
                    u = i - 1
                    n = len(tiles(units[u][0])) * 128
                    act.wait_ge(turned_ps, u + 1)
                    if u >= 2:
                        act.wait_ge(valued, u - 1)
                    nc.scalar.activation(turned[:, u % 2, 0:n], turn[:, 0:n], ACT.Copy).then_inc(turned_sb, 1)

        @block.vector
        def _(dve):
            v = nc.vector
            link = chain(dve, dve_chain)
            dve.wait_ge(sink_in, 16)
            for g in range(2):
                for hh in range(2):
                    v.tensor_copy(k2[64 * hh:64 * hh + 64, g, :], k_[64 * g:64 * g + 64, 0, :])
            v.tensor_scalar(neg_sink, sink, -1.0, None, ALU.mult).then_inc(ready, 1)
            dve.wait_ge(ready, 1)
            for i in range(n_units + 3):
                if i < n_units:
                    q, h = units[i]
                    w = window(q)
                    b = slice(i % 2, i % 2 + 1)
                    n = len(tiles(q)) * 128
                    dve.wait_ge(scored, i + 1)
                    if w[0] == q - 1:
                        link(v.tensor_tensor(score(i)[:, 256:384], score(i)[:, 256:384], c.tab["win_l"], ALU.add))
                    if w[-1] == q + 1:
                        link(v.tensor_tensor(score(i)[:, n - 128:n], score(i)[:, n - 128:n], c.tab["win_r"], ALU.add))
                    link(v.reduce_max(top[:, b], score(i)[:, 0:n], AX.X))
                    if i >= 2:
                        dve.wait_ge(sink_exped, i - 1)
                    v.tensor_scalar(neg[:, b], top[:, b], -scale, neg_sink[:, h:h + 1], ALU.mult, ALU.min)\
                        .then_inc(maxed, 1)
                if 0 <= i - 1 < n_units:
                    u = i - 1
                    b = slice(u % 2, u % 2 + 1)
                    n = len(tiles(units[u][0])) * 128
                    dve.wait_ge(sink_exped, u + 1)
                    link(v.tensor_tensor(total[:, b], total[:, b], sink_exp[:, b], ALU.add))
                    link(v.reciprocal(total[:, b], total[:, b]))
                    v.tensor_scalar(prob[:, u % 2, 0:n], prob[:, u % 2, 0:n], total[:, b], None, ALU.mult)\
                        .then_inc(weighed, 1)
                if 0 <= i - 3 < n_units:
                    u = i - 3
                    q, h = units[u]
                    pa = slice(64 * (h % 2), 64 * (h % 2) + 64)
                    dve.wait_ge(valued, u + 1)
                    v.tensor_copy(out[pa, h // 2, q * 128:(q + 1) * 128], c.ps[pa, 6 + u % 2, 0:128]).then_inc(written, 1)


class Hyena:

    def __init__(self, c):
        at = [KT * N_X]

        def take(n):
            at[0] += n
            return c.arena[:, at[0] - n:at[0]]

        self.out = c.arena[:, 0:KT * N_X].rearrange("p (k t) -> p k t", k=KT)
        four = lambda ap: ap.rearrange("p (s t n) -> p s t n", s=2, t=4)
        self.fwd, self.back, self.kern, self.lags = (four(take(4096)) for _ in range(4))
        self.spec = self.lags
        self.tmp = take(1536).rearrange("p (n c) -> p n c", n=3)
        ht = lambda i: c.ht[:, i * 2048:i * 2048 + 2048].rearrange("p (t n) -> p t n", t=4)
        self.v, self.x1, self.x2t = ht(0), ht(1), ht(2)
        self.z1t = self.x1
        self.decay = c.z.rearrange("p t d -> p (t d)").rearrange("p (t n) -> p t n", t=4)
        self.w3 = c.arena[0:HEAD, 4 * N_X:8 * N_X]
        spare = c.gates[:, :, 1, :].rearrange("p v (h n) -> p v h n", h=2)
        self.root, self.bias0, self.h1, self.h2 = spare[:, 0, 0], spare[:, 0, 1], spare[0:64, 1, 0], spare[0:64, 1, 1]
        self.small = c.small[:, 0:256]


def turn_tiles(c, jobs, copies=()):
    nc = c.nc
    st, sem = stage(c)
    with st, nc.Block() as block:
        turned, act_out, dve_out, copied = sem("turned"), sem("act_out"), sem("dve_out"), sem("copied")

        @block.tensor
        def _(pe):
            for n, (_, blocks) in enumerate(jobs):
                if n >= 8:
                    pe.wait_ge(dve_out if n % 2 else act_out, (n - 8) // 2 + 1)
                for i, b in enumerate(blocks):
                    last = nc.tensor.transpose(c.ps[:, n % 8, i * 128:(i + 1) * 128], b, c.tab["ident"])
                last.then_inc(turned, 1)

        @block.scalar
        def _(act):
            for n, (dst, _) in enumerate(jobs):
                if n % 2 == 0:
                    act.wait_ge(turned, n + 1)
                    nc.scalar.activation(dst, c.ps[:, n % 8, :], ACT.Copy).then_inc(act_out, 1)

        @block.vector
        def _(dve):
            for n, (dst, _) in enumerate(jobs):
                if n % 2:
                    dve.wait_ge(turned, n + 1)
                    nc.vector.tensor_copy(dst, c.ps[:, n % 8, :]).then_inc(dve_out, 1)

        @block.gpsimd
        def _(pool):
            for dst, src in copies:
                nc.gpsimd.tensor_copy(dst, src).then_inc(copied, 1)


def filter_features(c, hy):
    nc, a = c.nc, c.a
    st, sem = stage(c)
    w1, w2 = hy.small[0:33, 0:64], hy.small[0:64, 64:128]
    cols = hy.small[0:64, 128:132]
    n_, r_ = hy.tmp[0:64, 0, :], hy.tmp[0:64, 1, :]
    hi = float(np.float32(6.28125))
    lo = 2 * math.pi - hi
    magic = 12582912.0
    with st, nc.Block() as block:
        w_in, tables_in, product, chained, sined = (sem(n) for n in ("w_in", "tables_in", "product", "chained", "sined"))

        @block.sync
        def _(sp):
            sp.dma_start(w1, a["hy_w1"][0]).then_inc(w_in, 16)
            sp.dma_start(w2, a["hy_w2"][0]).then_inc(w_in, 16)
            for i, v in enumerate((a["hy_b1"][0], a["hy_b2"][0], a["hy_freq"][0, 0], a["hy_freq"][0, 1])):
                sp.dma_start(cols[:, i:i + 1], v.unsqueeze(1)).then_inc(w_in, 16)
            sp.dma_start(hy.w3, a["hy_w3"][0]).then_inc(tables_in, 16)
            sp.dma_start(hy.decay, a["t_decay"].rearrange("(t p) n -> p t n", p=128)).then_inc(tables_in, 16)
            sp.dma_start(hy.bias0, a["hy_bias"][0, 0].partition_broadcast(128)).then_inc(tables_in, 16)
            for s in range(2):
                sp.dma_start(hy.fwd[:, s], a["t_fwd"][s].rearrange("(t p) n -> p t n", p=128)).then_inc(tables_in, 16)
                sp.dma_start(hy.back[:, s], a["t_back"][s].rearrange("(t p) n -> p t n", p=128)).then_inc(tables_in, 16)
            sp.wait_ge(tables_in, 112)

        @block.tensor
        def _(pe):
            pe.wait_ge(w_in, 96)
            nc.tensor.matmul(c.ps[0:64, 0, :], w1, c.tab["feats"][0:33, :], start=True, stop=True).then_inc(product, 1)
            pe.wait_ge(sined, 1)
            nc.tensor.matmul(c.ps[0:64, 1, :], w2, hy.h1, start=True, stop=True).then_inc(product, 1)

        @block.vector
        def _(dve):
            v = nc.vector
            link = chain(dve, chained)
            for i, h in enumerate((hy.h1, hy.h2)):
                dve.wait_ge(product, i + 1)
                link(v.tensor_scalar(h, c.ps[0:64, i, :], cols[:, i:i + 1], cols[:, 2 + i:3 + i], ALU.add, ALU.mult))
                link(v.tensor_scalar(n_, h, 1 / (2 * math.pi), magic, ALU.mult, ALU.add))
                link(v.tensor_scalar(n_, n_, -magic, None, ALU.add))
                link(v.scalar_tensor_tensor(h, n_, -hi, h, ALU.mult, ALU.add))
                link(v.scalar_tensor_tensor(h, n_, -lo, h, ALU.mult, ALU.add))
                link(v.tensor_scalar(h, h, 3.1415925, -3.1415925, ALU.min, ALU.max))

        @block.scalar
        def _(act):
            for i, h in enumerate((hy.h1, hy.h2)):
                act.wait_ge(chained, 6 * (i + 1))
                nc.scalar.activation(h, h, ACT.Sin).then_inc(sined, 1)


def filter_lags(c, hy, order):
    nc = c.nc
    st, sem = stage(c)
    sq = hy.tmp
    with st, nc.Block() as block:
        product, decayed, squared, used, summed, act_chain, combined = \
            (sem(n) for n in ("product", "decayed", "squared", "used", "summed", "act_chain", "combined"))

        @block.tensor
        def _(pe):
            def square_sum(t):
                for side in range(2):
                    n = 2 * t + side
                    pe.wait_ge(squared, n + 1)
                    nc.tensor.matmul(c.ps[:, 7, :], c.tab["ones"], sq[:, n % 3, :], start=n == 0, stop=n == 7,
                                     ).then_inc(used, 1)

            for t in range(4):
                for side in range(2):
                    n = 2 * t + side
                    if n >= 6:
                        pe.wait_ge(decayed, n - 5)
                    col = (order * 2 + side) * 512
                    nc.tensor.matmul(c.ps[:, n % 6, :], hy.h2[:, t * 128:(t + 1) * 128], hy.w3[:, col:col + 512],
                                     start=True, stop=True).then_inc(product, 1)
                if t:
                    square_sum(t - 1)
            square_sum(3)

        @block.vector
        def _(dve):
            v = nc.vector
            for t in range(4):
                for side in range(2):
                    n = 2 * t + side
                    dve.wait_ge(product, n + 1)
                    dst = hy.lags[:, side, t, :]
                    if side and t == 0:
                        v.scalar_tensor_tensor(dst, c.ps[:, n % 6, :], c.tab["nonzero"], hy.decay[:, t, :],
                                               ALU.mult, ALU.mult).then_inc(decayed, 1)
                    else:
                        v.tensor_tensor(dst, c.ps[:, n % 6, :], hy.decay[:, t, :], ALU.mult).then_inc(decayed, 1)
                dve.wait_ge(squared, 2 * t + 2)
                v.tensor_tensor(hy.lags[:, 0, t, :], hy.lags[:, 0, t, :], hy.lags[:, 1, t, :], ALU.add)\
                    .then_inc(combined, 1)
                dve.wait_ge(combined, 2 * t + 1)
                v.scalar_tensor_tensor(hy.lags[:, 1, t, :], hy.lags[:, 1, t, :], -2.0, hy.lags[:, 0, t, :],
                                       ALU.mult, ALU.add).then_inc(combined, 1)

        @block.scalar
        def _(act):
            link = chain(act, act_chain)
            for n in range(8):
                act.wait_ge(decayed, n + 1)
                if n >= 3:
                    act.wait_ge(used, n - 2)
                nc.scalar.activation(sq[:, n % 3, :], hy.lags[:, n % 2, n // 2, :], ACT.Square).then_inc(squared, 1)
            act.wait_ge(used, 8)
            link(nc.scalar.activation(hy.root, c.ps[:, 7, :], ACT.Ln, bias=EPS))
            link(nc.scalar.activation(hy.root, hy.root, ACT.Exp, scale=-0.5))


def transform(c, src, hy, finish):
    nc = c.nc
    st, sem = stage(c)
    with st, nc.Block() as block:
        product, chained = sem("product"), sem("chained")

        @block.tensor
        def _(pe):
            for f in range(4):
                for s in range(2):
                    n = 2 * f + s
                    for t in range(4):
                        last = nc.tensor.matmul(c.ps[:, n, :], hy.fwd[:, s, t, f * 128:(f + 1) * 128], src(s)[:, t, :],
                                                start=t == 0, stop=t == 3)
                    last.then_inc(product, 1)

        @block.vector
        def _(dve):
            link = chain(dve, chained)
            for f in range(4):
                dve.wait_ge(product, 2 * f + 2)
                finish(link, f, c.ps[:, 2 * f, :], c.ps[:, 2 * f + 1, :])


def inverse(c, hy, by_token, finish):
    nc = c.nc
    st, sem = stage(c)
    with st, nc.Block() as block:
        product, chained = sem("product"), sem("chained")

        @block.tensor
        def _(pe):
            for i in range(4):
                for n in range(8):
                    s, f = n // 4, n % 4
                    table, spec = hy.back[:, s, f, :], hy.spec[:, s, f, :]
                    cut = slice(i * 128, (i + 1) * 128)
                    lhs, rhs = (table[:, cut], spec) if by_token else (spec[:, cut], table)
                    last = nc.tensor.matmul(c.ps[:, i, :], lhs, rhs, start=n == 0, stop=n == 7)
                last.then_inc(product, 1)

        @block.vector
        def _(dve):
            link = chain(dve, chained)
            for i in range(4):
                dve.wait_ge(product, i + 1)
                finish(link, i, c.ps[:, i, :])


def hyena(c):
    nc = c.nc
    v = nc.vector
    hy = Hyena(c)
    u = cd_buffers(c)[7]
    block_of = lambda buf, i, j: buf[:, i, j * 128:(j + 1) * 128]
    turn_tiles(c, [(hy.v[:, t, :], [block_of(u, k, t) for k in range(4)]) for t in range(4)]
               + [(hy.x1[:, t, :], [block_of(u, 4 + k, t) for k in range(4)]) for t in range(4)],
               [(hy.x2t[:, k, :], u[:, 8 + k, :]) for k in range(4)])
    filter_features(c, hy)
    root = hy.root

    def scaled(link, f, cos, sin):
        v.tensor_tensor(hy.kern[:, 0, f, :], cos, root, ALU.mult)
        v.tensor_tensor(hy.kern[:, 1, f, :], sin, root, ALU.mult)

    def complex_product(link, f, cos, sin):
        hc, hs, t0, t1, t2 = hy.kern[:, 0, f, :], hy.kern[:, 1, f, :], hy.tmp[:, 0, :], hy.tmp[:, 1, :], hy.tmp[:, 2, :]
        v.tensor_tensor(t0, cos, hc, ALU.mult)
        link(v.tensor_tensor(t1, sin, hs, ALU.mult))
        v.tensor_tensor(hy.spec[:, 0, f, :], t0, t1, ALU.subtract)
        link(v.tensor_tensor(t2, cos, hs, ALU.mult))
        link(v.tensor_tensor(t0, sin, hc, ALU.mult))
        link(v.tensor_tensor(hy.spec[:, 1, f, :], t2, t0, ALU.add))

    def gate_tokens(link, t, conv):
        z = hy.v[:, t, :]
        link(v.tensor_tensor(z, z, hy.bias0, ALU.mult))
        link(v.tensor_tensor(z, z, conv, ALU.add))
        link(v.tensor_tensor(z, z, hy.x1[:, t, :], ALU.mult))

    def gate_features(link, k, conv):
        t0 = hy.tmp[:, 0, :]
        link(v.scalar_tensor_tensor(t0, hy.z1t[:, k, :], hy_bias_col(c, k), conv, ALU.mult, ALU.add))
        link(v.tensor_tensor(hy.out[:, 4 + k, :], t0, hy.x2t[:, k, :], ALU.mult))

    for order in range(2):
        filter_lags(c, hy, order)
        transform(c, lambda s: hy.lags[:, s], hy, scaled)
        transform(c, lambda s: hy.v, hy, complex_product)
        if order == 0:
            inverse(c, hy, True, gate_tokens)
            turn_tiles(c, [(hy.z1t[:, k, :], [block_of(hy.v, t, k) for t in range(4)]) for k in range(4)])
        else:
            inverse(c, hy, False, gate_features)


def layer_cd(c):
    with c.nc.Block() as block:
        @block.sync
        def _(sp):
            sp.wait_ge(c.tables_back, 32)
    spread_modulation(c, 1)
    norm_to_features(c, 0, range(TT))
    out, q, k, _, v, _, _, u = cd_buffers(c)
    project_features(c, "swa_q", 4, q, "rope", z=0)
    project_features(c, "swa_k", 1, k, "rope", cols=128)
    project_tokens(c, "swa_v", ht_view(c), KT, 1, 128, range(TT), lambda t, j: v[:, t, :])
    project_features(c, "hy_in", 12, u, "conv", z=0, taps=lambda t, n: hy_tap(c, t, n))
    window_attention(c)
    hyena(c)
    project_tokens(c, "cd_out", out, KT, 1, 256, range(TX), lambda t, j: mixed_rows(c)[:, t, j * 256:(j + 1) * 256])
    add_branch(c, 0, range(TX))
    feed_forward(c, 1, 0, range(TX))


def store(c):
    with c.nc.Block() as block:
        @block.sync
        def _(sp):
            sp.dma_start(c.a["out"][0].rearrange("(t p) d -> p t d", p=128), c.x).then_inc(c.stored, 16)
            sp.wait_ge(c.stored, 16)


def build_program(nc, a):
    with ExitStack() as ctx:
        c = Core(nc, a, ctx)
        plan_all(c)
        load_inputs(c)
        modulation(c, 0)
        layer_ab(c)
        layer_cd(c)
        store(c)


_INS = ("x", "c", "ctx", "c_ctx", "w_mod", "b_mod", "norm_g", "ffn_w_up", "ffn_conv", "ffn_w_down", "ab_w_in",
        "ab_w_out", "gdn_conv", "gdn_a_log", "gdn_dt_bias", "gdn_norm_g", "diff_lambda", "diff_norm_g", "cd_w_in",
        "cd_w_out", "swa_sink", "hy_conv", "hy_w1", "hy_b1", "hy_w2", "hy_b2", "hy_w3", "hy_freq", "hy_bias")


def kernel(**inputs):
    import concourse.bacc as bacc
    from concourse.bass_utils import run_bass_kernel_spmd

    nc = bacc.Bacc("TRN2", target_bir_lowering=False, num_devices=1)
    arrays = {f"in_{name}": np.ascontiguousarray(inputs[name]) for name in _INS}
    arrays["in_c_ctx"] = arrays["in_c_ctx"].reshape(1, D)
    arrays.update({f"in_{name}": table for name, table in constant_tables().items()})
    a = {name[3:]: nc.dram_tensor(name, v.shape, mybir.dt.from_np(v.dtype), kind="ExternalInput").ap()
         for name, v in arrays.items()}
    a["out"] = nc.dram_tensor("out", (1, N_X, D), F32, kind="ExternalOutput").ap()
    build_program(nc, a)
    r = run_bass_kernel_spmd(nc, [arrays], core_ids=[0])
    return r.results[0]["out"]
```

```python
import math
from contextlib import ExitStack

import numpy as np

import concourse.bass as bass
from concourse import mybir

F32 = mybir.dt.float32
ALU = mybir.AluOpType
ACT = mybir.ActivationFunctionType
AX = mybir.AxisListType

D = 1024
KT = D // 128
N_X, N_Z = 512, 256
N_ALL = N_X + N_Z
TX, TZ = N_X // 128, N_Z // 128
TT = TX + TZ
D_FF = 2816
FT = D_FF // 128
EPS = 1e-6
HEAD = 64
CHUNK = 64
GH = 8
PAIRS = GH // 2
GW = 512
CX, CZ = N_X // CHUNK, N_Z // CHUNK
STEPS = CX + CZ
NEG = -1e30
LAM_INIT = 0.2
N_FREQ = 512
RING = 4
SLOT = 2048
LEVELS = (1, 2, 4, 8, 16, 32)

_TABLE = {}
_at = 0
for _name, _n in (("ident", 128), ("rot", 128), ("heads", 128), ("ones", 128), ("cos", 512), ("sin", 512),
                  ("tri", 128), ("tri2", 256), ("mask_a", 128), ("mask_q", 128), ("m1", 128), ("mt", 768),
                  ("eye", 64), ("win_l", 128), ("win_r", 128), ("pick", 32), ("row_of", 256), ("nonzero", 1),
                  ("feats", 512)):
    _TABLE[_name] = (_at, _n)
    _at += _n
TABLE_COLS = _at


def constant_tables():
    f = np.float32
    t = np.zeros((128, TABLE_COLS), f)

    def put(name, a, rows=128):
        o, n = _TABLE[name]
        t[:rows, o:o + n] = np.asarray(a, f).reshape(rows, n)

    put("ident", np.eye(128))
    rot = np.zeros((128, 128))
    for d in range(128):
        if d % 32 < 16:
            rot[d + 16, d] = -1
        else:
            rot[d - 16, d] = 1
    put("rot", rot)
    put("heads", np.kron(np.eye(2), np.ones((64, 64))))
    put("ones", np.ones((128, 128)))
    inv = (f(10000.0) ** (-np.arange(0, 32, 2, dtype=f) / f(32))).astype(f)
    tok = np.arange(N_X)
    ang = np.zeros((128, N_X), f)
    for d in range(128):
        pos = (tok // 64 if d % 64 < 32 else tok % 64).astype(f)
        ang[d] = pos * inv[d % 16]
    put("cos", np.cos(ang))
    put("sin", np.sin(ang))
    i, j = np.arange(64)[:, None], np.arange(64)[None, :]
    both = lambda a: np.tile(a, (2, 1))
    two = lambda fwd, bwd: both(np.concatenate([fwd, bwd], axis=1))
    put("tri", two(i <= j, i >= j))
    put("tri2", np.concatenate([np.kron(np.eye(2), i <= j), np.kron(np.eye(2), i >= j)], axis=1))
    put("mask_a", two(np.where(i > j, 0, NEG), np.where(i < j, 0, NEG)))
    put("mask_q", two(np.where(i <= j, 0, NEG), np.where(i >= j, 0, NEG)))
    level = lambda b: (i // (2 * b) == j // (2 * b)) & ((i // b) % 2 == 1) & ((j // b) % 2 == 0)
    put("m1", two(level(1), level(1).T))
    put("mt", np.concatenate([two(level(b).T, level(b)) for b in LEVELS], axis=1))
    put("eye", both(np.eye(64)))
    q, m = np.arange(128)[:, None], np.arange(128)[None, :]
    put("win_l", np.where(m >= q, 0, NEG))
    put("win_r", np.where(m <= q, 0, NEG))
    pick = np.zeros((32, 2, 2, 2, PAIRS))
    for direction in range(2):
        for hh in range(2):
            for what in range(2):
                for p in range(PAIRS):
                    pick[what * 16 + direction * 8 + 2 * p + hh, direction, hh, what, p] = 1
    put("pick", pick, 32)
    row_of = np.zeros((4, 32, 2, 128))
    row_of[:, 0, 0] = row_of[:, 1, 1] = 1
    put("row_of", row_of)
    nz = np.ones(128)
    nz[0] = 0
    put("nonzero", nz)
    n = N_X
    pos = np.arange(n, dtype=f)
    tt = pos / f(n - 1)
    fa = (f(2.0 * math.pi) * pos / f(n))[:, None] * np.linspace(1e-4, 15, 16, dtype=f)[None, :]
    feats = np.concatenate([tt[:, None], np.cos(fa), -np.sin(fa)], axis=-1)
    by_parity = np.concatenate([np.arange(0, n, 2), np.arange(1, n, 2)])
    put("feats", feats[by_parity].T, 33)
    lo, hi = math.log(1e-2) / 1.5, math.log(1e-2) / 0.3
    decay = np.exp(-tt[:, None] * np.abs(np.linspace(lo, hi, 512, dtype=f))[None, :]).astype(f)
    w = 2 * np.pi * (np.arange(N_FREQ // 2) + 0.5) / (2 * N_FREQ)
    ph = by_parity[:, None] * w[None, :]
    fwd = np.stack([np.cos(ph), np.sin(ph)]).astype(f)
    back = (np.stack([np.cos(ph.T), np.sin(ph.T)]) / N_FREQ).astype(f)
    return {"t_table": t, "t_decay": decay[by_parity], "t_fwd": fwd, "t_back": back}


class Core:

    def __init__(self, nc, a, ctx):
        self.nc, self.a, self.ctx = nc, a, ctx
        self.at = 0
        self.mem = ctx.enter_context(nc.sbuf_tensor("mem", [128, 53200], F32))
        self.ps = ctx.enter_context(nc.psum_tensor("banks", [128, 8, 512], F32))
        self.table, self.tab = self.room(TABLE_COLS), {}
        for name, (o, n) in _TABLE.items():
            self.tab[name] = self.table[:, o:o + n]
        self.x = self.room(TX * D).rearrange("p (t d) -> p t d", d=D)
        self.z = self.room(TZ * D).rearrange("p (t d) -> p t d", d=D)
        self.cols = self.room(512).rearrange("p (j c) -> p j c", j=4)
        self.sc = self.room(16).rearrange("p (k u) -> p k u", u=2)
        self.modc = self.room(64).rearrange("p (v k u) -> p v k u", v=4, u=2)
        self.coef = self.room(64).rearrange("p (m v u k) -> p m v u k", m=2, v=2, u=2)
        self.stat = self.room(256)
        self.gates = self.room(4 * D).rearrange("p (v u d) -> p v u d", v=2, u=2)
        self.ht = self.room(KT * N_ALL)
        self.ring = self.room(RING * SLOT)
        self.small = self.room(12 * 96 + 16)
        self.arena = self.mem[:, self.at:53200]
        self.arena_size = 53200 - self.at
        self.loads, self.range_of, self.issued = [], {}, 0
        self.slot_in = [ctx.enter_context(nc.semaphore(f"weights_in_{i}")) for i in range(RING)]
        self.tables_back = ctx.enter_context(nc.semaphore("tables_back"))
        self.stored = ctx.enter_context(nc.semaphore("stored"))
        self.stage_n, self.spent = 0, []

    def room(self, n):
        self.at += n
        return self.mem[:, self.at - n:self.at]

    def plan(self, name, views):
        self.range_of[name] = (len(self.loads), len(self.loads) + len(views))
        self.loads += views

    def slot(self, n, k, cols):
        o = (n % RING) * SLOT
        return self.ring[:, o:o + k * cols].rearrange("p (k n) -> p k n", k=k)

    def issue(self, sp, stage, freed, ahead=RING):
        lo, hi = self.range_of[stage]
        for n in range(self.issued, min(hi + ahead, len(self.loads))):
            if n - RING >= lo:
                sp.wait_ge(*freed(n - RING - lo))
            src = self.loads[n]
            sp.dma_start(self.slot(n, src.shape[1], src.shape[2]), src).then_inc(self.slot_in[n % RING], 16)
            self.issued = n + 1

    def prefetch(self, sp, stage):
        lo = self.range_of[stage][0]
        for n in range(lo, lo + RING):
            src = self.loads[n]
            sp.dma_start(self.slot(n, src.shape[1], src.shape[2]), src).then_inc(self.slot_in[n % RING], 16)
            self.issued = n + 1

    def arrived(self, pe, n):
        pe.wait_ge(self.slot_in[n % RING], 16 * (n // RING + 1))


def chain(eng, sem):
    count = [0]

    def link(ins):
        count[0] += 1
        ins.then_inc(sem, 1)
        eng.wait_ge(sem, count[0])
    return link


def stage(c):
    c.stage_n += 1
    n = c.stage_n
    if len(c.spent) > 100:
        c.nc.clear_and_free_semaphores(c.spent)
        c.nc.all_engine_barrier()
        c.spent = []

    def sem(name):
        c.spent.append(c.nc.alloc_semaphore(f"{name}_{n}"))
        return c.spent[-1]
    return ExitStack(), sem


def rows_of(ap):
    return ap.rearrange("(u c) -> u c", c=128)


def load_inputs(c):
    nc, a = c.nc, c.a
    st, sem = stage(c)
    rows = c.arena[:, 0:512].rearrange("p (j c) -> p j c", j=4)
    taps = [a["ffn_conv"][l].rearrange("t (u c) -> t u c", c=128) for l in range(2)]
    batches = [
        [a["norm_g"].rearrange("l g (k c) -> (l g k) c", c=128), rows_of(a["c"][0]), rows_of(a["c_ctx"][0]),
         a["gdn_conv"][0].rearrange("t (u c) -> (t u) c", c=128)],
        [taps[0][0], taps[0][1], a["hy_conv"][0].rearrange("t (u c) -> (t u) c", c=128)],
        [taps[0][2], taps[1][0], rows_of(a["hy_bias"][0, 1])],
        [taps[1][1], taps[1][2]],
    ]
    sizes = [sum(v.shape[0] for v in b) for b in batches]
    with st, nc.Block() as block:
        table_in, rows_in, x_in, z_in = sem("table_in"), sem("rows_in"), sem("x_in"), sem("z_in")
        turned, columns = sem("turned"), sem("columns")
        n_rows = sum(len(b) for b in batches)

        @block.sync
        def _(sp):
            sp.dma_start(c.table, a["t_table"]).then_inc(table_in, 16)
            for j, views in enumerate(batches):
                r = 0
                for v in views:
                    sp.dma_start(rows[r:r + v.shape[0], j, :], v).then_inc(rows_in, 16)
                    r += v.shape[0]
            c.issue(sp, "start", None)

        @block.scalar
        def _(act):
            act.dma_start(c.x, a["x"][0].rearrange("(t p) d -> p t d", p=128)).then_inc(x_in, 16)
            act.dma_start(c.z, a["ctx"][0].rearrange("(t p) d -> p t d", p=128)).then_inc(z_in, 16)
            act.wait_ge(columns, 4)
            nc.scalar.activation(c.sc.rearrange("p k u -> p u k"),
                                 c.cols[:, 0, 64:80].rearrange("p (u k) -> p u k", u=2), ACT.Silu)
            act.wait_ge(x_in, 16)
            act.wait_ge(z_in, 16)

        @block.tensor
        def _(pe):
            pe.wait_ge(table_in, 16)
            pe.wait_ge(rows_in, 16 * n_rows)
            for j, n in enumerate(sizes):
                last = nc.tensor.transpose(c.ps[:, j, 0:n], rows[0:n, j, :], c.tab["ident"][0:n, 0:n])
                last.then_inc(turned, 1)

        @block.vector
        def _(dve):
            for j, n in enumerate(sizes):
                dve.wait_ge(turned, j + 1)
                nc.vector.tensor_copy(c.cols[:, j, 0:n], c.ps[:, j, 0:n]).then_inc(columns, 1)


def norm_col(c, l, g):
    o = (l * 4 + g) * 8
    return c.cols[:, 0, o:o + 8]


def gdn_tap(c, t, tile):
    return c.cols[:, 0, 80 + 12 * t + tile:81 + 12 * t + tile]


def hy_tap(c, t, tile):
    return c.cols[:, 1, 88 + 12 * t + tile:89 + 12 * t + tile]


def hy_bias_col(c, tile):
    return c.cols[:, 2, 88 + tile:89 + tile]


def ffn_tap(c, l, t, tile):
    j, o = {(0, 0): (1, 0), (0, 1): (1, 44), (0, 2): (2, 0), (1, 0): (2, 44), (1, 1): (3, 0), (1, 2): (3, 44)}[l, t]
    return c.cols[:, j, o + tile:o + tile + 1]


class Modulation:

    LOADS = 6 * 4

    def __init__(self, c, l):
        self.c, self.l = c, l
        o = c.arena_size - 3072
        self.mod, self.bias = c.arena[:, o:o + 1536], c.arena[:, o + 1536:o + 3072]
        self.gain = c.small[:, 0:512]
        self.weights = c.arena[:, o - 2048:o].rearrange("p (k n) -> p k n", k=2)

    def load_rows(self, eng, rows_in):
        a, l = self.c.a, self.l
        for g in range(4):
            for r in range(2):
                p = slice(32 * g + r, 32 * g + r + 1)
                eng.dma_start(self.bias[p, :].rearrange("p (i n) -> p i n", i=6),
                              a["b_mod"][l:l + 1, :].rearrange("a (i g n) -> a i g n", i=6, g=4)[:, :, g, :])\
                    .then_inc(rows_in, 16)
                for w in range(2):
                    eng.dma_start(self.gain[p, 256 * w:256 * w + 256],
                                  a["norm_g"][l, 1 + 2 * w:2 + 2 * w, 256 * g:256 * g + 256]).then_inc(rows_in, 16)

    ROWS_IN = 16 * 24

    def product(self, n, w, bank):
        c = self.c
        for kk in range(2):
            k = 2 * (n % 4) + kk
            for g in range(4):
                last = c.nc.tensor.matmul(c.ps[32 * g:32 * g + 2, bank, 0:256], c.sc[:, k, :],
                                          w[:, kk, 256 * g:256 * g + 256], start=k == 0, stop=k == KT - 1)
        return last

    def drain(self, i, bank):
        c = self.c
        for g in range(4):
            p = slice(32 * g, 32 * g + 2)
            last = c.nc.vector.tensor_tensor(self.mod[p, 256 * i:256 * i + 256], c.ps[p, bank, 0:256],
                                             self.bias[p, 256 * i:256 * i + 256], ALU.add)
        return last


def modulation(c, l):
    st, sem = stage(c)
    m = Modulation(c, l)
    name = f"mod{l}"
    lo, _ = c.range_of[name]
    with st, c.nc.Block() as block:
        rows_in, product, drained = sem("rows_in"), sem("product"), sem("drained")

        @block.sync
        def _(sp):
            c.issue(sp, name, lambda j: (product, j + 1))

        @block.scalar
        def _(act):
            m.load_rows(act, rows_in)

        @block.tensor
        def _(pe):
            for n in range(m.LOADS):
                if n % 4 == 0 and n >= 8:
                    pe.wait_ge(drained, n // 4 - 1)
                c.arrived(pe, lo + n)
                m.product(n, c.slot(lo + n, 2, D), n // 4 % 2).then_inc(product, 1)

        @block.vector
        def _(dve):
            dve.wait_ge(rows_in, m.ROWS_IN)
            for i in range(6):
                dve.wait_ge(product, 4 * (i + 1))
                m.drain(i, i % 2).then_inc(drained, 1)


def spread_modulation(c, l):
    nc = c.nc
    st, sem = stage(c)
    m = Modulation(c, l)
    mod, gain = m.mod, m.gain
    columns_of = (0, 1, 3, 4)
    with st, nc.Block() as block:
        gate_rows, turned, columns = sem("gate_rows"), sem("turned"), sem("columns")
        gate, spread_dve, spread_act, act_chain = sem("gate"), sem("spread_dve"), sem("spread_act"), sem("act_chain")

        @block.tensor
        def _(pe):
            for w, i in enumerate(columns_of):
                for k in range(KT):
                    g, kk = k // 2, k % 2
                    p = slice(32 * g, 32 * g + 2)
                    last = nc.tensor.matmul(c.ps[:, 4 + g, 4 * w + 2 * kk:4 * w + 2 * kk + 2],
                                            mod[p, 256 * i + 128 * kk:256 * i + 128 * kk + 128],
                                            c.tab["ident"][p, p], start=True, stop=True)
            last.then_inc(turned, 1)
            pe.wait_ge(gate_rows, 8)
            for n in range(4):
                w, r = n // 2, n % 2
                if n == 1:
                    pe.wait_ge(columns, 4)
                elif n >= 2:
                    pe.wait_ge(spread_dve, 2 * (n - 1))
                    pe.wait_ge(spread_act, 2 * (n - 1))
                for g in range(4):
                    p = slice(32 * g, 32 * g + 2)
                    last = nc.tensor.matmul(c.ps[:, 4 * (n % 2) + g, 0:256], c.tab["row_of"][p, r * 128:(r + 1) * 128],
                                            mod[p, 256 * (2, 5)[w]:256 * (2, 5)[w] + 256], start=True, stop=True)
                last.then_inc(gate, 1)

        @block.vector
        def _(dve):
            for w, i in enumerate((2, 5)):
                for g in range(4):
                    p = slice(32 * g, 32 * g + 2)
                    nc.vector.tensor_tensor(mod[p, 256 * i:256 * i + 256], mod[p, 256 * i:256 * i + 256],
                                            gain[p, 256 * w:256 * w + 256], ALU.mult).then_inc(gate_rows, 1)
            dve.wait_ge(turned, 1)
            for g in range(4):
                nc.vector.tensor_copy(c.modc[:, :, 2 * g:2 * g + 2, :],
                                      c.ps[:, 4 + g, 0:16].rearrange("p (v k u) -> p v k u", v=4, k=2)).then_inc(columns, 1)
            dve.wait_ge(columns, 4)
            for m_ in range(2):
                for r in range(2):
                    nc.vector.scalar_tensor_tensor(c.coef[:, m_, 0, r, :], c.modc[:, 2 * m_ + 1, :, r], 1.0,
                                                   norm_col(c, l, 2 * m_), ALU.add, ALU.mult)
                    nc.vector.tensor_copy(c.coef[:, m_, 1, r, :], c.modc[:, 2 * m_, :, r])
            for n in range(4):
                w, r = n // 2, n % 2
                dve.wait_ge(gate, n + 1)
                for g in range(2):
                    nc.vector.tensor_copy(c.gates[:, w, r, 256 * g:256 * g + 256],
                                          c.ps[:, 4 * (n % 2) + g, 0:256]).then_inc(spread_dve, 1)

        @block.scalar
        def _(act):
            link = chain(act, act_chain)
            if l == 0:
                for t in range(TT):
                    link(nc.scalar.activation(c.arena[:, 0:D], token_tile(c, t), ACT.Square,
                                              accum_out=norm_squares(c)[:, t:t + 1]))
            for n in range(4):
                w, r = n // 2, n % 2
                act.wait_ge(gate, n + 1)
                for g in range(2, 4):
                    nc.scalar.activation(c.gates[:, w, r, 256 * g:256 * g + 256],
                                         c.ps[:, 4 * (n % 2) + g, 0:256], ACT.Copy).then_inc(spread_act, 1)


def ht_view(c):
    return c.ht.rearrange("p (k t) -> p k t", k=KT)


def token_tile(c, t):
    return c.x[:, t, :] if t < TX else c.z[:, t - TX, :]


def norm_to_features(c, m, tiles):
    nc = c.nc
    st, sem = stage(c)
    y = c.arena[:, D:3 * D].rearrange("p (b d) -> p b d", b=2)
    rstd = c.stat[:, 0:TT]
    ht = ht_view(c)
    with st, nc.Block() as block:
        act_chain, stats, scaled = sem("act_chain"), sem("stats"), sem("scaled")
        turned, act_out, dve_out = sem("turned"), sem("act_out"), sem("dve_out")

        @block.scalar
        def _(act):
            link = chain(act, act_chain)
            n = len(tiles)
            link(nc.scalar.activation(rstd[:, 0:n], norm_squares(c)[:, 0:n], ACT.Ln, bias=EPS, scale=1.0 / D))
            nc.scalar.activation(rstd[:, 0:n], rstd[:, 0:n], ACT.Exp, scale=-0.5).then_inc(stats, 1)
            for t in tiles:
                act.wait_ge(turned, 2 * t + 1)
                r = int(t >= TX)
                for k in range(4):
                    nc.scalar.activation(ht[:, k, t * 128:(t + 1) * 128], c.ps[:, (t % 4) * 2, k * 128:(k + 1) * 128],
                                         ACT.Identity, scale=c.coef[:, m, 0, r, k:k + 1],
                                         bias=c.coef[:, m, 1, r, k:k + 1]).then_inc(act_out, 1)

        @block.vector
        def _(dve):
            dve.wait_ge(stats, 1)
            for i in range(len(tiles) + 1):
                if i < len(tiles):
                    if i >= 2:
                        dve.wait_ge(turned, 2 * (i - 1))
                    nc.vector.tensor_scalar(y[:, i % 2, :], token_tile(c, tiles[i]), rstd[:, i:i + 1], None,
                                            ALU.mult).then_inc(scaled, 1)
                if i:
                    t = tiles[i - 1]
                    r = int(t >= TX)
                    dve.wait_ge(turned, 2 * i)
                    for k in range(4, KT):
                        nc.vector.tensor_scalar(ht[:, k, t * 128:(t + 1) * 128],
                                                c.ps[:, (t % 4) * 2 + 1, (k - 4) * 128:(k - 3) * 128],
                                                c.coef[:, m, 0, r, k:k + 1], c.coef[:, m, 1, r, k:k + 1],
                                                ALU.mult, ALU.add).then_inc(dve_out, 1)

        @block.tensor
        def _(pe):
            for t in tiles:
                if t >= 4:
                    pe.wait_ge(act_out, 4 * (t - 3))
                    pe.wait_ge(dve_out, 4 * (t - 3))
                pe.wait_ge(scaled, t + 1)
                for k in range(KT):
                    last = nc.tensor.transpose(c.ps[:, (t % 4) * 2 + k // 4, (k % 4) * 128:(k % 4 + 1) * 128],
                                               y[:, t % 2, k * 128:(k + 1) * 128], c.tab["ident"])
                    if k % 4 == 3:
                        last.then_inc(turned, 1)


def plan_all(c):
    a = c.a
    ktiles = lambda w: w.rearrange("(k p) n -> p k n", p=128)
    chunks = lambda w, n=256: [ktiles(w)[:, :, i:i + n] for i in range(0, w.shape[1], n)]
    down = lambda w: [ktiles(w)[:, h * 11:(h + 1) * 11, i:i + 128] for i in range(0, D, 128) for h in range(2)]

    def up(w):
        both = chunks(w)
        return [both[i] for j in range(11) for i in (j, 11 + j)]

    mods = lambda w: [ktiles(w)[:, k:k + 2, i * D:(i + 1) * D] for i in range(6) for k in range(0, KT, 2)]
    c.range_of["start"] = (0, 0)
    ab, cd = a["ab_w_in"][0], a["cd_w_in"][0]
    c.plan("mod0", mods(a["w_mod"][0]))
    c.plan("diff_qk", chunks(ab[:, 2080:3104]))
    c.plan("diff_v", chunks(ab[:, 3104:3616]))
    c.plan("gdn_gates", chunks(ab[:, 2048:2080], 32))
    c.plan("gdn_gate", chunks(ab[:, 1536:2048]))
    c.plan("gdn_qkv", chunks(ab[:, 0:1536]))
    c.plan("ab_out", chunks(a["ab_w_out"][0]))
    c.plan("up0", up(a["ffn_w_up"][0]))
    c.plan("down0", down(a["ffn_w_down"][0]))
    c.plan("swa_q", chunks(cd[:, 0:512]))
    c.plan("swa_k", chunks(cd[:, 512:640], 128))
    c.plan("swa_v", chunks(cd[:, 640:768], 128))
    c.plan("hy_in", chunks(cd[:, 768:2304]))
    c.plan("cd_out", chunks(a["cd_w_out"][0]))
    c.plan("up1", up(a["ffn_w_up"][1]))
    c.plan("down1", down(a["ffn_w_down"][1]))


def project_features(c, name, n_tiles, dst, kind, z=N_Z, taps=None, cols=256, ahead=RING):
    nc = c.nc
    st, sem = stage(c)
    lo, _ = c.range_of[name]
    ht = ht_view(c)
    per = cols // 128
    slots = 3
    work = c.arena[:, c.arena_size - 3072:].rearrange("p (n b t) -> p n b t", n=3, b=2)
    raw, turned_cos, turned_sin = work[:, 0], work[:, 1], work[:, 2]
    conv = kind.startswith("conv")
    per_tile = 2 if z else 1
    with st, nc.Block() as block:
        product, drained, done, last_out = sem("product"), sem("drained"), sem("done"), sem("last_out")
        rotated, dve_chain = sem("rotated"), sem("dve_chain")

        @block.sync
        def _(sp):
            c.issue(sp, name, lambda j: (product, per * (j + 1)), ahead)

        @block.tensor
        def _(pe):
            def rotate(n):
                pe.wait_ge(drained, per_tile * n + 1)
                if n >= 2:
                    pe.wait_ge(done, n - 1)
                nc.tensor.matmul(c.ps[:, 6 + n % 2, :], c.tab["rot"], raw[:, n % 2, :],
                                 start=True, stop=True).then_inc(rotated, 1)

            for n in range(n_tiles):
                if n >= slots:
                    pe.wait_ge(drained, per_tile * (n - slots + 1))
                    if conv:
                        pe.wait_ge(done, n - slots + 1)
                if n % per == 0:
                    c.arrived(pe, lo + n // per)
                w = c.slot(lo + n // per, KT, cols)[:, :, n % per * 128:n % per * 128 + 128]
                for k in range(KT):
                    last = nc.tensor.matmul(c.ps[:, 2 * (n % slots), :], w[:, k, :], ht[:, k, 0:N_X],
                                            start=k == 0, stop=k == KT - 1)
                    if z:
                        last = nc.tensor.matmul(c.ps[:, 2 * (n % slots) + 1, 0:z], w[:, k, :],
                                                ht[:, k, N_X:N_X + z], start=k == 0, stop=k == KT - 1)
                last.then_inc(product, 1)
                if kind == "rope" and n:
                    rotate(n - 1)
            if kind == "rope":
                rotate(n_tiles - 1)

        @block.scalar
        def _(act):
            def finish(n):
                act.wait_ge(done, n + 1)
                nc.scalar.activation(dst[:, n, :], dst[:, n, :], ACT.Silu).then_inc(last_out, 1)

            for n in range(n_tiles):
                act.wait_ge(product, n + 1)
                px, pz = c.ps[:, 2 * (n % slots), :], c.ps[:, 2 * (n % slots) + 1, 0:z]
                if kind == "rope":
                    if n >= 2:
                        act.wait_ge(done, n - 1)
                    nc.scalar.activation(raw[:, n % 2, :], px, ACT.Copy).then_inc(drained, 1)
                elif conv:
                    nc.scalar.activation(dst[:, n, 0:N_X], px, ACT.Identity, scale=taps(1, n)).then_inc(drained, 1)
                else:
                    nc.scalar.activation(dst[:, n, 0:N_X], px, ACT.Silu if kind == "silu" else ACT.Copy)\
                        .then_inc(drained, 1)
                if z:
                    if conv:
                        nc.scalar.activation(dst[:, n, N_X:N_X + z], pz, ACT.Identity,
                                             scale=taps(1, n)).then_inc(drained, 1)
                    else:
                        nc.scalar.activation(dst[:, n, N_X:N_X + z], pz, ACT.Silu if kind == "silu" else ACT.Copy)\
                            .then_inc(drained, 1)
                if kind == "conv_silu" and n:
                    finish(n - 1)
            if kind == "conv_silu":
                finish(n_tiles - 1)

        @block.vector
        def _(dve):
            link = chain(dve, dve_chain)
            for n in range(n_tiles):
                if kind == "rope":
                    dve.wait_ge(drained, per_tile * n + 1)
                    nc.vector.tensor_tensor(turned_cos[:, n % 2, :], raw[:, n % 2, :], c.tab["cos"], ALU.mult)
                    dve.wait_ge(rotated, n + 1)
                    link(nc.vector.tensor_tensor(turned_sin[:, n % 2, :], c.ps[:, 6 + n % 2, :], c.tab["sin"], ALU.mult))
                    nc.vector.tensor_tensor(dst[:, n, 0:N_X], turned_cos[:, n % 2, :], turned_sin[:, n % 2, :],
                                            ALU.add).then_inc(done, 1)
                elif conv:
                    dve.wait_ge(drained, per_tile * (n + 1))
                    convolve(c, link, dst[:, n, :], c.ps[:, 2 * (n % slots), :], c.ps[:, 2 * (n % slots) + 1, :], z,
                             lambda t: taps(t, n)).then_inc(done, 1)


def convolve(c, link, y, px, pz, z, tap):
    v = c.nc.vector
    parts = [(y[:, 0:N_X], px, N_X)] + ([(y[:, N_X:N_X + z], pz, z)] if z else [])
    for out, src, n in parts:
        step = v.scalar_tensor_tensor(out[:, 1:n], src[:, 0:n - 1], tap(0), out[:, 1:n], ALU.mult, ALU.add)
        if n == parts[-1][2]:
            link(step)
    for out, src, n in parts:
        step = v.scalar_tensor_tensor(out[:, 0:n - 1], src[:, 1:n], tap(2), out[:, 0:n - 1], ALU.mult, ALU.add)
    return step


def project_tokens(c, name, src, k_tiles, loads_per, cols, tiles, dst, mod_layer=None, squares=False):
    nc = c.nc
    st, sem = stage(c)
    lo, hi = c.range_of[name]
    n_chunks = (hi - lo) // loads_per
    k_per = k_tiles // loads_per
    side = mod_layer is not None
    n_banks = 6 if side else 8
    units = [(j, t) for j in range(n_chunks) for t in tiles]
    m = Modulation(c, mod_layer)
    assert not side or m.LOADS == len(units) // 2
    with st, nc.Block() as block:
        product, act_out, dve_out = sem("product"), sem("act_out"), sem("dve_out")
        mod_in, mod_used, mod_drained, rows_in = sem("mod_in"), sem("mod_used"), sem("mod_drained"), sem("rows_in")
        act_chain = sem("act_chain")

        @block.sync
        def _(sp):
            c.issue(sp, name, lambda j: (product, len(tiles) * (j // loads_per + 1)))

        if side:
            @block.gpsimd
            def _(pool):
                weights = c.a["w_mod"][mod_layer].rearrange("(k p) n -> p k n", p=128)
                for q in range(m.LOADS):
                    if q:
                        pool.wait_ge(mod_used, q)
                    k, i = 2 * (q % 4), q // 4
                    pool.dma_start(m.weights, weights[:, k:k + 2, i * D:(i + 1) * D]).then_inc(mod_in, 16)

        @block.tensor
        def _(pe):
            for n, (j, t) in enumerate(units):
                if n >= n_banks:
                    pe.wait_ge(dve_out if n % 2 else act_out, (n - n_banks) // 2 + 1)
                if t == tiles[0]:
                    for i in range(loads_per):
                        c.arrived(pe, lo + j * loads_per + i)
                for k in range(k_tiles):
                    w = c.slot(lo + j * loads_per + k // k_per, k_per, cols)[:, k % k_per, :]
                    last = nc.tensor.matmul(c.ps[:, n % n_banks, 0:cols], src[:, k, t * 128:(t + 1) * 128], w,
                                            start=k == 0, stop=k == k_tiles - 1)
                last.then_inc(product, 1)
                if side and n % 2:
                    q = n // 2
                    if q % 4 == 0 and q >= 8:
                        pe.wait_ge(mod_drained, q // 4 - 1)
                    pe.wait_ge(mod_in, 16 * (q + 1))
                    m.product(q, m.weights, 6 + q // 4 % 2).then_inc(mod_used, 1)

        @block.scalar
        def _(act):
            link = chain(act, act_chain)
            junk = c.small[:, 512:512 + cols]
            if side:
                m.load_rows(act, rows_in)

            def square(n):
                j, t = units[n]
                act.wait_ge(dve_out if n % 2 else act_out, n // 2 + 1)
                link(nc.scalar.activation(junk, dst(t, j), ACT.Square,
                                          accum_out=branch_squares(c, n_chunks)[:, t, j:j + 1]))

            for n, (j, t) in enumerate(units):
                if n % 2 == 0:
                    act.wait_ge(product, n + 1)
                    nc.scalar.activation(dst(t, j), c.ps[:, n % n_banks, 0:cols], ACT.Copy).then_inc(act_out, 1)
                if squares and n:
                    square(n - 1)
            if squares:
                square(len(units) - 1)

        @block.vector
        def _(dve):
            for n, (j, t) in enumerate(units):
                if n % 2 == 1:
                    dve.wait_ge(product, n + 1)
                    nc.vector.tensor_copy(dst(t, j), c.ps[:, n % n_banks, 0:cols]).then_inc(dve_out, 1)
                if side and n % 8 == 7:
                    part = n // 8
                    if part == 0:
                        dve.wait_ge(rows_in, m.ROWS_IN)
                    dve.wait_ge(mod_used, 4 * (part + 1))
                    m.drain(part, 6 + part % 2).then_inc(mod_drained, 1)


def outc(c):
    return c.arena[:, 0:KT * N_ALL].rearrange("p (k t) -> p k t", k=KT)


def diff_buffers(c):
    o = KT * N_ALL
    qk = c.arena[:, o:o + 8 * N_ALL].rearrange("p (k t) -> p k t", k=8)
    v = c.arena[:, o + 8 * N_ALL:o + 8 * N_ALL + TT * 512].rearrange("p (t e) -> p t e", t=TT)
    return qk, v, o + 8 * N_ALL + TT * 512


def lambda_value(c):
    nc, a = c.nc, c.a
    st, sem = stage(c)
    lam = c.small[:, 0:256].rearrange("p (u d) -> p u d", u=4)
    prod = c.small[:, 256:384].rearrange("p (u d) -> p u d", u=2)
    dots = c.stat[:, 200:202]
    with st, nc.Block() as block:
        rows_in, multiplied, summed, exps, link_sem = (sem(n) for n in ("rows_in", "multiplied", "summed", "exps", "link"))

        @block.sync
        def _(sp):
            sp.dma_start(lam, a["diff_lambda"][0].partition_broadcast(128)).then_inc(rows_in, 16)
            sp.dma_start(c.stat[:, 204:205], a["diff_norm_g"][0].unsqueeze(1)).then_inc(rows_in, 16)

        @block.vector
        def _(dve):
            link = chain(dve, link_sem)
            dve.wait_ge(rows_in, 32)
            link(nc.vector.tensor_tensor(prod, lam[:, 0:4:2, :], lam[:, 1:4:2, :], ALU.mult))
            nc.vector.tensor_reduce(dots, prod, AX.X, ALU.add).then_inc(summed, 1)
            dve.wait_ge(exps, 1)
            link(nc.vector.tensor_tensor(c.stat[:, 203:204], dots[:, 1:2], dots[:, 0:1], ALU.subtract))
            link(nc.vector.tensor_scalar(c.stat[:, 203:204], c.stat[:, 203:204], -LAM_INIT, None, ALU.add))
            link(nc.vector.tensor_scalar(c.stat[:, 204:205], c.stat[:, 204:205], 1.0 - LAM_INIT, None, ALU.mult))

        @block.scalar
        def _(act):
            act.wait_ge(summed, 1)
            nc.scalar.activation(dots, dots, ACT.Exp).then_inc(exps, 1)


def diff_attention(c):
    nc = c.nc
    st, sem = stage(c)
    qk, v, o = diff_buffers(c)
    out = outc(c)
    prob = c.arena[:, o:o + 6 * N_ALL].rearrange("p (b s m) -> p b s m", b=3, s=2)
    o += 6 * N_ALL
    turned = c.arena[:, o:o + 2 * N_ALL].rearrange("p (b m) -> p b m", b=2)
    raw = out[:, 0:4, :]
    by_unit = raw.rearrange("p k t -> p (k t)").rearrange("p (n e) -> p n e", e=128)
    top, neg, total, lam = (c.stat[:, i * 4:i * 4 + 4].rearrange("p (b s) -> p b s", b=2) for i in range(4))
    rstd = c.stat[:, 16:16 + 4 * TT]
    junk = c.small[:, 0:128]
    units = [(q, h, 0) for h in range(4) for q in range(TX)] + [(q, h, N_X) for h in range(4) for q in (TX, TX + 1)]
    n_units = len(units)
    place = lambda u: units[u][1] * TT + units[u][0]
    scale = HEAD ** -0.5
    flat = c.ps.rearrange("p b n -> p (b n)")
    score = lambda s: flat[:, s * 1024:s * 1024 + N_ALL]
    turn = flat[:, 2048:2048 + N_ALL]
    with st, nc.Block() as block:
        scored, maxed, exped, weighed = sem("scored"), sem("maxed"), sem("exped"), sem("weighed")
        turned_ps, turned_sb, valued, kept = sem("turned_ps"), sem("turned_sb"), sem("valued"), sem("kept")
        rooted, normed, back, written = sem("rooted"), sem("normed"), sem("back"), sem("written")
        dve_chain, act_chain = sem("dve_chain"), sem("act_chain")

        def keys(u):
            return range(units[u][2] // 128, TT)

        @block.tensor
        def _(pe):
            def scores(u, s):
                q, h, first = units[u]
                if u:
                    pe.wait_ge(exped, 2 * (u - 1) + s + 1)
                r = slice(64 * s, 64 * s + 64)
                lhs = qk[r, h, q * 128:(q + 1) * 128]
                if not first:
                    nc.tensor.matmul(score(s)[:, 0:N_X], lhs, qk[r, 4 + h, 0:N_X], start=True, stop=True)
                nc.tensor.matmul(score(s)[:, N_X:N_ALL], lhs, qk[r, 4 + h, N_X:N_ALL],
                                 start=True, stop=True).then_inc(scored, 1)

            def turn_unit(u):
                pe.wait_ge(weighed, u + 1)
                if u:
                    pe.wait_ge(turned_sb, u)
                for m in keys(u):
                    last = nc.tensor.transpose(turn[:, m * 128:(m + 1) * 128],
                                               prob[:, u % 3, 0, m * 128:(m + 1) * 128], c.tab["ident"])
                last.then_inc(turned_ps, 1)

            def values(u):
                pe.wait_ge(turned_sb, u + 1)
                if u >= 2:
                    pe.wait_ge(kept, u - 1)
                h = units[u][1]
                for m in keys(u):
                    last = nc.tensor.matmul(c.ps[:, 6 + u % 2, 0:128], turned[:, u % 2, m * 128:(m + 1) * 128],
                                            v[:, m, h * 128:(h + 1) * 128], start=m == keys(u)[0], stop=m == TT - 1)
                last.then_inc(valued, 1)

            for i in range(n_units + 3):
                if i < n_units:
                    scores(i, 0)
                if 0 <= i - 2 < n_units:
                    turn_unit(i - 2)
                if i < n_units:
                    scores(i, 1)
                if 0 <= i - 3 < n_units:
                    values(i - 3)
            for h in range(4):
                pe.wait_ge(normed, h + 1)
                if h >= 2:
                    pe.wait_ge(written, h - 1)
                for t in range(TT):
                    last = nc.tensor.transpose(flat[:, (h % 2) * 1024 + t * 128:(h % 2) * 1024 + (t + 1) * 128],
                                               by_unit[:, h * TT + t, :], c.tab["ident"])
                last.then_inc(back, 1)

        @block.scalar
        def _(act):
            link = chain(act, act_chain)

            def exps(u, s):
                first = units[u][2]
                act.wait_ge(maxed, 2 * u + s + 1)
                if u >= 3:
                    act.wait_ge(turned_ps, u - 2)
                nc.scalar.activation(prob[:, u % 3, s, first:N_ALL], score(s)[:, first:N_ALL], ACT.Exp,
                                     bias=neg[:, u % 2, s:s + 1], scale=scale,
                                     accum_out=total[:, u % 2, s:s + 1]).then_inc(exped, 1)

            for i in range(n_units + 4):
                if i < n_units:
                    exps(i, 0)
                if 0 <= i - 2 < n_units:
                    u = i - 2
                    act.wait_ge(turned_ps, u + 1)
                    if u >= 2:
                        act.wait_ge(valued, u - 1)
                    first = units[u][2]
                    nc.scalar.activation(turned[:, u % 2, first:N_ALL], turn[:, first:N_ALL],
                                         ACT.Copy).then_inc(turned_sb, 1)
                if i < n_units:
                    exps(i, 1)
                if 0 <= i - 4 < n_units:
                    u = i - 4
                    act.wait_ge(valued, u + 1)
                    nc.scalar.activation(by_unit[:, place(u), :], c.ps[:, 6 + u % 2, 0:128], ACT.Copy).then_inc(kept, 1)
                    act.wait_ge(kept, u + 1)
                    link(nc.scalar.activation(junk, by_unit[:, place(u), :], ACT.Square,
                                              accum_out=rstd[:, place(u):place(u) + 1]))
            link(nc.scalar.activation(rstd, rstd, ACT.Ln, bias=EPS, scale=1.0 / 128))
            nc.scalar.activation(rstd, rstd, ACT.Exp, scale=-0.5).then_inc(rooted, 1)
            for h in range(4):
                act.wait_ge(back, h + 1)
                nc.scalar.activation(out[:, 4 + h, :], flat[:, (h % 2) * 1024:(h % 2) * 1024 + N_ALL], ACT.Copy,
                                     scale=c.stat[:, 204:205]).then_inc(written, 1)

        @block.vector
        def _(dve):
            link = chain(dve, dve_chain)

            def maxima(u, s):
                first = units[u][2]
                dve.wait_ge(scored, 2 * u + s + 1)
                link(nc.vector.reduce_max(top[:, u % 2, s:s + 1], score(s)[:, first:N_ALL], AX.X))
                if u >= 2:
                    dve.wait_ge(exped, 2 * u - 2)
                nc.vector.tensor_scalar(neg[:, u % 2, s:s + 1], top[:, u % 2, s:s + 1], -scale, None,
                                        ALU.mult).then_inc(maxed, 1)

            for i in range(n_units + 1):
                if i < n_units:
                    maxima(i, 0)
                if i:
                    u = i - 1
                    first = units[u][2]
                    b = u % 2
                    dve.wait_ge(exped, 2 * u + 2)
                    link(nc.vector.reciprocal(total[:, b, :], total[:, b, :]))
                    link(nc.vector.tensor_tensor(lam[:, b, 1:2], total[:, b, 1:2], c.stat[:, 203:204], ALU.mult))
                    link(nc.vector.tensor_scalar(prob[:, u % 3, 1, first:N_ALL], prob[:, u % 3, 1, first:N_ALL],
                                                 lam[:, b, 1:2], None, ALU.mult))
                    nc.vector.scalar_tensor_tensor(prob[:, u % 3, 0, first:N_ALL], prob[:, u % 3, 0, first:N_ALL],
                                                   total[:, b, 0:1], prob[:, u % 3, 1, first:N_ALL],
                                                   ALU.mult, ALU.add).then_inc(weighed, 1)
                if i < n_units:
                    maxima(i, 1)
            dve.wait_ge(rooted, 1)
            for h in range(4):
                units_of = by_unit[:, h * TT:(h + 1) * TT, :]
                nc.vector.tensor_tensor(units_of, units_of, rstd[:, h * TT:(h + 1) * TT].unsqueeze(2)
                                        .to_broadcast([128, TT, 128]), ALU.mult).then_inc(normed, 1)


def gdn_buffers(c):
    o = KT * N_ALL
    qkv = c.arena[:, o:o + 12 * N_ALL].rearrange("p (k t) -> p k t", k=12)
    gate = c.arena[:, o + 12 * N_ALL:o + 16 * N_ALL].rearrange("p (k t) -> p k t", k=4)
    return qkv, gate, o + 16 * N_ALL


SMALL = ("g", "beta", "gc", "exp_gc", "exp_tail", "exp_last", "beta_exp_gc", "work")


def small(c, name):
    i = SMALL.index(name)
    return c.small[:, 96 * i:96 * i + 96]


def chunk_of(step, direction):
    if step < CZ:
        return N_X + CHUNK * (step if direction == 0 else CZ - 1 - step)
    return CHUNK * (step - CZ if direction == 0 else CX - 1 - (step - CZ))


def gdn_gates(c):
    nc, a = c.nc, c.a
    st, sem = stage(c)
    lo, _ = c.range_of["gdn_gates"]
    ht = ht_view(c)
    ba = gdn_buffers(c)[1][0:32, 0, :]
    raw = c.arena[:, c.arena_size - 192:].rearrange("p (s v) -> p s v", v=8)
    va = c.arena[:, c.arena_size - 400:c.arena_size - 384]
    rates = va[:, 0:16].rearrange("p (v s) -> p v s", v=2)
    by_head = c.arena[:, c.arena_size - 384:c.arena_size - 352].rearrange("p (i s) -> p i s", i=2)
    s24 = lambda n: small(c, n).rearrange("p (s v) -> p s v", v=4)
    by_dir = lambda ap, d: ap.rearrange("p (s u v) -> p s u v", u=2, v=4)[:, :, d, :]
    with st, nc.Block() as block:
        consts_in, product, drained, picked, summed = (sem(n) for n in ("consts_in", "product", "drained", "picked", "summed"))
        act_step, dve_step, rates_in = sem("act_step"), sem("dve_step"), sem("rates_in")

        @block.sync
        def _(sp):
            for i, name in enumerate(("gdn_a_log", "gdn_dt_bias")):
                sp.dma_start(by_head[:, i, :], a[name][0].rearrange("u h -> (u h)").partition_broadcast(128))\
                    .then_inc(consts_in, 16)
            c.issue(sp, "gdn_gates", lambda j: (product, 1))

        @block.tensor
        def _(pe):
            c.arrived(pe, lo)
            w = c.slot(lo, KT, 32)
            for x, n, bank in ((0, N_X, 0), (N_X, N_Z, 1)):
                for k in range(KT):
                    last = nc.tensor.matmul(c.ps[0:32, bank, 0:n], w[:, k, :], ht[:, k, x:x + n],
                                            start=k == 0, stop=k == KT - 1)
            last.then_inc(product, 1)
            pe.wait_ge(drained, 1)
            pick = c.tab["pick"][0:32, :].rearrange("p (u h v) -> p u h v", u=2, h=2)
            for s in range(STEPS):
                for r in range(2):
                    t0 = chunk_of(s, r)
                    for hh in range(2):
                        last = nc.tensor.matmul(c.ps[64 * hh:64 * hh + 64, 2, (2 * s + r) * 8:(2 * s + r) * 8 + 8],
                                                ba[:, t0:t0 + CHUNK], pick[:, r, hh, :], start=True, stop=True)
            last.then_inc(picked, 1)
            pe.wait_ge(dve_step, 10)
            for r in range(2):
                nc.tensor.matmul(c.ps[:, 3 + r, 0:48], c.tab["tri2"][:, r * 128:(r + 1) * 128], by_dir(small(c, "g"), r),
                                 start=True, stop=True)
            nc.tensor.matmul(c.ps[:, 5, 0:96], c.tab["heads"], small(c, "g"), start=True, stop=True).then_inc(summed, 1)

        @block.vector
        def _(dve):
            v = nc.vector
            link = chain(dve, dve_step)
            dve.wait_ge(product, 1)
            v.tensor_copy(ba[:, 0:N_X], c.ps[0:32, 0, :])
            v.tensor_copy(ba[:, N_X:N_ALL], c.ps[0:32, 1, 0:N_Z]).then_inc(drained, 1)
            dve.wait_ge(picked, 1)
            link(v.tensor_copy(raw.rearrange("p s v -> p (s v)"), c.ps[:, 2, 0:192]))
            dve.wait_ge(consts_in, 32)
            for hh in range(2):
                half = slice(64 * hh, 64 * hh + 64)
                last = v.tensor_copy(rates[half], by_head[half, :, hh::2])
            last.then_inc(rates_in, 1)
            dve.wait_ge(rates_in, 1)
            alpha = raw[:, :, 4:8]
            dt = rates[:, 1, :].rearrange("p (u v) -> p u v", u=2).unsqueeze(1).to_broadcast([128, STEPS, 2, 4])
            link(v.tensor_tensor(alpha.rearrange("p (s u) v -> p s u v", u=2),
                                 alpha.rearrange("p (s u) v -> p s u v", u=2), dt, ALU.add))
            link(v.tensor_scalar(s24("work"), alpha, -1.0, None, ALU.mult))
            link(v.tensor_tensor(s24("work"), s24("work"), alpha, ALU.min))
            dve.wait_ge(act_step, 4)
            link(v.tensor_scalar(s24("beta"), s24("beta"), 1.0, None, ALU.add))
            link(v.reciprocal(s24("beta"), s24("beta")))
            link(v.tensor_scalar(s24("g"), alpha, 0.0, None, ALU.max))
            link(v.tensor_tensor(s24("g"), s24("g"), s24("work"), ALU.add))
            rate = rates[:, 0, :].rearrange("p (u v) -> p u v", u=2).unsqueeze(1).to_broadcast([128, STEPS, 2, 4])
            g4 = small(c, "g").rearrange("p (s u v) -> p s u v", u=2, v=4)
            link(v.tensor_tensor(g4, g4, rate, ALU.mult))
            link(v.tensor_scalar(s24("g"), s24("g"), -1.0, None, ALU.mult))
            dve.wait_ge(summed, 1)
            for r in range(2):
                link(v.tensor_copy(by_dir(small(c, "gc"), r), c.ps[:, 3 + r, 0:48].rearrange("p (s v) -> p s v", v=4)))
            link(v.tensor_copy(small(c, "exp_last"), c.ps[:, 5, 0:96]))
            link(v.tensor_tensor(small(c, "exp_tail"), small(c, "exp_last"), small(c, "gc"), ALU.subtract))
            dve.wait_ge(act_step, 7)
            link(v.tensor_tensor(small(c, "beta_exp_gc"), small(c, "beta"), small(c, "exp_gc"), ALU.mult))

        @block.scalar
        def _(act):
            link = chain(act, act_step)
            act.wait_ge(dve_step, 1)
            link(nc.scalar.activation(s24("beta"), raw[:, :, 0:4], ACT.Exp, scale=-1.0))
            act.wait_ge(dve_step, 4)
            link(nc.scalar.activation(s24("work"), s24("work"), ACT.Exp))
            link(nc.scalar.activation(rates[:, 0, :], rates[:, 0, :], ACT.Exp))
            link(nc.scalar.activation(s24("work"), s24("work"), ACT.Ln, bias=1.0))
            act.wait_ge(dve_step, 14)
            nc.scalar.activation(small(c, "exp_gc"), small(c, "gc"), ACT.Exp).then_inc(act_step, 1)
            nc.scalar.activation(small(c, "exp_last"), small(c, "exp_last"), ACT.Exp).then_inc(act_step, 1)
            nc.scalar.activation(small(c, "exp_tail"), small(c, "exp_tail"), ACT.Exp).then_inc(act_step, 1)


def head_norm(c, buf, tiles, n_sum, extra, finish, sq, root):
    nc = c.nc
    st, sem = stage(c)
    sq, root = (ap.rearrange("p (b t) -> p b t", t=N_ALL) for ap in (sq, root))
    flat = c.ps.rearrange("p b n -> p (b n)")
    with st, nc.Block() as block:
        squared, summed, logged, rooted, dve_chain = \
            (sem(n) for n in ("squared", "summed", "logged", "rooted", "dve_chain"))

        @block.tensor
        def _(pe):
            for n in range(len(tiles)):
                pe.wait_ge(squared, n + 1)
                if n >= 4:
                    pe.wait_ge(logged, n - 3)
                s = (n % 4) * 2
                nc.tensor.matmul(c.ps[:, s, :], c.tab["heads"], sq[:, n % 2, 0:N_X], start=True, stop=True)
                nc.tensor.matmul(c.ps[:, s + 1, 0:N_Z], c.tab["heads"], sq[:, n % 2, N_X:N_ALL],
                                 start=True, stop=True).then_inc(summed, 1)

        @block.scalar
        def _(act):
            def square(n):
                if n < len(tiles):
                    if n >= 2:
                        act.wait_ge(summed, n - 1)
                    nc.scalar.activation(sq[:, n % 2, :], buf[:, tiles[n], :], ACT.Square).then_inc(squared, 1)

            square(0)
            for n in range(len(tiles)):
                square(n + 1)
                act.wait_ge(summed, n + 1)
                nc.scalar.activation(root[:, n, :], flat[:, (n % 4) * 1024:(n % 4) * 1024 + N_ALL],
                                     ACT.Ln, bias=EPS, scale=1.0 / n_sum).then_inc(logged, 1)
            for n in range(len(tiles)):
                act.wait_ge(logged, n + 1)
                nc.scalar.activation(root[:, n, :], root[:, n, :], ACT.Exp, bias=extra(n),
                                     scale=-0.5).then_inc(rooted, 1)

        @block.vector
        def _(dve):
            link = chain(dve, dve_chain)
            for n in range(len(tiles)):
                dve.wait_ge(rooted, n + 1)
                finish(link, buf[:, tiles[n], :], root[:, n, :], n)


def chunk_tables(c):
    view = lambda ap: ap.rearrange("p (k t) -> p k t", k=4)
    n = 4 * N_ALL
    return view(c.ring[:, 0:n]), view(c.ht[:, 0:n]), view(c.ht[:, n:2 * n])


def idle_tables(c):
    o = _TABLE["win_l"][0]
    return [c.table[:, o + 512 * i:o + 512 * i + 512] for i in range((TABLE_COLS - o) // 512)]


def reload_tables(c, sp, loaded):
    for o, n in ((_TABLE["cos"][0], 1024), (_TABLE["win_l"][0], TABLE_COLS - _TABLE["win_l"][0])):
        sp.dma_start(c.table[:, o:o + n], c.a["t_table"][:, o:o + n]).then_inc(loaded, 16)


def chunk_products(c):
    nc = c.nc
    st, sem = stage(c)
    qkv, _, _ = gdn_buffers(c)
    q, k, v = (qkv[:, 4 * i:4 * i + 4, :] for i in range(3))
    k_rows, k_k, k_q = chunk_tables(c)
    bank = lambda g, what: c.ps[:, 4 * (g % 2) + what, :]
    groups = N_ALL // 128
    q_and_k = qkv.rearrange("p (u k) t -> p k u t", u=3)[:, :, 0:2]

    def place(copy, g, what, cross):
        for chunk in range(2):
            hh = 1 - chunk if cross else chunk
            t = slice(128 * g + 64 * chunk, 128 * g + 64 * chunk + 64)
            src = bank(g, what)[64 * chunk:64 * chunk + 64, :].rearrange("p (v h e) -> p v h e", v=4, h=2)[:, :, hh]
            last = copy((k_rows, v)[what][64 * hh:64 * hh + 64, :, t], src)
        return last

    with st, nc.Block() as block:
        turned, multiplied, dve_drained, act_drained = (sem(n) for n in ("turned", "multiplied", "dve_drained", "act_drained"))

        @block.tensor
        def _(pe):
            for g in range(groups):
                if g >= 2:
                    pe.wait_ge(dve_drained, g - 1)
                for what in range(2):
                    for p in range(4):
                        last = nc.tensor.transpose(bank(g, what)[:, 128 * p:128 * p + 128],
                                                   (k, v)[what][:, p, 128 * g:128 * g + 128], c.tab["ident"])
                last.then_inc(turned, 1)
                for half in range(2):
                    t = slice(128 * g + 64 * half, 128 * g + 64 * half + 64)
                    for p in range(4):
                        for hh in range(2):
                            pa = slice(64 * hh, 64 * hh + 64)
                            out = bank(g, 2 + half)[pa, :].rearrange("p (u v e) -> p u v e", u=2, v=4)
                            last = nc.tensor.matmul(out[:, :, p], k[pa, p, t], q_and_k[pa, p, :, t],
                                                    start=True, stop=True)
                last.then_inc(multiplied, 1)

        @block.scalar
        def _(act):
            for g in range(groups):
                act.wait_ge(turned, g + 1)
                copy = lambda dst, src: nc.scalar.activation(dst, src, ACT.Copy)
                place(copy, g, 0, False)
                place(copy, g, 1, False).then_inc(act_drained, 1)

        @block.vector
        def _(dve):
            for g in range(groups):
                dve.wait_ge(act_drained, g + 1)
                place(nc.vector.tensor_copy, g, 0, True)
                place(nc.vector.tensor_copy, g, 1, True)
                dve.wait_ge(multiplied, g + 1)
                for half in range(2):
                    t = slice(128 * g + 64 * half, 128 * g + 64 * half + 64)
                    both = bank(g, 2 + half).rearrange("p (u v e) -> p u v e", u=2, v=4)
                    nc.vector.tensor_copy(k_q[:, :, t], both[:, 0])
                    last = nc.vector.tensor_copy(k_k[:, :, t], both[:, 1])
                last.then_inc(dve_drained, 1)


def delta_rule(c):
    nc = c.nc
    st, sem = stage(c)
    qkv, gate, o = gdn_buffers(c)
    k_rows, k_k, k_q = chunk_tables(c)
    out = outc(c)
    pool = [c.arena[:, o + 512 * i:o + 512 * i + 512] for i in range((c.arena_size - o) // 512)]
    pool += [c.ring[:, 4 * N_ALL + 512 * i:4 * N_ALL + 512 * i + 512] for i in range((RING * SLOT - 4 * N_ALL) // 512)]
    pool += [c.tab["cos"], c.tab["sin"]] + idle_tables(c)
    take = lambda: pool.pop()
    two = lambda: [take(), take()]
    q_k, q_dec, X_t = (two() for _ in range(3))
    decay, dist, v_beta, v_new, S, S_kept, g_tri = (take() for _ in range(7))
    by_heads = lambda ap: ap.rearrange("p (v h e) -> p v h e", v=4, h=2)
    A, X, T, k_tail = ([by_heads(take()) for r in range(2)] for _ in range(4))
    parts = (slice(0, 64), slice(64, 128))
    tail_by_heads = c.arena[:, c.arena_size - 192:].rearrange("p (n h) -> p n h", h=2)
    half = lambda ap, r: ap[:, 256 * r:256 * r + 256]
    four = lambda ap: ap.rearrange("p (u v e) -> p u v e", u=2, v=4)
    rows = lambda name, s: small(c, name)[:, 8 * s:8 * s + 8].unsqueeze(2).to_broadcast([128, 8, 64])
    rows_r = lambda name, s, r: small(c, name)[:, 8 * s + 4 * r:8 * s + 4 * r + 4].unsqueeze(2).to_broadcast([128, 4, 64])
    eight = lambda ap: ap.rearrange("p (n e) -> p n e", n=8)
    pairs = lambda ap: ap.rearrange("p (v e) -> p v e", v=4)
    table = lambda ap: ap.rearrange("p (u e) -> p u e", u=2).unsqueeze(2).to_broadcast([128, 2, 4, 64])
    table_r = lambda ap, r: ap[:, 64 * r:64 * r + 64].unsqueeze(1).to_broadcast([128, 4, 64])
    eye = c.tab["eye"].unsqueeze(1).to_broadcast([128, 4, 64])
    mask_t = lambda n, r: table_r(c.tab["mt"][:, n * 128:(n + 1) * 128], r)
    chunk = lambda buf, s, r: buf[:, 0:4, chunk_of(s, r):chunk_of(s, r) + 64]
    NL = len(LEVELS)
    heads = [(p, slice(64 * hh, 64 * hh + 64), slice(p * 64, p * 64 + 64)) for p in range(4) for hh in range(2)]
    blocks = [(r, p, pa, slice(256 * r + 64 * p, 256 * r + 64 * p + 64)) for r in range(2) for p, pa, _ in heads]
    B_GR, B_X, B_XT, B_REC, B_OUT, B_STATE = 0, 1, 3, 5, 6, 7

    with st, nc.Block() as block:
        names = ("g_spread", "decays", "dist_read", "masked_dist", "exps", "q_dec_exps", "q_scaled", "a_ready",
                 "v_scaled", "k_scaled", "state_read", "residual", "v_ps", "v_ready", "out_ps", "state_ps",
                 "state", "out_added", "dve_chain", "inverse_set", "zeroed",
                 "tail_placed", "k_k_scaled", "lowered", "block_masked", "state_kept")
        s_ = {n: sem(n) for n in names}
        level_t, level_masked, grown, inverse_t, inverse = ([sem(f"{n}{r}") for r in range(2)]
                                                 for n in ("level_t", "level_masked", "grown", "inverse_t", "inverse"))

        @block.tensor
        def _(pe):
            mm = nc.tensor.matmul

            def decays(s):
                pe.wait_ge(s_["g_spread"], s + 1)
                if s:
                    pe.wait_ge(s_["dist_read"], s)
                    pe.wait_ge(s_["q_dec_exps"], s)
                mm(c.ps[:, B_GR, :], c.tab["heads"], g_tri, start=True, stop=True).then_inc(s_["decays"], 1)

            def transposed_a(s, n, r):
                if n == 0:
                    pe.wait_ge(s_["a_ready"], s + 1)
                else:
                    pe.wait_ge(inverse_t[r], NL * s + n)
                for p in range(4):
                    fr = slice(64 * p, 64 * p + 64)
                    rhs = c.tab["eye"] if n == 0 else half(X_t[s % 2], r)[:, fr]
                    last = mm(c.ps[:, (B_XT if n else B_X) + r, fr], A[r][:, p].rearrange("p h e -> p (h e)"), rhs, start=True, stop=True)
                last.then_inc(level_t[r], 1)

            def products(s, n, r):
                if n == 1:
                    pe.wait_ge(s_["inverse_set"], s + 1)
                else:
                    pe.wait_ge(inverse[r], (NL - 2) * s + n - 1)
                pe.wait_ge(level_masked[r], NL * s + n + 1)
                whole = lambda m, p: m[r][:, p].rearrange("p h e -> p (h e)")
                for p in range(4):
                    last = mm(c.ps[:, B_XT + r, 128 * p:128 * p + 128], whole(X, p), whole(T, p), start=True, stop=True)
                if n < NL - 1:
                    for p in range(4):
                        last = mm(c.ps[:, B_X + r, 128 * p:128 * p + 128], whole(T, p), whole(X, p), start=True, stop=True)
                last.then_inc(grown[r], 1)

            def read_state(s):
                pe.wait_ge(s_["state"], s + 1)
                for r, p, pa, fr in blocks:
                    t0 = chunk_of(s, r)
                    last = mm(c.ps[pa, B_REC, fr], qkv[pa, 4 + p, t0:t0 + 64], S[pa, fr], start=True, stop=True)
                last.then_inc(s_["state_read"], 1)

            def new_values(s):
                for r in range(2):
                    pe.wait_ge(inverse_t[r], NL * (s + 1))
                pe.wait_ge(s_["residual"], s + 1)
                for r, p, pa, fr in blocks:
                    last = mm(c.ps[pa, B_REC, fr], X_t[s % 2][pa, fr], v_beta[pa, fr],
                              start=True, stop=True)
                last.then_inc(s_["v_ps"], 1)

            def outputs(s):
                pe.wait_ge(s_["v_ready"], s + 1)
                pe.wait_ge(s_["k_scaled"], s + 1)
                for r in range(2):
                    for p in range(4):
                        fr = slice(256 * r + 64 * p, 256 * r + 64 * p + 64)
                        last = mm(c.ps[:, B_STATE, fr], k_tail[r][:, p].rearrange("p h e -> p (h e)"), v_new[:, fr],
                                  start=True, stop=True)
                last.then_inc(s_["state_ps"], 1)
                pe.wait_ge(s_["q_scaled"], s + 1)
                if s:
                    pe.wait_ge(s_["out_added"], s)
                for r, p, pa, fr in blocks:
                    mm(c.ps[pa, B_OUT, fr], S[pa, fr], q_dec[s % 2][pa, fr], start=True, stop=False)
                    last = mm(c.ps[pa, B_OUT, fr], v_new[pa, fr], q_k[s % 2][pa, fr], start=False, stop=True)
                last.then_inc(s_["out_ps"], 1)

            decays(0)
            for s in range(STEPS):
                for r in range(2):
                    transposed_a(s, 0, r)
                if s:
                    read_state(s - 1)
                if s + 1 < STEPS:
                    decays(s + 1)
                for n in range(1, NL):
                    for r in range(2):
                        transposed_a(s, n, r)
                    for r in range(2):
                        products(s, n, r)
                    if s and n == 1:
                        new_values(s - 1)
                    if s and n == 2:
                        outputs(s - 1)
            read_state(STEPS - 1)
            new_values(STEPS - 1)
            outputs(STEPS - 1)

        @block.scalar
        def _(act):
            def decay_exps(s):
                act.wait_ge(s_["masked_dist"], 2 * s + 1)
                nc.scalar.activation(decay, decay, ACT.Exp).then_inc(s_["exps"], 1)
                if s >= 2:
                    act.wait_ge(s_["out_ps"], s - 1)
                act.wait_ge(s_["dist_read"], s + 1)
                nc.scalar.activation(q_dec[s % 2], c.ps[:, B_GR, :], ACT.Exp).then_inc(s_["q_dec_exps"], 1)
                act.wait_ge(s_["masked_dist"], 2 * s + 2)
                nc.scalar.activation(q_k[s % 2], q_k[s % 2], ACT.Exp).then_inc(s_["exps"], 1)

            def place_lower(s):
                act.wait_ge(s_["lowered"], s + 1)
                for r in range(2):
                    if s:
                        act.wait_ge(level_t[r], NL * s)
                    else:
                        act.wait_ge(s_["zeroed"], 1)
                    for hh, pa in enumerate(parts):
                        last = nc.scalar.activation(A[r][pa, :, hh], pairs(half(decay, r))[pa], ACT.Copy)
                last.then_inc(s_["a_ready"], 1)

            decay_exps(0)
            place_lower(0)
            for s in range(STEPS + 1):
                if s:
                    act.wait_ge(s_["v_ps"], s)
                    nc.scalar.activation(v_new, c.ps[:, B_REC, :], ACT.Copy).then_inc(s_["v_ready"], 1)
                if s + 1 < STEPS:
                    decay_exps(s + 1)
                    place_lower(s + 1)

        @block.gpsimd
        def _(pool_):
            tt = nc.gpsimd.tensor_tensor

            def spread(s):
                if s:
                    pool_.wait_ge(s_["decays"], s)
                tt(four(g_tri), rows("g", s).rearrange("p (u v) e -> p u v e", u=2), table(c.tab["tri"]),
                   ALU.mult).then_inc(s_["g_spread"], 1)

            def mask(s):
                pool_.wait_ge(s_["dist_read"], s + 1)
                tt(four(decay), four(dist), table(c.tab["mask_a"]), ALU.add).then_inc(s_["masked_dist"], 1)
                if s >= 2:
                    pool_.wait_ge(s_["out_ps"], s - 1)
                tt(four(q_k[s % 2]), table(c.tab["mask_q"]), four(dist), ALU.subtract).then_inc(s_["masked_dist"], 1)
                pool_.wait_ge(s_["masked_dist"], 2 * s + 2)
                for r in range(2):
                    last = tt(pairs(half(dist, r)), chunk(k_k, s, r), rows_r("beta", s, r), ALU.mult)
                last.then_inc(s_["k_k_scaled"], 1)

            def block_mask(s):
                pool_.wait_ge(s_["a_ready"], s + 1)
                for r in range(2):
                    last = tt(pairs(half(decay, r)), pairs(half(decay, r)), table_r(c.tab["m1"], r), ALU.mult)
                last.then_inc(s_["block_masked"], 1)

            def keep_state(s):
                pool_.wait_ge(s_["state"], s + 1)
                tt(eight(S_kept), eight(S), rows("exp_last", s), ALU.mult).then_inc(s_["state_kept"], 1)

            def scale_queries(s):
                pool_.wait_ge(s_["q_dec_exps"], s + 1)
                for r in range(2):
                    tt(four(q_dec[s % 2])[:, r], four(q_dec[s % 2])[:, r], chunk(qkv, s, r), ALU.mult)
                pool_.wait_ge(s_["exps"], 2 * s + 2)
                for r in range(2):
                    last = tt(four(q_k[s % 2])[:, r], four(q_k[s % 2])[:, r], chunk(k_q, s, r), ALU.mult)
                last.then_inc(s_["q_scaled"], 1)

            for m in (*X, *T, *A):
                last = nc.gpsimd.memset(m, 0.0)
            last.then_inc(s_["zeroed"], 1)
            spread(0)
            mask(0)
            scale_queries(0)
            block_mask(0)
            for s in range(STEPS):
                if s + 1 < STEPS:
                    spread(s + 1)
                    mask(s + 1)
                if s:
                    pool_.wait_ge(s_["v_ps"], s)
                for r in range(2):
                    last = tt(pairs(half(v_beta, r)), chunk(qkv[:, 8:12, :], s, r), rows_r("beta", s, r), ALU.mult)
                last.then_inc(s_["v_scaled"], 1)
                if s:
                    pool_.wait_ge(s_["state_ps"], s)
                else:
                    pool_.wait_ge(s_["tail_placed"], 1)
                for r in range(2):
                    k = chunk(k_rows, s, r).unsqueeze(2).to_broadcast([128, 4, 2, 64])
                    tail = tail_by_heads[:, 8 * s + 4 * r:8 * s + 4 * r + 4, :].unsqueeze(3).to_broadcast([128, 4, 2, 64])
                    last = tt(k_tail[r], k, tail, ALU.mult)
                last.then_inc(s_["k_scaled"], 1)
                if s + 1 < STEPS:
                    scale_queries(s + 1)
                keep_state(s)
                if s + 1 < STEPS:
                    block_mask(s + 1)

        @block.vector
        def _(dve):
            v = nc.vector
            link = chain(dve, s_["dve_chain"])

            def residual(s):
                dve.wait_ge(s_["state_read"], s + 1)
                link(v.tensor_tensor(eight(dist), eight(c.ps[:, B_REC, :]), rows("beta_exp_gc", s), ALU.mult))
                dve.wait_ge(s_["v_scaled"], s + 1)
                v.tensor_tensor(v_beta, v_beta, dist, ALU.subtract).then_inc(s_["residual"], 1)

            def state(s):
                dve.wait_ge(s_["out_ps"], s + 1)
                dve.wait_ge(s_["state_kept"], s + 1)
                v.tensor_tensor(S, S_kept, c.ps[:, B_STATE, :], ALU.add).then_inc(s_["state"], 1)
                first = s < CZ // 2 or CZ <= s < CZ + CX // 2
                for r in range(2):
                    dst, src = chunk(out, s, r), four(c.ps[:, B_OUT, :])[:, r]
                    last = v.tensor_copy(dst, src) if first else v.tensor_tensor(dst, dst, src, ALU.add)
                last.then_inc(s_["out_added"], 1)

            def distances(s):
                dve.wait_ge(s_["decays"], s + 1)
                v.tensor_tensor(eight(dist), rows("gc", s), eight(c.ps[:, B_GR, :]), ALU.subtract)\
                    .then_inc(s_["dist_read"], 1)

            def lower(s):
                dve.wait_ge(s_["k_k_scaled"], s + 1)
                dve.wait_ge(s_["exps"], 2 * s + 1)
                v.tensor_tensor(decay, decay, dist, ALU.mult).then_inc(s_["lowered"], 1)

            def first_inverse(s):
                dve.wait_ge(s_["block_masked"], s + 1)
                for r in range(2):
                    for hh, pa in enumerate(parts):
                        last = v.tensor_tensor(X[r][pa, :, hh], eye[pa], pairs(half(decay, r))[pa], ALU.subtract)
                last.then_inc(s_["inverse_set"], 1)

            def mask_level(s, n, r):
                dve.wait_ge(level_t[r], NL * s + n + 1)
                for hh, pa in enumerate(parts):
                    last = v.tensor_tensor(T[r][pa, :, hh], pairs(c.ps[pa, (B_XT if n else B_X) + r, 0:256]), mask_t(n, r)[pa], ALU.mult)
                last.then_inc(level_masked[r], 1)

            v.memset(S, 0.0).then_inc(s_["state"], 1)
            link(v.memset(tail_by_heads, 0.0))
            for hh, pa in enumerate(parts):
                last = v.tensor_copy(tail_by_heads[pa, :, hh], small(c, "exp_tail")[pa])
            last.then_inc(s_["tail_placed"], 1)
            dve.wait_ge(s_["zeroed"], 1)
            def grow(s, n, r):
                whole = X[r].rearrange("p v h e -> p (v h e)")
                v.tensor_tensor(whole, whole, c.ps[:, B_X + r, :], ALU.subtract).then_inc(inverse[r], 1)

            def grow_t(s, n, r):
                if n:
                    dve.wait_ge(grown[r], (NL - 1) * s + n)
                else:
                    dve.wait_ge(level_masked[r], NL * s + 1)
                for hh, pa in enumerate(parts):
                    dst = pairs(half(X_t[s % 2], r))[pa]
                    more = by_heads(c.ps[:, B_XT + r, :])[pa, :, hh] if n else T[r][pa, :, hh]
                    last = v.tensor_tensor(dst, dst if n else eye[pa], more, ALU.subtract)
                last.then_inc(inverse_t[r], 1)

            distances(0)
            lower(0)
            for s in range(STEPS):
                mask_level(s, 0, 0)
                mask_level(s, 0, 1)
                grow_t(s, 0, 0)
                grow_t(s, 0, 1)
                first_inverse(s)
                for n in range(1, NL):
                    mask_level(s, n, 0)
                    if n > 1:
                        grow(s, n - 1, 1)
                    mask_level(s, n, 1)
                    if s and n == 1:
                        residual(s - 1)
                    if s and n == 3:
                        state(s - 1)
                    if s + 1 < STEPS:
                        if n == 2:
                            distances(s + 1)
                        if n == 4:
                            lower(s + 1)
                    grow_t(s, n, 0)
                    if n < NL - 1:
                        grow(s, n, 0)
                    grow_t(s, n, 1)
            residual(STEPS - 1)
            state(STEPS - 1)


def norm_qk(c):
    buf, _, o = gdn_buffers(c)
    head_norm(c, buf, range(8), 1, lambda n: math.log(GW // GH) * -0.5 if n < 4 else 0.0,
              lambda link, y, root, n: c.nc.vector.tensor_tensor(y, y, root, ALU.mult),
              c.arena[:, o:o + 2 * N_ALL], c.ht)


def gdn_output(c):
    nc, a = c.nc, c.a
    _, gate, o = gdn_buffers(c)
    gain = c.stat[:, 205:206]
    st, sem = stage(c)
    gain_in = sem("gain_in")
    with st:
        with nc.Block() as block:
            @block.sync
            def _(sp):
                for hh in range(2):
                    sp.dma_start(gain[64 * hh:64 * hh + 64, :], a["gdn_norm_g"][0].unsqueeze(1)).then_inc(gain_in, 16)
                c.prefetch(sp, "ab_out")
                reload_tables(c, sp, c.tables_back)
                sp.wait_ge(gain_in, 32)

    def finish(link, y, root, n):
        link(nc.vector.scalar_tensor_tensor(y, y, gain, root, ALU.mult, ALU.mult))
        return nc.vector.tensor_tensor(y, y, gate[:, n, :], ALU.mult)

    head_norm(c, outc(c), range(4), HEAD, lambda n: 0.0, finish, c.ht[:, 0:2 * N_ALL], c.ht[:, 2 * N_ALL:6 * N_ALL])


def mixed_rows(c):
    return c.ht.rearrange("p (t d) -> p t d", t=TT)


def branch_squares(c, n_chunks):
    return c.stat[:, 32:32 + TT * n_chunks].rearrange("p (t j) -> p t j", t=TT)


def norm_squares(c):
    return c.stat[:, 8:8 + TT]


def add_branch(c, w, tiles, n_chunks, next_norm=True):
    nc = c.nc
    st, sem = stage(c)
    y = mixed_rows(c)
    junk = c.arena[:, 0:D]
    rstd = c.stat[:, 0:TT]
    n = len(tiles)
    with st, nc.Block() as block:
        summed, stats, dve_chain, added = sem("summed"), sem("stats"), sem("dve_chain"), sem("added")
        act_chain = sem("act_chain")

        @block.scalar
        def _(act):
            link = chain(act, act_chain)
            act.wait_ge(summed, 1)
            link(nc.scalar.activation(rstd[:, 0:n], rstd[:, 0:n], ACT.Ln, bias=EPS, scale=1.0 / D))
            nc.scalar.activation(rstd[:, 0:n], rstd[:, 0:n], ACT.Exp, scale=-0.5).then_inc(stats, 1)
            if next_norm:
                for i, t in enumerate(tiles):
                    act.wait_ge(added, i + 1)
                    link(nc.scalar.activation(junk, token_tile(c, t), ACT.Square, accum_out=norm_squares(c)[:, i:i + 1]))

        @block.vector
        def _(dve):
            link = chain(dve, dve_chain)
            nc.vector.reduce_sum(rstd[:, 0:n], branch_squares(c, n_chunks)[:, 0:n, :], AX.X).then_inc(summed, 1)
            dve.wait_ge(stats, 1)
            for t in tiles:
                link(nc.vector.scalar_tensor_tensor(y[:, t, :], y[:, t, :], rstd[:, t:t + 1],
                                                    c.gates[:, w, int(t >= TX), :], ALU.mult, ALU.mult))
                nc.vector.tensor_tensor(token_tile(c, t), token_tile(c, t), y[:, t, :], ALU.add).then_inc(added, 1)


def ffn_up(c, l, z):
    nc = c.nc
    st, sem = stage(c)
    name = f"up{l}"
    lo, _ = c.range_of[name]
    ht = ht_view(c)
    hidden, o = ffn_hidden(c)
    n_all = N_X + z
    gbuf = c.arena[:, o:o + 2 * N_ALL].rearrange("p (b t) -> p b t", b=2)
    with st, nc.Block() as block:
        product, drained, summed, gated, done, dve_chain = \
            (sem(n) for n in ("product", "drained", "summed", "gated", "done", "dve_chain"))

        @block.sync
        def _(sp):
            c.issue(sp, name, lambda j: (product, 2 * (2 * (j // 2) + 2)))

        @block.tensor
        def _(pe):
            for n in range(FT):
                for half in range(2):
                    chunk = lo + 2 * (n // 2) + half
                    if n % 2 == 0:
                        c.arrived(pe, chunk)
                    if n >= 2:
                        pe.wait_ge(summed, 2 * (n - 2) + half + 1)
                    w = c.slot(chunk, KT, 256)[:, :, n % 2 * 128:n % 2 * 128 + 128]
                    bank = 4 * (n % 2) + 2 * half
                    for k in range(KT):
                        last = nc.tensor.matmul(c.ps[:, bank, :], w[:, k, :], ht[:, k, 0:N_X],
                                                start=k == 0, stop=k == KT - 1)
                        if z:
                            last = nc.tensor.matmul(c.ps[:, bank + 1, 0:z], w[:, k, :], ht[:, k, N_X:N_X + z],
                                                    start=k == 0, stop=k == KT - 1)
                    last.then_inc(product, 1)

        def middle_tap(n, half):
            return ffn_tap(c, l, 1, n + half * FT)

        @block.scalar
        def _(act):
            def gate(n):
                act.wait_ge(summed, 2 * n + 2)
                nc.scalar.activation(gbuf[:, n % 2, 0:n_all], gbuf[:, n % 2, 0:n_all], ACT.Silu).then_inc(gated, 1)

            for n in range(FT):
                for half in range(2):
                    act.wait_ge(product, 2 * n + half + 1)
                    bank = 4 * (n % 2) + 2 * half
                    if half and n >= 2:
                        act.wait_ge(done, n - 1)
                    dst = gbuf[:, n % 2, :] if half else hidden[:, n, :]
                    nc.scalar.activation(dst[:, 0:N_X], c.ps[:, bank, :], ACT.Identity,
                                         scale=middle_tap(n, half)).then_inc(drained, 1)
                    if z:
                        nc.scalar.activation(dst[:, N_X:n_all], c.ps[:, bank + 1, 0:z], ACT.Identity,
                                             scale=middle_tap(n, half)).then_inc(drained, 1)
                    if half == 0 and n:
                        gate(n - 1)
            gate(FT - 1)

        @block.vector
        def _(dve):
            link = chain(dve, dve_chain)
            per = 2 if z else 1

            def multiply(n):
                dve.wait_ge(gated, n + 1)
                nc.vector.tensor_tensor(hidden[:, n, 0:n_all], hidden[:, n, 0:n_all], gbuf[:, n % 2, 0:n_all],
                                        ALU.mult).then_inc(done, 1)

            for n in range(FT):
                for half in range(2):
                    dve.wait_ge(drained, per * (2 * n + half + 1))
                    bank = 4 * (n % 2) + 2 * half
                    dst = gbuf[:, n % 2, :] if half else hidden[:, n, :]
                    convolve(c, link, dst, c.ps[:, bank, :], c.ps[:, bank + 1, :], z,
                             lambda t: ffn_tap(c, l, t, n + half * FT)).then_inc(summed, 1)
                    if half == 0 and n:
                        multiply(n - 1)
            multiply(FT - 1)


def ffn_hidden(c):
    return c.arena[:, 0:FT * N_ALL].rearrange("p (k t) -> p k t", k=FT), FT * N_ALL


def feed_forward(c, l, z, tiles):
    norm_to_features(c, 1, tiles)
    ffn_up(c, l, z)
    project_tokens(c, f"down{l}", ffn_hidden(c)[0], FT, 2, 128, tiles,
                   lambda t, j: mixed_rows(c)[:, t, j * 128:(j + 1) * 128], mod_layer=1 if l == 0 else None, squares=True)
    add_branch(c, 1, tiles, 8, next_norm=l == 0)


def layer_ab(c):
    spread_modulation(c, 0)
    norm_to_features(c, 0, range(TT))
    project_features(c, "diff_qk", 8, diff_buffers(c)[0], "rope")
    project_tokens(c, "diff_v", ht_view(c), KT, 1, 256, range(TT),
                   lambda t, j: diff_buffers(c)[1][:, t, j * 256:(j + 1) * 256])
    lambda_value(c)
    diff_attention(c)
    gdn_gates(c)
    project_features(c, "gdn_gate", 4, gdn_buffers(c)[1], "silu")
    project_features(c, "gdn_qkv", 12, gdn_buffers(c)[0], "conv_silu", taps=lambda t, n: gdn_tap(c, t, n),
                     ahead=0)
    norm_qk(c)
    chunk_products(c)
    delta_rule(c)
    gdn_output(c)
    project_tokens(c, "ab_out", outc(c), KT, 1, 256, range(TT),
                   lambda t, j: mixed_rows(c)[:, t, j * 256:(j + 1) * 256], squares=True)
    add_branch(c, 0, range(TT), 4)
    feed_forward(c, 0, N_Z, range(TT))


def cd_buffers(c):
    at = [0]

    def take(n):
        at[0] += n
        return c.arena[:, at[0] - n:at[0]]

    out = take(KT * N_X).rearrange("p (k t) -> p k t", k=KT)
    q = take(4 * N_X).rearrange("p (k t) -> p k t", k=4)
    k = take(N_ALL).rearrange("p (k t) -> p k t", k=1)
    k2 = take(2 * N_ALL).rearrange("p (g t) -> p g t", g=2)
    v = take(TT * 128).rearrange("p (t e) -> p t e", t=TT)
    prob = take(3 * 640).rearrange("p (b m) -> p b m", b=3)
    turned = take(2 * 640).rearrange("p (b m) -> p b m", b=2)
    u = take(12 * N_X).rearrange("p (k t) -> p k t", k=12)
    return out, q, k, k2, v, prob, turned, u


def window_attention(c):
    nc, a = c.nc, c.a
    st, sem = stage(c)
    out, q_, k_, k2, v_, prob, turned, _ = cd_buffers(c)
    top, neg, total, sink_exp = (c.stat[:, 2 * i:2 * i + 2] for i in range(4))
    sink, neg_sink = c.stat[:, 16:24], c.stat[:, 24:32]
    units = [(q, h) for q in range(TX) for h in range(8)]
    n_units = len(units)
    scale = HEAD ** -0.5
    flat = c.ps.rearrange("p b n -> p (b n)")
    score = lambda u: flat[:, (u % 2) * 1024:(u % 2) * 1024 + 640]
    turn = flat[:, 2048:2048 + 640]
    window = lambda q: range(max(0, q - 1), min(TX, q + 2))
    tiles = lambda q: [TX, TX + 1] + list(window(q))
    with st, nc.Block() as block:
        names = ("sink_in", "ready", "scored", "maxed", "exped", "sink_exped", "weighed", "turned_ps", "turned_sb",
                 "valued", "written", "dve_chain")
        sink_in, ready, scored, maxed, exped, sink_exped, weighed, turned_ps, turned_sb, valued, written, dve_chain = \
            (sem(n) for n in names)

        @block.sync
        def _(sp):
            sp.dma_start(sink, a["swa_sink"][0].partition_broadcast(128)).then_inc(sink_in, 16)

        @block.tensor
        def _(pe):
            pe.wait_ge(ready, 1)
            for i in range(n_units + 3):
                if i < n_units:
                    q, h = units[i]
                    if i >= 2:
                        pe.wait_ge(exped, i - 1)
                    pa = slice(64 * (h % 2), 64 * (h % 2) + 64)
                    lhs, keys, s = q_[pa, h // 2, q * 128:(q + 1) * 128], k2[pa, h // 4, :], score(i)
                    w = window(q)
                    first = w[0] * 128
                    nc.tensor.matmul(s[:, 0:N_Z], lhs, keys[:, N_X:N_ALL], start=True, stop=True)
                    last = nc.tensor.matmul(s[:, N_Z:512], lhs, keys[:, first:first + 256], start=True, stop=True)
                    if len(w) == 3:
                        last = nc.tensor.matmul(s[:, 512:640], lhs, keys[:, first + 256:first + 384],
                                                start=True, stop=True)
                    last.then_inc(scored, 1)
                if 0 <= i - 2 < n_units:
                    u = i - 2
                    q, h = units[u]
                    pe.wait_ge(weighed, u + 1)
                    if u:
                        pe.wait_ge(turned_sb, u)
                    for m in range(len(tiles(q))):
                        last = nc.tensor.transpose(turn[:, m * 128:(m + 1) * 128],
                                                   prob[:, u % 3, m * 128:(m + 1) * 128], c.tab["ident"])
                    last.then_inc(turned_ps, 1)
                if 0 <= i - 3 < n_units:
                    u = i - 3
                    q, h = units[u]
                    pe.wait_ge(turned_sb, u + 1)
                    if u >= 2:
                        pe.wait_ge(written, u - 1)
                    pa, g = slice(64 * (h % 2), 64 * (h % 2) + 64), h // 4
                    for m, t in enumerate(tiles(q)):
                        last = nc.tensor.matmul(c.ps[pa, 6 + u % 2, 0:128], v_[:, t, 64 * g:64 * g + 64],
                                                turned[:, u % 2, m * 128:(m + 1) * 128],
                                                start=m == 0, stop=m == len(tiles(q)) - 1)
                    last.then_inc(valued, 1)

        @block.scalar
        def _(act):
            for i in range(n_units + 2):
                if 0 <= i - 2 < n_units:
                    u = i - 2
                    n = len(tiles(units[u][0])) * 128
                    act.wait_ge(turned_ps, u + 1)
                    if u >= 2:
                        act.wait_ge(valued, u - 1)
                    nc.scalar.activation(turned[:, u % 2, 0:n], turn[:, 0:n], ACT.Copy).then_inc(turned_sb, 1)
                if i < n_units:
                    q, h = units[i]
                    n = len(tiles(q)) * 128
                    act.wait_ge(maxed, i + 1)
                    if i >= 3:
                        act.wait_ge(turned_ps, i - 2)
                    nc.scalar.activation(prob[:, i % 3, 0:n], score(i)[:, 0:n], ACT.Exp, bias=neg[:, i % 2:i % 2 + 1],
                                         scale=scale, accum_out=total[:, i % 2:i % 2 + 1]).then_inc(exped, 1)
                    nc.scalar.activation(sink_exp[:, i % 2:i % 2 + 1], sink[:, h:h + 1], ACT.Exp,
                                         bias=neg[:, i % 2:i % 2 + 1]).then_inc(sink_exped, 1)

        @block.vector
        def _(dve):
            v = nc.vector
            link = chain(dve, dve_chain)
            dve.wait_ge(sink_in, 16)
            for g in range(2):
                for hh in range(2):
                    v.tensor_copy(k2[64 * hh:64 * hh + 64, g, :], k_[64 * g:64 * g + 64, 0, :])
            v.tensor_scalar(neg_sink, sink, -1.0, None, ALU.mult).then_inc(ready, 1)
            dve.wait_ge(ready, 1)
            for i in range(n_units + 4):
                if i < n_units:
                    q, h = units[i]
                    w = window(q)
                    b = slice(i % 2, i % 2 + 1)
                    n = len(tiles(q)) * 128
                    dve.wait_ge(scored, i + 1)
                    if w[0] == q - 1:
                        link(v.tensor_tensor(score(i)[:, 256:384], score(i)[:, 256:384], c.tab["win_l"], ALU.add))
                    if w[-1] == q + 1:
                        link(v.tensor_tensor(score(i)[:, n - 128:n], score(i)[:, n - 128:n], c.tab["win_r"], ALU.add))
                    link(v.reduce_max(top[:, b], score(i)[:, 0:n], AX.X))
                    if i >= 2:
                        dve.wait_ge(sink_exped, i - 1)
                    v.tensor_scalar(neg[:, b], top[:, b], -scale, neg_sink[:, h:h + 1], ALU.mult, ALU.min)\
                        .then_inc(maxed, 1)
                if 0 <= i - 1 < n_units:
                    u = i - 1
                    b = slice(u % 2, u % 2 + 1)
                    n = len(tiles(units[u][0])) * 128
                    dve.wait_ge(sink_exped, u + 1)
                    link(v.tensor_tensor(total[:, b], total[:, b], sink_exp[:, b], ALU.add))
                    link(v.reciprocal(total[:, b], total[:, b]))
                    v.tensor_scalar(prob[:, u % 3, 0:n], prob[:, u % 3, 0:n], total[:, b], None, ALU.mult)\
                        .then_inc(weighed, 1)
                if 0 <= i - 4 < n_units:
                    u = i - 4
                    q, h = units[u]
                    pa = slice(64 * (h % 2), 64 * (h % 2) + 64)
                    dve.wait_ge(valued, u + 1)
                    v.tensor_copy(out[pa, h // 2, q * 128:(q + 1) * 128], c.ps[pa, 6 + u % 2, 0:128]).then_inc(written, 1)


class Hyena:

    def __init__(self, c):
        at = [KT * N_X]

        def take(n):
            at[0] += n
            return c.arena[:, at[0] - n:at[0]]

        self.out = c.arena[:, 0:KT * N_X].rearrange("p (k t) -> p k t", k=KT)
        four = lambda ap: ap.rearrange("p (s t n) -> p s t n", s=2, t=4)
        self.fwd = four(take(2048))
        self.back = take(2048).rearrange("p (s f n) -> p s f n", s=2, f=2)
        self.kern, self.lags = (four(take(4096)) for _ in range(2))
        self.spec = self.lags
        self.tmp = take(5632).rearrange("p (n c) -> p n c", n=11)
        ht = lambda i: c.ht[:, i * 2048:i * 2048 + 2048].rearrange("p (t n) -> p t n", t=4)
        self.v, self.x1, self.x2t = ht(0), ht(1), ht(2)
        self.z1t = self.x1
        self.decay = c.z.rearrange("p t d -> p (t d)").rearrange("p (t n) -> p t n", t=4)
        self.w3 = c.arena[0:HEAD, 4 * N_X:8 * N_X]
        spare = c.gates[:, :, 1, :].rearrange("p v (h n) -> p v h n", h=2)
        self.root, self.bias0, self.h1, self.h2 = spare[:, 0, 0], spare[:, 0, 1], spare[0:64, 1, 0], spare[0:64, 1, 1]
        self.small = c.small[:, 0:256]


def turn_tiles(c, jobs, copies=()):
    nc = c.nc
    st, sem = stage(c)
    with st, nc.Block() as block:
        turned, act_out, dve_out, copied = sem("turned"), sem("act_out"), sem("dve_out"), sem("copied")

        @block.tensor
        def _(pe):
            for n, (_, blocks) in enumerate(jobs):
                if n >= 8:
                    pe.wait_ge(dve_out if n % 2 else act_out, (n - 8) // 2 + 1)
                for i, b in enumerate(blocks):
                    last = nc.tensor.transpose(c.ps[:, n % 8, i * 128:(i + 1) * 128], b, c.tab["ident"])
                last.then_inc(turned, 1)

        @block.scalar
        def _(act):
            for n, (dst, _) in enumerate(jobs):
                if n % 2 == 0:
                    act.wait_ge(turned, n + 1)
                    nc.scalar.activation(dst, c.ps[:, n % 8, :], ACT.Copy).then_inc(act_out, 1)

        @block.vector
        def _(dve):
            for n, (dst, _) in enumerate(jobs):
                if n % 2:
                    dve.wait_ge(turned, n + 1)
                    nc.vector.tensor_copy(dst, c.ps[:, n % 8, :]).then_inc(dve_out, 1)

        @block.gpsimd
        def _(pool):
            for dst, src in copies:
                nc.gpsimd.tensor_copy(dst, src).then_inc(copied, 1)


def filter_features(c, hy):
    nc, a = c.nc, c.a
    st, sem = stage(c)
    w1, w2 = hy.small[0:33, 0:64], hy.small[0:64, 64:128]
    cols = hy.small[0:64, 128:132]
    n_, r_ = hy.tmp[0:64, 0, :], hy.tmp[0:64, 1, :]
    hi = float(np.float32(6.28125))
    lo = 2 * math.pi - hi
    magic = 12582912.0
    with st, nc.Block() as block:
        w_in, tables_in, product, chained, sined = (sem(n) for n in ("w_in", "tables_in", "product", "chained", "sined"))

        @block.sync
        def _(sp):
            sp.dma_start(w1, a["hy_w1"][0]).then_inc(w_in, 16)
            sp.dma_start(w2, a["hy_w2"][0]).then_inc(w_in, 16)
            for i, v in enumerate((a["hy_b1"][0], a["hy_b2"][0], a["hy_freq"][0, 0], a["hy_freq"][0, 1])):
                sp.dma_start(cols[:, i:i + 1], v.unsqueeze(1)).then_inc(w_in, 16)
            sp.dma_start(hy.w3, a["hy_w3"][0]).then_inc(tables_in, 16)
            sp.dma_start(hy.decay, a["t_decay"].rearrange("(t p) n -> p t n", p=128)).then_inc(tables_in, 16)
            sp.dma_start(hy.bias0, a["hy_bias"][0, 0].partition_broadcast(128)).then_inc(tables_in, 16)
            for s in range(2):
                sp.dma_start(hy.fwd[:, s], a["t_fwd"][s].rearrange("(t p) n -> p t n", p=128)).then_inc(tables_in, 16)
                sp.dma_start(hy.back[:, s], a["t_back"][s].rearrange("(t p) n -> p t n", p=128)).then_inc(tables_in, 16)
            sp.wait_ge(tables_in, 112)

        @block.tensor
        def _(pe):
            pe.wait_ge(w_in, 96)
            nc.tensor.matmul(c.ps[0:64, 0, :], w1, c.tab["feats"][0:33, :], start=True, stop=True).then_inc(product, 1)
            pe.wait_ge(sined, 1)
            nc.tensor.matmul(c.ps[0:64, 1, :], w2, hy.h1, start=True, stop=True).then_inc(product, 1)

        @block.vector
        def _(dve):
            v = nc.vector
            link = chain(dve, chained)
            for i, h in enumerate((hy.h1, hy.h2)):
                dve.wait_ge(product, i + 1)
                link(v.tensor_scalar(h, c.ps[0:64, i, :], cols[:, i:i + 1], cols[:, 2 + i:3 + i], ALU.add, ALU.mult))
                link(v.tensor_scalar(n_, h, 1 / (2 * math.pi), magic, ALU.mult, ALU.add))
                link(v.tensor_scalar(n_, n_, -magic, None, ALU.add))
                link(v.scalar_tensor_tensor(h, n_, -hi, h, ALU.mult, ALU.add))
                link(v.scalar_tensor_tensor(h, n_, -lo, h, ALU.mult, ALU.add))
                link(v.tensor_scalar(h, h, 3.1415925, -3.1415925, ALU.min, ALU.max))

        @block.scalar
        def _(act):
            for i, h in enumerate((hy.h1, hy.h2)):
                act.wait_ge(chained, 6 * (i + 1))
                nc.scalar.activation(h, h, ACT.Sin).then_inc(sined, 1)


def filter_lags(c, hy, order):
    nc = c.nc
    st, sem = stage(c)
    sq = hy.tmp
    with st, nc.Block() as block:
        product, decayed, squared, used, summed, act_chain, combined = \
            (sem(n) for n in ("product", "decayed", "squared", "used", "summed", "act_chain", "combined"))

        @block.tensor
        def _(pe):
            def square_sum(t):
                for side in range(2):
                    n = 2 * t + side
                    pe.wait_ge(squared, n + 1)
                    nc.tensor.matmul(c.ps[:, 7, :], c.tab["ones"], sq[:, n % 3, :], start=n == 0, stop=n == 7,
                                     ).then_inc(used, 1)

            for t in range(4):
                for side in range(2):
                    n = 2 * t + side
                    if n >= 6:
                        pe.wait_ge(decayed, n - 5)
                    col = (order * 2 + side) * 512
                    nc.tensor.matmul(c.ps[:, n % 6, :], hy.h2[:, t * 128:(t + 1) * 128], hy.w3[:, col:col + 512],
                                     start=True, stop=True).then_inc(product, 1)
                if t:
                    square_sum(t - 1)
            square_sum(3)

        @block.vector
        def _(dve):
            v = nc.vector
            for t in range(4):
                for side in range(2):
                    n = 2 * t + side
                    dve.wait_ge(product, n + 1)
                    dst = hy.lags[:, side, t, :]
                    if side and t == 0:
                        v.scalar_tensor_tensor(dst, c.ps[:, n % 6, :], c.tab["nonzero"], hy.decay[:, t, :],
                                               ALU.mult, ALU.mult).then_inc(decayed, 1)
                    else:
                        v.tensor_tensor(dst, c.ps[:, n % 6, :], hy.decay[:, t, :], ALU.mult).then_inc(decayed, 1)
                dve.wait_ge(squared, 2 * t + 2)
                v.tensor_tensor(hy.lags[:, 0, t, :], hy.lags[:, 0, t, :], hy.lags[:, 1, t, :], ALU.add)\
                    .then_inc(combined, 1)
                dve.wait_ge(combined, 2 * t + 1)
                v.scalar_tensor_tensor(hy.lags[:, 1, t, :], hy.lags[:, 1, t, :], -2.0, hy.lags[:, 0, t, :],
                                       ALU.mult, ALU.add).then_inc(combined, 1)

        @block.scalar
        def _(act):
            link = chain(act, act_chain)
            for n in range(8):
                act.wait_ge(decayed, n + 1)
                if n >= 3:
                    act.wait_ge(used, n - 2)
                nc.scalar.activation(sq[:, n % 3, :], hy.lags[:, n % 2, n // 2, :], ACT.Square).then_inc(squared, 1)
            act.wait_ge(used, 8)
            link(nc.scalar.activation(hy.root, c.ps[:, 7, :], ACT.Ln, bias=EPS))
            link(nc.scalar.activation(hy.root, hy.root, ACT.Exp, scale=-0.5))


def transform(c, src, hy, values, finish, finish_pool=None, join=None):
    nc = c.nc
    st, sem = stage(c)
    with st, nc.Block() as block:
        product, chained, pool_chained = sem("product"), sem("chained"), sem("pool_chained")
        even_out, unfolded, finished, pool_finished = sem("even_out"), sem("unfolded"), sem("finished"), sem("pool_finished")

        @block.tensor
        def _(pe):
            for f in range(2):
                for s in range(2):
                    for odd in range(2):
                        for t in range(2):
                            last = nc.tensor.matmul(c.ps[:, 4 * f + 2 * s + odd, :],
                                                    hy.fwd[:, s, 2 * odd + t, f * 128:(f + 1) * 128],
                                                    src(s)[:, 2 * odd + t, :], start=t == 0, stop=t == 1)
                    last.then_inc(product, 1)

        @block.vector
        def _(dve):
            link = chain(dve, chained)
            for f in range(2):
                for s in range(2):
                    dve.wait_ge(product, 2 * f + s + 1)
                    dve.wait_ge(even_out, 2 * f + s + 1)
                    total, mirrored, odd = values(s, 0, f), values(s, 1, f), c.ps[:, 4 * f + 2 * s + 1, :]
                    nc.vector.tensor_tensor(mirrored, *((odd, total) if s else (total, odd)), ALU.subtract)
                    nc.vector.tensor_tensor(total, total, odd, ALU.add).then_inc(unfolded, 1)
                dve.wait_ge(unfolded, 2 * f + 2)
                last = finish(link, f)
                if finish_pool:
                    link(last)
                    dve.wait_ge(pool_finished, f + 1)
                    last = join(link, f)
                last.then_inc(finished, 1)

        @block.scalar
        def _(act):
            for f in range(2):
                if f and finish_pool:
                    act.wait_ge(finished, f)
                    act.wait_ge(pool_finished, f)
                for s in range(2):
                    act.wait_ge(product, 2 * f + s + 1)
                    nc.scalar.activation(values(s, 0, f), c.ps[:, 4 * f + 2 * s, :], ACT.Copy).then_inc(even_out, 1)

        if finish_pool:
            @block.gpsimd
            def _(pool):
                link = chain(pool, pool_chained)
                for f in range(2):
                    pool.wait_ge(unfolded, 2 * f + 2)
                    finish_pool(link, f).then_inc(pool_finished, 1)


def inverse(c, hy, by_token, finish):
    nc = c.nc
    st, sem = stage(c)
    with st, nc.Block() as block:
        product, chained = sem("product"), sem("chained")

        @block.tensor
        def _(pe):
            for i in range(4):
                cut = slice(i * 128, (i + 1) * 128)
                for odd in ([i // 2] if by_token else range(2)):
                    tokens = slice(256 * odd, 256 * odd + 256)
                    for n in range(4):
                        s, f = n // 2, n % 2
                        table, spec = hy.back[:, s, f, :], hy.spec[:, s, 2 * odd + f, :]
                        if by_token:
                            last = nc.tensor.matmul(c.ps[:, i, :], table[:, cut], spec, start=n == 0, stop=n == 3)
                        else:
                            last = nc.tensor.matmul(c.ps[:, i, tokens], spec[:, cut], table[:, tokens],
                                                    start=n == 0, stop=n == 3)
                last.then_inc(product, 1)

        @block.vector
        def _(dve):
            link = chain(dve, chained)
            for i in range(4):
                dve.wait_ge(product, i + 1)
                finish(link, i, c.ps[:, i, :])


def hyena(c):
    nc = c.nc
    v = nc.vector
    hy = Hyena(c)
    u = cd_buffers(c)[7]
    block_of = lambda buf, i, j: buf[:, i, j * 128:(j + 1) * 128]

    def tokens_of(k, t):
        first = 256 * (t % 2) + t // 2
        return u[:, k, first:first + 255:2]

    turn_tiles(c, [(hy.v[:, t, :], [tokens_of(k, t) for k in range(4)]) for t in range(4)]
               + [(hy.x1[:, t, :], [tokens_of(4 + k, t) for k in range(4)]) for t in range(4)],
               [(hy.x2t[:, k, :], u[:, 8 + k, :]) for k in range(4)])
    filter_features(c, hy)
    root = hy.root

    kern_of = lambda s, mirror, f: hy.kern[:, s, 2 * mirror + f, :]

    def scaled(link, f):
        for s in range(2):
            for mirror in range(2):
                last = v.tensor_tensor(kern_of(s, mirror, f), kern_of(s, mirror, f), root, ALU.mult)
        return last

    z = lambda s, mirror: hy.tmp[:, 2 * s + mirror, :]
    def product_c(link, f):
        one, part, other = (hy.tmp[:, i, :] for i in (4, 5, 6))
        for mirror, total in enumerate((one, other)):
            v.tensor_tensor(total, z(0, mirror), kern_of(0, mirror, f), ALU.mult)
            link(v.tensor_tensor(part, z(1, mirror), kern_of(1, mirror, f), ALU.mult))
            link(v.tensor_tensor(total, total, part, ALU.subtract))
        v.tensor_tensor(hy.spec[:, 0, f, :], one, other, ALU.add)
        return v.tensor_tensor(hy.spec[:, 0, 2 + f, :], one, other, ALU.subtract)

    one_s, part_s, other_s, other_part_s = (hy.tmp[:, i, :] for i in (7, 8, 9, 10))

    def product_s(link, f):
        tt = nc.gpsimd.tensor_tensor
        tt(one_s, z(0, 0), kern_of(1, 0, f), ALU.mult)
        link(tt(part_s, z(1, 0), kern_of(0, 0, f), ALU.mult))
        tt(one_s, one_s, part_s, ALU.add)
        tt(other_s, z(0, 1), kern_of(1, 1, f), ALU.mult)
        return tt(other_part_s, z(1, 1), kern_of(0, 1, f), ALU.mult)

    def join_s(link, f):
        link(v.tensor_tensor(other_s, other_s, other_part_s, ALU.add))
        v.tensor_tensor(hy.spec[:, 1, f, :], one_s, other_s, ALU.subtract)
        return v.tensor_tensor(hy.spec[:, 1, 2 + f, :], one_s, other_s, ALU.add)

    def gate_tokens(link, t, conv):
        z = hy.v[:, t, :]
        link(v.tensor_tensor(z, z, hy.bias0, ALU.mult))
        link(v.tensor_tensor(z, z, conv, ALU.add))
        link(v.tensor_tensor(z, z, hy.x1[:, t, :], ALU.mult))

    def gate_features(link, k, conv):
        t0 = hy.tmp[:, 0, :]
        link(v.scalar_tensor_tensor(t0, hy.z1t[:, k, :], hy_bias_col(c, k), conv, ALU.mult, ALU.add))
        tokens = lambda ap: ap.rearrange("p (m e) -> p e m", e=2)
        link(v.tensor_tensor(tokens(hy.out[:, 4 + k, :]), t0.rearrange("p (e m) -> p e m", e=2), tokens(hy.x2t[:, k, :]),
                             ALU.mult))

    for order in range(2):
        filter_lags(c, hy, order)
        transform(c, lambda s: hy.lags[:, s], hy, kern_of, scaled)
        transform(c, lambda s: hy.v, hy, lambda s, mirror, f: z(s, mirror), product_c, product_s, join_s)
        if order == 0:
            inverse(c, hy, True, gate_tokens)
            turn_tiles(c, [(hy.z1t[:, k, :], [block_of(hy.v, t, k) for t in range(4)]) for k in range(4)])
        else:
            inverse(c, hy, False, gate_features)


def layer_cd(c):
    with c.nc.Block() as block:
        @block.sync
        def _(sp):
            sp.wait_ge(c.tables_back, 32)
    spread_modulation(c, 1)
    norm_to_features(c, 0, range(TT))
    out, q, k, _, v, _, _, u = cd_buffers(c)
    project_features(c, "swa_q", 4, q, "rope", z=0)
    project_features(c, "swa_k", 1, k, "rope", cols=128)
    project_tokens(c, "swa_v", ht_view(c), KT, 1, 128, range(TT), lambda t, j: v[:, t, :])
    project_features(c, "hy_in", 12, u, "conv", z=0, taps=lambda t, n: hy_tap(c, t, n))
    window_attention(c)
    hyena(c)
    project_tokens(c, "cd_out", out, KT, 1, 256, range(TX), lambda t, j: mixed_rows(c)[:, t, j * 256:(j + 1) * 256], squares=True)
    add_branch(c, 0, range(TX), 4)
    feed_forward(c, 1, 0, range(TX))


def store(c):
    with c.nc.Block() as block:
        @block.sync
        def _(sp):
            sp.dma_start(c.a["out"][0].rearrange("(t p) d -> p t d", p=128), c.x).then_inc(c.stored, 16)
            sp.wait_ge(c.stored, 16)


def build_program(nc, a):
    with ExitStack() as ctx:
        c = Core(nc, a, ctx)
        plan_all(c)
        load_inputs(c)
        modulation(c, 0)
        layer_ab(c)
        layer_cd(c)
        store(c)


_INS = ("x", "c", "ctx", "c_ctx", "w_mod", "b_mod", "norm_g", "ffn_w_up", "ffn_conv", "ffn_w_down", "ab_w_in",
        "ab_w_out", "gdn_conv", "gdn_a_log", "gdn_dt_bias", "gdn_norm_g", "diff_lambda", "diff_norm_g", "cd_w_in",
        "cd_w_out", "swa_sink", "hy_conv", "hy_w1", "hy_b1", "hy_w2", "hy_b2", "hy_w3", "hy_freq", "hy_bias")


def kernel(**inputs):
    import concourse.bacc as bacc
    from concourse.bass_utils import run_bass_kernel_spmd

    nc = bacc.Bacc("TRN2", target_bir_lowering=False, num_devices=1)
    arrays = {f"in_{name}": np.ascontiguousarray(inputs[name]) for name in _INS}
    arrays["in_c_ctx"] = arrays["in_c_ctx"].reshape(1, D)
    arrays.update({f"in_{name}": table for name, table in constant_tables().items()})
    a = {name[3:]: nc.dram_tensor(name, v.shape, mybir.dt.from_np(v.dtype), kind="ExternalInput").ap()
         for name, v in arrays.items()}
    a["out"] = nc.dram_tensor("out", (1, N_X, D), F32, kind="ExternalOutput").ap()
    build_program(nc, a)
    r = run_bass_kernel_spmd(nc, [arrays], core_ids=[0])
    return r.results[0]["out"]
```
